# Optimizing a Trainium2 kernel written in Bass

```python
import functools
import jax
import jax.numpy as jnp
from jax import lax
import numpy as np

D_MODEL = 1024
BATCH = 1
SEQ = 1024
DEPTH = 1
DEC_BATCH = 8
DEC_SEQ = 8
PAST_LEN = 2048
PAGE_SIZE = 128

N_META = 16
N_HEADS = 16
HEAD_DIM = 64
N_KV_HEADS = 4
ATT_WIDTH = N_HEADS * HEAD_DIM
KV_WIDTH = N_KV_HEADS * HEAD_DIM
IDX_HEADS = 8
IDX_DIM = 64
TOPK_MAX = 256
Q_BLOCK = 128
GLA_HEADS = 4
GLA_DK = D_MODEL // 2 // GLA_HEADS
GLA_DV = D_MODEL // GLA_HEADS
GLA_KW = GLA_HEADS * GLA_DK
GLA_VW = GLA_HEADS * GLA_DV
GLA_GATE_RANK = 16
GLA_TAU = 16.0
GLA_CHUNK = 64
N_BRANCHES = 2
D_FF = 4 * D_MODEL
LN_EPS = 1e-5
DEEPNORM_ALPHA = (2 * DEPTH) ** 0.25
DEEPNORM_BETA = (8 * DEPTH) ** -0.25
IN_SIZES = (ATT_WIDTH, KV_WIDTH, KV_WIDTH, IDX_HEADS * IDX_DIM, IDX_DIM, IDX_HEADS,
            GLA_KW, GLA_KW, GLA_VW, GLA_VW, GLA_GATE_RANK, N_BRANCHES * D_MODEL)
IN_WIDTH = sum(IN_SIZES)

kernel_name = 'dsa_gla_gated_hybrid_step'

def layer_norm(x, g, b):
    xf = x.astype(jnp.float32)
    mu = jnp.mean(xf, -1, keepdims=True)
    var = jnp.mean(jnp.square(xf - mu), -1, keepdims=True)
    y = (xf - mu) * lax.rsqrt(var + LN_EPS) * g.astype(jnp.float32) + b.astype(jnp.float32)
    return y.astype(x.dtype)

def in_proj(h, w_in, w_gla_a2, b_gla_a):
    B, T, _ = h.shape
    points = [int(p) for p in np.cumsum(IN_SIZES)[:-1]]
    q, k, v, qi, ki, wi, gq, gk, gv, og, a1, gt = jnp.split(h @ w_in, points, axis=-1)
    loga = jax.nn.log_sigmoid((a1 @ w_gla_a2).astype(jnp.float32) + b_gla_a.astype(jnp.float32)) / GLA_TAU
    gates = jax.nn.sigmoid(gt.astype(jnp.float32)).reshape(B, T, N_BRANCHES, D_MODEL)
    return (q.reshape(B, T, N_HEADS, HEAD_DIM), k.reshape(B, T, N_KV_HEADS, HEAD_DIM),
            v.reshape(B, T, N_KV_HEADS, HEAD_DIM), qi.reshape(B, T, IDX_HEADS, IDX_DIM), ki, wi,
            gq.reshape(B, T, GLA_HEADS, GLA_DK), gk.reshape(B, T, GLA_HEADS, GLA_DK),
            gv.reshape(B, T, GLA_HEADS, GLA_DV), og, loga.reshape(B, T, GLA_HEADS, GLA_DK), gates)

def indexer_scores(qi, wi, ki):
    s = jnp.einsum('bqhd,bld->bqhl', qi, ki).astype(jnp.float32) * IDX_DIM ** -0.5
    w = wi.astype(jnp.float32) * IDX_HEADS ** -0.5
    return jnp.einsum('bqhl,bqh->bql', jax.nn.relu(s), w)

def gathered_attention(q, k_sel, v_sel, valid):
    B, Q, H, hd = q.shape
    qg = q.reshape(B, Q, N_KV_HEADS, H // N_KV_HEADS, hd)
    s = jnp.einsum('bqngd,bqknd->bqngk', qg, k_sel).astype(jnp.float32) * hd ** -0.5
    s = jnp.where(valid[:, :, None, None, :], s, -jnp.inf)
    p = jax.nn.softmax(s, axis=-1).astype(v_sel.dtype)
    return jnp.einsum('bqngk,bqknd->bqngd', p, v_sel).reshape(B, Q, H * hd)

def dsa_prompt(q, k, v, qi, wi, ki, topk):
    B, T = q.shape[:2]
    n_blk = -(-T // Q_BLOCK)
    pad = n_blk * Q_BLOCK - T

    def blocks(a):
        a = jnp.pad(a, [(0, 0), (0, pad)] + [(0, 0)] * (a.ndim - 2))
        return jnp.moveaxis(a.reshape((B, n_blk, Q_BLOCK) + a.shape[2:]), 1, 0)

    key_pos = jnp.arange(T)
    take_rows = jax.vmap(lambda rows, idx: rows[idx])

    def one_block(xs):
        qb, qib, wib, start = xs
        pos = start + jnp.arange(Q_BLOCK)
        causal = key_pos[None, :] <= pos[:, None]
        sc = jnp.where(causal[None], indexer_scores(qib, wib, ki), -jnp.inf)
        _, idx = lax.top_k(sc, topk)
        valid = idx <= pos[None, :, None]
        return gathered_attention(qb, take_rows(k, idx), take_rows(v, idx), valid)

    out = lax.map(one_block, (blocks(q), blocks(qi), blocks(wi), jnp.arange(n_blk) * Q_BLOCK))
    return jnp.moveaxis(out, 0, 1).reshape(B, n_blk * Q_BLOCK, -1)[:, :T]

def dsa_sample(q, k, v, qi, wi, ki, cache_k, cache_v, cache_kidx, page_table, topk):
    DB, S = q.shape[:2]
    past = page_table.shape[1] * PAGE_SIZE
    ki_past = cache_kidx[page_table].reshape(DB, past, IDX_DIM)
    ki_all = jnp.concatenate([ki_past, ki.astype(ki_past.dtype)], axis=1)
    pos = past + jnp.arange(S)
    causal = jnp.arange(past + S)[None, :] <= pos[:, None]
    sc = jnp.where(causal[None], indexer_scores(qi, wi, ki_all), -jnp.inf)
    _, idx = lax.top_k(sc, topk)
    valid = idx <= pos[None, :, None]
    is_new = (idx >= past)[..., None, None]
    past_idx = jnp.minimum(idx, past - 1)
    phys = jax.vmap(lambda pt, i: pt[i])(page_table, past_idx // PAGE_SIZE)
    off = past_idx % PAGE_SIZE
    new_idx = jnp.clip(idx - past, 0, S - 1)
    take_rows = jax.vmap(lambda rows, i: rows[i])
    k_sel = jnp.where(is_new, take_rows(k, new_idx).astype(cache_k.dtype), cache_k[phys, off])
    v_sel = jnp.where(is_new, take_rows(v, new_idx).astype(cache_v.dtype), cache_v[phys, off])
    return gathered_attention(q, k_sel, v_sel, valid)

def gla_chunked(q, k, v, loga, s0, chunk):
    B, T, H, DK = q.shape
    DV = v.shape[-1]
    n = T // chunk
    f32 = jnp.float32
    q = (q.astype(f32) * DK ** -0.5).reshape(B, n, chunk, H, DK)
    k = k.astype(f32).reshape(B, n, chunk, H, DK)
    v = v.astype(f32).reshape(B, n, chunk, H, DV)
    b = jnp.cumsum(loga.astype(f32).reshape(B, n, chunk, H, DK), axis=2)
    b_last = b[:, :, -1:]
    q_d = q * jnp.exp(b)
    k_d = k * jnp.exp(-b)
    causal = jnp.tril(jnp.ones((chunk, chunk), bool))
    attn = jnp.where(causal, jnp.einsum('bnchd,bnshd->bnhcs', q_d, k_d), 0.0)
    o_intra = jnp.einsum('bnhcs,bnshv->bnchv', attn, v)
    u = jnp.einsum('bnchd,bnchv->nbhdv', k * jnp.exp(b_last - b), v)
    decay = jnp.exp(jnp.moveaxis(b_last[:, :, 0], 1, 0))[..., None]

    def step(s, xs):
        d, uc = xs
        return d * s + uc, s

    s_final, s_prev = lax.scan(step, s0.astype(f32), (decay, u))
    o_inter = jnp.einsum('bnchd,nbhdv->bnchv', q_d, s_prev)
    return (o_intra + o_inter).reshape(B, T, H, DV), s_final

def gla_prompt(q, k, v, loga):
    B, T, H, _ = q.shape
    pad = (-N_META) % GLA_CHUNK
    fp = lambda a: jnp.pad(a, ((0, 0), (pad, 0), (0, 0), (0, 0)))
    s0 = jnp.zeros((B, H, GLA_DK, GLA_DV), jnp.float32)
    o, s = gla_chunked(fp(q), fp(k), fp(v), fp(loga), s0, GLA_CHUNK)
    return o[:, pad:], s

def gla_sample(q, k, v, loga, s0):
    return gla_chunked(q, k, v, loga, s0, q.shape[1])

def token_mixer(h, w_in, w_gla_a2, b_gla_a, gla_norm_g, w_proj_attn, w_proj_gla, w_out, attend, recur):
    B, T, _ = h.shape
    q, k, v, qi, ki, wi, gq, gk, gv, og, loga, gates = in_proj(h, w_in, w_gla_a2, b_gla_a)
    att = attend(q, k, v, qi, wi, ki).astype(h.dtype)
    o, s_new = recur(gq, gk, gv, loga)
    o = o * lax.rsqrt(jnp.mean(jnp.square(o), -1, keepdims=True) + LN_EPS) * gla_norm_g.astype(jnp.float32)
    gla = (o.reshape(B, T, GLA_VW) * jax.nn.silu(og.astype(jnp.float32))).astype(h.dtype)
    merged = gates[:, :, 0] * (att @ w_proj_attn) + gates[:, :, 1] * (gla @ w_proj_gla)
    return merged.astype(h.dtype) @ w_out, (k, v, ki, s_new.astype(h.dtype))

def post_norm_block(h, mix, ln1_g, ln1_b, w_ff_up, w_ff_down, ln2_g, ln2_b):
    h = layer_norm(DEEPNORM_ALPHA * h + mix, ln1_g, ln1_b)
    ff = jnp.square(jax.nn.relu(h @ w_ff_up)) @ w_ff_down
    return layer_norm(DEEPNORM_ALPHA * h + ff, ln2_g, ln2_b)

def setup_inputs(seed: int = 0) -> dict:
    key = jax.random.key(seed)
    ks = jax.random.split(key, 24)
    f32 = jnp.float32
    n_pages = PAST_LEN // PAGE_SIZE
    n_pool = (5 * DEC_BATCH * n_pages) // 4
    nrm = lambda kk, shape, scale=1.0: jax.random.normal(kk, shape, f32) * scale
    page_table = jax.random.permutation(ks[6], n_pool)[: DEC_BATCH * n_pages]
    page_table = page_table.reshape(DEC_BATCH, n_pages).astype(jnp.int32)
    return {
        'x_prompt': nrm(ks[0], (BATCH, SEQ, D_MODEL)),
        'x_sample': nrm(ks[1], (DEC_BATCH, DEC_SEQ, D_MODEL)),
        'cache_k': nrm(ks[2], (DEPTH, n_pool, PAGE_SIZE, N_KV_HEADS, HEAD_DIM)),
        'cache_v': nrm(ks[3], (DEPTH, n_pool, PAGE_SIZE, N_KV_HEADS, HEAD_DIM)),
        'cache_kidx': nrm(ks[4], (DEPTH, n_pool, PAGE_SIZE, IDX_DIM)),
        'state_gla': nrm(ks[5], (DEPTH, DEC_BATCH, GLA_HEADS, GLA_DK, GLA_DV)),
        'page_table': page_table,
        'meta_tokens': nrm(ks[7], (N_META, D_MODEL)),
        'ln_in_g': 1.0 + nrm(ks[8], (D_MODEL,), 0.02),
        'ln_in_b': nrm(ks[9], (D_MODEL,), 0.02),
        'w_in': nrm(ks[10], (DEPTH, D_MODEL, IN_WIDTH), D_MODEL ** -0.5),
        'w_gla_a2': nrm(ks[11], (DEPTH, GLA_GATE_RANK, GLA_KW), GLA_GATE_RANK ** -0.5),
        'b_gla_a': nrm(ks[12], (DEPTH, GLA_KW), 0.1),
        'gla_norm_g': 1.0 + nrm(ks[13], (DEPTH, GLA_DV), 0.02),
        'w_proj_attn': nrm(ks[14], (DEPTH, ATT_WIDTH, D_MODEL), ATT_WIDTH ** -0.5),
        'w_proj_gla': nrm(ks[15], (DEPTH, GLA_VW, D_MODEL), GLA_VW ** -0.5),
        'w_out': nrm(ks[16], (DEPTH, D_MODEL, D_MODEL), DEEPNORM_BETA * D_MODEL ** -0.5),
        'ln1_g': 1.0 + nrm(ks[17], (DEPTH, D_MODEL), 0.02),
        'ln1_b': nrm(ks[18], (DEPTH, D_MODEL), 0.02),
        'w_ff_up': nrm(ks[19], (DEPTH, D_MODEL, D_FF), D_MODEL ** -0.5),
        'w_ff_down': nrm(ks[20], (DEPTH, D_FF, D_MODEL), DEEPNORM_BETA * D_FF ** -0.5),
        'ln2_g': 1.0 + nrm(ks[21], (DEPTH, D_MODEL), 0.02),
        'ln2_b': nrm(ks[22], (DEPTH, D_MODEL), 0.02),
    }

def reference(x_prompt, x_sample, cache_k, cache_v, cache_kidx, state_gla, page_table,
              meta_tokens, ln_in_g, ln_in_b, w_in, w_gla_a2, b_gla_a, gla_norm_g,
              w_proj_attn, w_proj_gla, w_out, ln1_g, ln1_b, w_ff_up, w_ff_down, ln2_g, ln2_b):
    B, S_p, D = x_prompt.shape
    S_s = x_sample.shape[1]
    past = page_table.shape[1] * PAGE_SIZE
    topk_prompt = min(TOPK_MAX, S_p // 4)
    topk_sample = min(TOPK_MAX, (past + S_s) // 4)

    meta = jnp.broadcast_to(meta_tokens.astype(x_prompt.dtype)[None], (B, N_META, D))
    hp = layer_norm(jnp.concatenate([meta, x_prompt], axis=1), ln_in_g, ln_in_b)
    hs = layer_norm(x_sample, ln_in_g, ln_in_b)

    kp_l, vp_l, kip_l, sp_l, ks_l, vs_l, kis_l, ss_l = [], [], [], [], [], [], [], []
    for l in range(DEPTH):
        mix_w = (w_in[l], w_gla_a2[l], b_gla_a[l], gla_norm_g[l], w_proj_attn[l], w_proj_gla[l], w_out[l])
        ffn_w = (ln1_g[l], ln1_b[l], w_ff_up[l], w_ff_down[l], ln2_g[l], ln2_b[l])
        mix_p, (kp, vp, kip, sp) = token_mixer(
            hp, *mix_w, attend=functools.partial(dsa_prompt, topk=topk_prompt), recur=gla_prompt)
        hp = post_norm_block(hp, mix_p, *ffn_w)
        attend_s = functools.partial(dsa_sample, cache_k=cache_k[l], cache_v=cache_v[l],
                                     cache_kidx=cache_kidx[l], page_table=page_table, topk=topk_sample)
        recur_s = functools.partial(gla_sample, s0=state_gla[l])
        mix_s, (ks_, vs_, kis_, ss_) = token_mixer(hs, *mix_w, attend=attend_s, recur=recur_s)
        hs = post_norm_block(hs, mix_s, *ffn_w)
        kp_l.append(kp); vp_l.append(vp); kip_l.append(kip); sp_l.append(sp)
        ks_l.append(ks_); vs_l.append(vs_); kis_l.append(kis_); ss_l.append(ss_)

    y_prompt = hp[:, N_META:]
    y_sample = hs
    k_prompt = jnp.stack(kp_l)
    v_prompt = jnp.stack(vp_l)
    kidx_prompt = jnp.stack(kip_l)
    gla_state_prompt = jnp.stack(sp_l)
    k_sample = jnp.stack(ks_l)
    v_sample = jnp.stack(vs_l)
    kidx_sample = jnp.stack(kis_l)
    gla_state_sample = jnp.stack(ss_l)
    return (y_prompt, y_sample, k_prompt, v_prompt, kidx_prompt, gla_state_prompt,
            k_sample, v_sample, kidx_sample, gla_state_sample)


_drawn_inputs = setup_inputs


def setup_inputs(seed=0):
    import zlib

    import numpy as np

    out = dict(_drawn_inputs(seed))
    spreads = {}
    factors = {'gla_norm_g': 24.468,
     'ln1_g': 2.737,
     'ln1_b': 2.785,
     'ln2_g': 7.604,
     'ln2_b': 7.785,
     'cache_k': 3.786,
     'cache_v': 2.982,
     'cache_kidx': 3.149}
    for name, (base, spread) in spreads.items():
        noise = np.random.default_rng([zlib.crc32(name.encode()), seed]).standard_normal(out[name].shape)
        drawn = base * np.exp(spread * noise) if base else spread * noise
        out[name] = jnp.asarray(drawn.astype(out[name].dtype))
    for name, factor in factors.items():
        out[name] = (out[name] * factor).astype(out[name].dtype)
    return out
```

```python
from contextlib import ExitStack

import numpy as np
import concourse.bass as bass
from concourse import mybir

F32 = mybir.dt.float32
F32R = mybir.dt.float32r
BF16 = mybir.dt.bfloat16
I32 = mybir.dt.int32
ALU = mybir.AluOpType
ACT = mybir.ActivationFunctionType
AX = mybir.AxisListType

P = 128
D = 1024
KC = D // P
SEQ, META, DB, DS = 1024, 16, 8, 8
TP = SEQ + META
TS = DB * DS
T = TP + TS
NT = -(-T // P)
N3 = T // 3
HD, NH, NKV, G = 64, 16, 4, 4
IH = 8
PAST, PAGE, NPG = 2048, 128, 16
NK = PAST + DS
TOPK = 256
GH, DK, DV, CH = 4, 128, 256, 64
RANK = 16
DFF = 4096
FB = DFF // 256
EPS = 1e-5
ALPHA = 2 ** 0.25
TAU = 16.0
NEG = -1e30
TAKEN = -3e38

UNIT = 2048
C_Q, C_K, C_V, C_QI, C_KI, C_GQ, C_GK, C_GV, C_OG, C_A1, C_GT = (
    0, 1024, 1280, 1536, 2048, 2120, 2632, 3144, 4168, 5192, 5208)
U_F1, U_Q, U_N, U_GATE, U_PA, U_PG, U_O, U_FF = 0, 4, 12, 21, 29, 33, 37, 41
N_UNITS = U_FF + 2 * FB


def is_natural(u):
    return U_N <= u < U_GATE or U_O <= u < U_FF


def halves_before(u):
    return sum(NT - 1 if is_natural(v) else 1 for v in range(min(u, U_FF))) + max(u - U_FF, 0)


def evacs_before(u):
    return sum(NT if is_natural(v) else 2 for v in range(u))


def rows_of(t):
    return min(P, T - t * P)


def pieces(n):
    k = -(-n // 512)
    w = -(-n // k)
    return n, w + w % 2, k


def keys_of(i):
    return pieces(META if i == NT - 1 else META + P * (i + 1))


def mask_at(i):
    return sum(keys_of(j)[1] * keys_of(j)[2] for j in range(i))


def build(nc, x_all, cache_k, cache_v, cache_kidx, state, page_table, ln_p, w_stream, w_a2, b_a,
          gnorm, outs):
    (y_p, y_s, k_p, v_p, ki_p, st_p, k_s, v_s, ki_s, st_s) = outs
    top = ExitStack()
    with top:
        def alloc(stack, name, shape, dt=F32):
            return stack.enter_context(nc.sbuf_tensor(name, shape, dt))

        def sb(name, shape, dt=F32):
            return alloc(top, name, shape, dt)

        def region(*specs):
            with ExitStack() as st:
                return [alloc(st, *s) for s in specs]

        def sem(name):
            return top.enter_context(nc.semaphore(name))

        def dram(name, shape):
            return nc.dram_tensor(name, shape, F32).ap()

        h_d = dram("h_d", (T, D))
        qiT_d = dram("qiT_d", (IH * HD, T))
        qT_d = dram("qT_d", (2048, T))
        gvog_d = dram("gvog_d", (T, 2048))
        gate_d = dram("gate_d", (2048, T))
        part_d = dram("part_d", (D, T))
        o_d = dram("o_d", (T, D))
        a1_d = dram("a1_d", (RANK, T))
        wi_d = dram("wi_d", (IH, TS))
        vs_d = dram("vs_d", (TS, NKV * HD))

        ps = top.enter_context(nc.psum_tensor("ps", [P, 8, 512], F32))
        flat = ps[:, :, :].rearrange("p b n -> p (b n)")

        ident = sb("ident", [P, P])
        identb = sb("identb", [P, P], BF16)
        raw = sb("raw", [P, 2, UNIT])
        w_hi = sb("w_hi", [P, 2, UNIT], F32R)
        w_lo = sb("w_lo", [P, 2, UNIT], F32R)
        xt_hi = sb("xt_hi", [P, KC, T], F32R)
        xt_lo = sb("xt_lo", [P, KC, T], F32R)
        small = sb("small", [P, 16])
        tri = sb("tri", [P, P])
        tri16 = sb("tri16", [P, META], BF16)
        causal = sb("causal", [P, CH])
        d8 = sb("d8", [TS, DB, DS])
        delta = sb("delta", [TS, DS])
        bsel = sb("bsel", [TS, DB])
        triS = sb("triS", [TS, DS])
        pt_sb = sb("pt_sb", [1, P], I32)
        m8 = sb("m8", [P, 8])
        mx = sb("mx", [P, 4])
        rsum = sb("rsum", [P, NH])
        ssq = sb("ssq", [P, 10, GH])
        pool_go = sb("pool_go", [P, 2])

        xin, hbuf, lg, lb, stats, mv = region(
            ("xin", [P, 2, D]), ("hbuf", [P, 2, D]), ("lg", [P, D]), ("lb", [P, D]),
            ("stats", [P, 2, 2, 6]), ("mv", [P, 2, 2]))
        with ExitStack() as att:
            kT3 = alloc(att, "kT3", [P, 4, T])
            winat = alloc(att, "winat", [P, NT, IH])
            IW = mask_at(8)
            with ExitStack() as b_st:
                stg = alloc(b_st, "stg", [P, 2, T])
                isc = alloc(b_st, "isc", [P, IW])
                iscS = alloc(b_st, "iscS", [TS, NK])
                kiS, qraw, qhi, qlo, relu = region(
                    ("kiS", [P, 1056], F32R), ("qraw", [P, 2, IH, P]), ("qhi", [P, IH, P], F32R),
                    ("qlo", [P, IH, P], F32R), ("relu", [P, 2, 1056]))
                kxraw, kxT, relu2, ib, qiS, wsel, wb = region(
                    ("kxraw", [P, 2, NPG, HD]), ("kxT", [HD, NK]), ("relu2", [HD, 2, 512]),
                    ("ib", [DS, NK]), ("qiS", [HD, DB, IH, DS]), ("wsel", [HD, DB]),
                    ("wb", [HD, DB, DS]))
                maskS = alloc(b_st, "maskS", [TS, NK], BF16)
                kt, pS, qblk, esel, attS, attT = region(
                    ("kt", [P, 2, 2, 512]), ("pS", [P, NK]),
                    ("qblk", [P, 2, DB, P]), ("esel", [TS, DB, NH, DS], BF16),
                    ("attS", [P, 2, G, DB, DS]), ("attT", [P, KC, TS]))
                masks = alloc(b_st, "masks", [P, IW], BF16)
                vnat = alloc(b_st, "vnat", [P, NT, NKV * HD])
                (nst,) = region(("nst", [P, 3, 256]))
                attn, qraw2 = region(("attn", [P, D]), ("qraw2", [P, 2, G, P]))
            kS, pP, ptb = region(
                ("kS", [P, NKV, 1056], F32R), ("pP", [P, 2, 1056]), ("ptb", [P, 2, 512]))
            with ExitStack() as c_st:
                alloc(c_st, "kS_place", [P, NKV * 1056 + 2 * 1056 + 1024])
                qh2, ql2 = region(("qh2", [P, G, P], F32R), ("ql2", [P, G, P], F32R))
            kpg, vpg, vnew, ptS = region(
                ("kpg", [P, 3, 4, 256]), ("vpg", [P, 4, 4, 256]), ("vnew", [DS, 2, 256]),
                ("ptS", [P, 2, 512]))
        gst, pst = region(("gst", [P, 2, T]), ("pst", [P, 2, T]))
        gq, gk, kd, zz, bb, a1T, reset, gv, gvs, s0, sx, kem, qdm, at, ken, wa2, ba, dec, bd64, ostg = region(
            ("gq", [P, T]), ("gk", [P, T]), ("kd", [P, T]), ("zz", [P, T]), ("bb", [P, T]),
            ("a1T", [RANK, T]), ("reset", [P, T], BF16), ("gv", [P, NT, DV]), ("gvs", [TS, DV]),
            ("s0", [P, DB, DV]), ("sx", [P, 4, DV]), ("kem", [TS, DB, DK]), ("qdm", [P, 576]),
            ("at", [P, 2, CH]), ("ken", [P, 2, DK]), ("wa2", [RANK, 512]), ("ba", [P, GH]),
            ("dec", [P, 25]), ("bd64", [TS, CH]), ("ostg", [P, 2, DV]))
        oin, ogin, gnb = region(("oin", [P, 2, D]), ("ogin", [P, 2, D]), ("gnb", [P, DV]))
        gst2, pst2, merged = region(("gst2", [P, 2, T]), ("pst2", [P, 2, T]), ("merged", [P, KC, T]))
        res = sb("res", [P, NT, D])
        lg2, lb2, stats2, mv2 = region(
            ("lg2", [P, D]), ("lb2", [P, D]), ("stats2", [P, 2, 2, 6]), ("mv2", [P, 2, 2]))
        a_hi, a_lo, rl = region(
            ("a_hi", [P, 2, 2, T], F32R), ("a_lo", [P, 2, 2, T], F32R), ("rl", [P, 2, T]))

        raw_in = [sem("raw_in0"), sem("raw_in1")]
        w_split = sem("w_split")
        half_done, unit_done = sem("half_done"), sem("unit_done")
        evac = sem("evac")
        stage = sem("stage")
        consts = sem("consts")
        ln_in = sem("ln_in")
        x_in = [sem("x_in0"), sem("x_in1")]
        x_free, var_ok, std_ok, h_ready = sem("x_free"), sem("var_ok"), sem("std_ok"), sem("h_ready")
        h_out = [sem("h_out0"), sem("h_out1")]
        tr_ok, hi_ok, lo_ok = sem("tr_ok"), sem("hi_ok"), sem("lo_ok")
        st_out = [sem("st_out0"), sem("st_out1")]
        nst_out = [sem(f"nst_out{i}") for i in range(3)]
        kn_tr, kn_ok = sem("kn_tr"), sem("kn_ok")
        kn_out = [sem("kn_out0"), sem("kn_out1")]
        ks_in, ks_hi, ks_ok, pads = sem("ks_in"), sem("ks_hi"), sem("ks_ok"), sem("pads")
        q_in = [sem("q_in0"), sem("q_in1")]
        q_hi_ok, q_lo_ok = sem("q_hi_ok"), sem("q_lo_ok")
        ix_mm, ix_relu, ix_acc = sem("ix_mm"), sem("ix_relu"), sem("ix_acc")
        sx_in, wb_ok = sem("sx_in"), sem("wb_ok")
        kx_in = [sem("kx_in0"), sem("kx_in1")]
        kx_tr, kx_ev, s_mm, s_relu, i_mm, i_ev, ib_out = (
            sem(n) for n in ("kx_tr", "kx_ev", "s_mm", "s_relu", "i_mm", "i_ev", "ib_out"))
        misc_out = sem("misc_out")
        c_ks_hi, c_ks_ok = sem("c_ks_hi"), sem("c_ks_ok")
        c_ks_in = [sem("c_ks_in0"), sem("c_ks_in1")]
        cq_in = [sem("cq_in0"), sem("cq_in1")]
        cq_hi, cq_lo = sem("cq_hi"), sem("cq_lo")
        qk_ok, mx_ok, exp_ok = sem("qk_ok"), sem("mx_ok"), sem("exp_ok")
        pt_tr, pt_a, pt_v, pv_ok, o_ev, att_tr = (
            sem(n) for n in ("pt_tr", "pt_a", "pt_v", "pv_ok", "o_ev", "att_tr"))
        d_set, d_cst = sem("d_set"), sem("d_cst")
        kg_in = [sem(f"kg_in{i}") for i in range(3)]
        vg_in = [sem(f"vg_in{i}") for i in range(4)]
        vn_in = [sem("vn_in0"), sem("vn_in1")]
        kt_tr, kt_a, kt_v, kt_qk = sem("kt_tr"), sem("kt_a"), sem("kt_v"), sem("kt_qk")
        d_qk, d_mx, d_exp, d_p, d_ptr, d_pa, d_pv, d_o, d_oev = (
            sem(n) for n in ("d_qk", "d_mx", "d_exp", "d_p", "d_ptr", "d_pa", "d_pv", "d_o", "d_oev"))
        d_att = sem("d_att")
        g_in = [sem("g_in0"), sem("g_in1")]
        s_done = sem("s_done")
        ga_set, ga_in, ga_z, ga_step, ga_e, ga_ready = (
            sem(n) for n in ("ga_set", "ga_in", "ga_z", "ga_step", "ga_e", "ga_ready"))
        ga_lg, ga_at, ga_am, ga_kn, ga_u, ga_s, ga_o, ga_oe, ga_head = (
            sem(n) for n in ("ga_lg", "ga_at", "ga_am", "ga_kn", "ga_u", "ga_s", "ga_o", "ga_oe", "ga_head"))
        ga_so, ga_q = sem("ga_so"), sem("ga_q")
        ga_oo = [sem("ga_oo0"), sem("ga_oo1")]
        po_in = [sem("po_in0"), sem("po_in1")]
        po_set, po_v, po_sd, po_sl, po_ok, po_tr, po_hi, po_lo = (
            sem(n) for n in ("po_set", "po_v", "po_sd", "po_sl", "po_ok", "po_tr", "po_hi", "po_lo"))
        mg_hi, mg_lo, res_in = sem("mg_hi"), sem("mg_lo"), sem("res_in")
        l_var, l_std, l_ok, l_tr, l_hi, l_lo = (
            sem(n) for n in ("l_var", "l_std", "l_ok", "l_tr", "l_hi", "l_lo"))
        ln2_in = sem("ln2_in")
        f_relu, f_sq, f_hi, f_lo, f_half, f_add = (
            sem(n) for n in ("f_relu", "f_sq", "f_hi", "f_lo", "f_half", "f_add"))

        def barrier(eng, n):
            eng.drain().then_inc(stage, 1)
            eng.wait_ge(stage, 4 * n)

        OT = [(i, P * i, P) for i in range(8)] + [(8, SEQ, META), (9, TP, TS)]

        block = top.enter_context(nc.Block())

        @block.gpsimd
        def _(pool):
            for tile, v in ((ident[:, :], 0.0), (identb[:, :], 0.0), (tri[:, :], 0.0), (tri16[:, :], 0.0),
                            (causal[:, :], 1.0), (d8[:, :, :], 0.0), (pool_go[:, :], 0.0)):
                pool.memset(tile, v)
            pool.drain()
            selects = [
                (ident[:, :], ALU.not_equal, 1.0, [[-1, P]], 1),
                (identb[:, :], ALU.not_equal, 1.0, [[-1, P]], 1),
                (tri[:, :], ALU.is_ge, NEG, [[-1, P]], 1),
                (tri16[:, :], ALU.is_ge, NEG, [[-1, META]], 1),
                (causal[0:CH, :], ALU.is_ge, 0.0, [[1, CH]], -1),
                (causal[CH:P, :], ALU.is_ge, 0.0, [[1, CH]], -1),
                (d8[:, :, :], ALU.not_equal, 1.0, [[-DS, DB], [-1, DS]], 1)]
            for n, (tile, compare, fill, pattern, mult) in enumerate(selects):
                if n:
                    pool.wait_ge(consts, n)
                pool.affine_select(out=tile, in_=tile, compare_op=compare, fill=fill, base=0,
                                   pattern=pattern, channel_multiplier=mult).then_inc(consts, 1)
            pool.wait_ge(consts, 7)

            def split(s, landed, used):
                pool.wait_ge(raw_in[s], landed)
                if used is not None:
                    pool.wait_ge(unit_done, used)
                pool.tensor_tensor(pool_go[:, 0:1], pool_go[:, 1:2], pool_go[:, 1:2], ALU.mult)
                pool.tensor_copy(w_hi[:, s, :], raw[:, s, :])
                pool.drain()
                pool.tensor_tensor(w_lo[:, s, :], raw[:, s, :], w_hi[:, s, :].bitcast(F32),
                                   ALU.subtract).then_inc(w_split, 1)

            split(0, 16, None)
            split(1, 16, None)
            with pool.Fori(1, N_UNITS // 2) as i:
                for s in range(2):
                    split(s, 16 * i + 16, 2 * i + s - 1)
            split(0, 16 * (N_UNITS // 2) + 16, N_UNITS - 2)

        @block.sync
        def _(sp):
            def load_unit(u, s, landed_before=None):
                if landed_before is not None:
                    sp.wait_ge(w_split, landed_before)
                src = w_stream[u, :, :] if isinstance(u, int) else \
                    w_stream[bass.ds(u, 1), :, :].rearrange("u p n -> (u p) n")
                sp.dma_start(raw[:, s, :], src).then_inc(raw_in[s], 16)

            def load_units(u0, u1):
                for u in range(u0, u1):
                    load_unit(u, u % 2, u - 1 if u >= 2 else None)

            sp.dma_start(xin[:, 0, :], x_all[0:P, :]).then_inc(x_in[0], 16)
            sp.dma_start(xin[:, 1, :], x_all[P:2 * P, :]).then_inc(x_in[1], 16)
            sp.dma_start(lg[:, :], ln_p[0:1, :].broadcast_to((P, D))).then_inc(ln_in, 16)
            sp.dma_start(lb[:, :], ln_p[1:2, :].broadcast_to((P, D))).then_inc(ln_in, 16)
            sp.dma_start(pt_sb[:, :], page_table).then_inc(ln_in, 16)
            load_units(0, 2)
            for t in range(NT):
                r = rows_of(t)
                sp.wait_ge(h_ready, t + 1)
                sp.dma_start(h_d[P * t:P * t + r, :], hbuf[:r, t % 2, :]).then_inc(h_out[t % 2], 16)
                if t + 2 < NT:
                    sp.wait_ge(x_free, t + 1)
                    r = rows_of(t + 2)
                    sp.dma_start(xin[:r, t % 2, :], x_all[P * (t + 2):P * (t + 2) + r, :]).then_inc(x_in[t % 2], 16)
            sp.wait_ge(h_out[0], 16 * 5)
            sp.wait_ge(h_out[1], 16 * 4)
            sp.wait_ge(ln_in, 48)
            load_units(2, 4)
            barrier(sp, 1)

            sp.wait_ge(evac, 4)
            sp.dma_start(a1_d, kT3[:RANK, 3, :]).then_inc(misc_out, 16)
            sp.dma_start(wi_d, kT3[HD:HD + IH, 2, TP:T]).then_inc(misc_out, 16)
            for t in range(NT):
                sp.wait_ge(kn_ok, t + 1)
                src, s = relu[:, t % 2, 0:384], kn_out[t % 2]
                if t < 8:
                    at0 = META + P * t
                    sp.dma_start(k_p[at0:at0 + P, :], src[:, 0:256]).then_inc(s, 16)
                    sp.dma_start(ki_p[at0:at0 + P, :], src[:, 256:320]).then_inc(s, 16)
                else:
                    sp.dma_start(k_p[0:META, :], src[0:META, 0:256]).then_inc(s, 16)
                    sp.dma_start(ki_p[0:META, :], src[0:META, 256:320]).then_inc(s, 16)
                    sp.dma_start(k_s, src[META:80, 0:256]).then_inc(s, 16)
                    sp.dma_start(ki_s, src[META:80, 256:320]).then_inc(s, 16)
            sp.wait_ge(kn_out[0], 32 * 4 + 64)
            sp.wait_ge(kn_out[1], 32 * 4)

            def dup_keys(dst, src_rows, done):
                for half in range(2):
                    d = dst[HD * half:HD * half + HD, :]
                    sp.dma_start(d[:, 0:META], src_rows[:, SEQ:TP]).then_inc(done, 16)
                    sp.dma_start(d[:, META:TP], src_rows[:, 0:SEQ]).then_inc(done, 16)

            dup_keys(relu[:, 1, :], kT3[0:HD, 2, :], ks_in)

            sp.wait_ge(st_out[0], 32)
            sp.wait_ge(st_out[1], 32)
            qi_v = qiT_d.rearrange("(h d) t -> d h t", d=HD)
            for i in range(1, 8):
                if i >= 3:
                    sp.wait_ge(q_lo_ok, i - 2)
                for half in range(2):
                    sp.dma_start(qraw[HD * half:HD * half + HD, i % 2, :, :],
                                 qi_v[:, :, P * i:P * i + P]).then_inc(q_in[i % 2], 16)
            load_units(4, 6)
            barrier(sp, 2)

            sp.wait_ge(misc_out, 32)
            for h in range(IH):
                sp.dma_start(qiS[:, :, h, :], qiT_d[HD * h:HD * h + HD, TP:T].rearrange(
                    "d (b t) -> d b t", t=DS)).then_inc(sx_in, 16)
                sp.dma_start(wsel[DS * h:DS * h + DS, :], wi_d[h, :].rearrange(
                    "(b t) -> t b", t=DS), allow_slow_non_contiguous=True).then_inc(sx_in, 16)
            for b in range(DB):
                if b >= 2:
                    sp.wait_ge(kx_tr, 4 * (b - 1))
                for pg in range(NPG):
                    page = sp.value_load(pt_sb[0:1, NPG * b + pg:NPG * b + pg + 1], min_val=0, max_val=159)
                    sp.dma_start(kxraw[:, b % 2, pg, :], cache_kidx[bass.ds(page, 1), :, :].rearrange(
                        "a p d -> (a p) d")).then_inc(kx_in[b % 2], 16)
                if b >= 1:
                    sp.wait_ge(i_ev, 5 * b)
                    sp.dma_start(iscS[DS * (b - 1):DS * b, :], ib[:, :]).then_inc(ib_out, 16)
            sp.wait_ge(i_ev, 5 * DB)
            sp.dma_start(iscS[DS * (DB - 1):DS * DB, :], ib[:, :]).then_inc(ib_out, 16)
            barrier(sp, 3)

            load_units(6, 12)
            load_units(12, 16)
            sp.wait_ge(evac, evacs_before(U_N + 1))
            sp.dma_start(v_p[META:TP, :].rearrange("(t p) c -> p t c", p=P), vnat[:, 0:8, :]).then_inc(misc_out, 16)
            sp.dma_start(v_p[0:META, :], vnat[0:META, 8, :]).then_inc(misc_out, 16)
            sp.dma_start(v_s, vnat[META:80, 8, :]).then_inc(misc_out, 16)
            sp.dma_start(vs_d, vnat[META:80, 8, :]).then_inc(misc_out, 16)
            with sp.Fori(8, 16) as i:
                for s in range(2):
                    load_unit(2 * i + s, s, 2 * i + s - 1)
            load_unit(32, 0, 31)
            barrier(sp, 4)

            for n in range(NKV):
                if n >= 2:
                    sp.wait_ge(c_ks_ok, n - 1)
                dup_keys(pP[:, n % 2, :], kT3[HD * (n % 2):HD * (n % 2) + HD, n // 2, :], c_ks_in[n % 2])
            q_v = qT_d[0:1024, :].rearrange("(h d) t -> d h t", d=HD)
            for i in range(NT):
                r = rows_of(i)
                for n in range(NKV):
                    j = NKV * i + n
                    if j >= 2:
                        sp.wait_ge(cq_lo, j - 1)
                    for half in range(2):
                        sp.dma_start(qraw2[HD * half:HD * half + HD, j % 2, :, :r],
                                     q_v[:, G * n:G * n + G, P * i:P * i + r]).then_inc(cq_in[j % 2], 16)
            barrier(sp, 5)

            sp.wait_ge(d_set, 1)
            sp.wait_ge(misc_out, 16 * 6)
            for j in range(2):
                for n2 in range(2):
                    for g in range(G):
                        head = G * (2 * j + n2) + g
                        sp.dma_start(
                            qblk[HD * n2:HD * n2 + HD, j, :, DS * head:DS * head + DS],
                            qT_d[HD * head:HD * head + HD, TP:T].rearrange("d (b t) -> d b t", t=DS)
                        ).then_inc(d_cst, 16)

            def load_pages(dst, cache, b, grp, done):
                for j in range(4):
                    at0 = NPG * b + 4 * grp + j
                    page = sp.value_load(pt_sb[0:1, at0:at0 + 1], min_val=0, max_val=159)
                    sp.dma_start(dst[:, j, :], cache[bass.ds(page, 1), :, :].rearrange(
                        "a p d -> (a p) d")).then_inc(done, 16)

            for b in range(DB):
                for grp in range(4):
                    gg = 4 * b + grp
                    if gg >= 3:
                        sp.wait_ge(kt_tr, gg - 2)
                    load_pages(kpg[:, gg % 3, :, :], cache_k, b, grp, kg_in[gg % 3])
                if b >= 2:
                    sp.wait_ge(d_o, b - 1)
                sp.dma_start(vnew[:, b % 2, :], vs_d[DS * b:DS * b + DS, :]).then_inc(vn_in[b % 2], 16)
                for grp in range(4):
                    if b >= 1:
                        sp.wait_ge(d_o, b)
                    load_pages(vpg[:, grp, :, :], cache_v, b, grp, vg_in[grp])
            sp.wait_ge(d_oev, DB)
            for j in range(2):
                for n2 in range(2):
                    for g in range(G):
                        head = G * (2 * j + n2) + g
                        sp.dma_start(attT[HD * (head % 2):HD * (head % 2) + HD, head // 2, :],
                                     attS[HD * n2:HD * n2 + HD, j, g, :, :].rearrange("p b t -> p (b t)")
                                     ).then_inc(d_att, 16)
            barrier(sp, 6)

            def load_gates(dst, first, src2=None, dst2=None, base=0):
                for m in range(KC):
                    if m >= 2:
                        sp.wait_ge(evac, evacs_before(base) + m - 1)
                    sp.dma_start(dst[:, m % 2, :], gate_d[first + P * m:first + P * m + P, :]).then_inc(g_in[m % 2], 16)
                    if src2 is not None:
                        sp.dma_start(dst2[:, m % 2, :], src2[P * m:P * m + P, :]).then_inc(g_in[m % 2], 16)
                    if m % 2 == 1:
                        load_units(base + 4 + m // 2, base + 5 + m // 2)

            load_gates(gst, 0, base=U_PA)
            barrier(sp, 7)

            sp.dma_start(a1T[:, :], a1_d).then_inc(ga_set, 16)
            sp.dma_start(wa2[:, :], w_a2).then_inc(ga_set, 16)
            sp.dma_start(ba[:, :], b_a.rearrange("(h p) -> p h", p=P), allow_slow_non_contiguous=True).then_inc(ga_set, 16)
            for h in range(GH):
                if h:
                    sp.wait_ge(ga_head, h)
                    sp.wait_ge(ga_so, 32 * h)
                sp.dma_start(gq[:, :], qT_d[1024 + DK * h:1024 + DK * h + DK, :]).then_inc(ga_in, 16)
                sp.dma_start(gk[:, :], qT_d[1536 + DK * h:1536 + DK * h + DK, :]).then_inc(ga_in, 16)
                cols = gvog_d[:, DV * h:DV * h + DV]
                sp.dma_start(gv[:, 0:8, :], cols[0:SEQ, :].rearrange("(t p) c -> p t c", p=P)).then_inc(ga_in, 16)
                sp.dma_start(gv[0:META, 8, :], cols[SEQ:TP, :]).then_inc(ga_in, 16)
                sp.dma_start(gvs[:, :], cols[TP:T, :]).then_inc(ga_in, 16)
                sp.dma_start(s0[:, :, :], state[:, h, :, :].rearrange("b p v -> p b v")).then_inc(ga_in, 16)
                for n, (i, at0, r) in enumerate([OT[8]] + OT[:8] + [OT[9]]):
                    e = 10 * h + n
                    sp.wait_ge(ga_oe, e + 1)
                    sp.dma_start(o_d[at0:at0 + r, DV * h:DV * h + DV], ostg[:r, e % 2, :]).then_inc(ga_oo[e % 2], 16)
                sp.wait_ge(ga_s, 26 * (h + 1))
                sp.dma_start(st_p[h, :, :], sx[:, 0, :]).then_inc(ga_so, 16)
                sp.dma_start(st_s[:, h, :, :].rearrange("b p v -> p b v"), s0[:, :, :]).then_inc(ga_so, 16)
            sp.wait_ge(ga_so, 32 * GH)
            sp.wait_ge(ga_oo[0], 16 * 20)
            sp.wait_ge(ga_oo[1], 16 * 20)
            barrier(sp, 8)

            sp.dma_start(gnb[:, :], gnorm.broadcast_to((P, DV))).then_inc(po_set, 16)
            for n, (i, at0, r) in enumerate(OT):
                if n >= 2:
                    sp.wait_ge(po_tr, n - 1)
                sp.dma_start(oin[:r, n % 2, :], o_d[at0:at0 + r, :]).then_inc(po_in[n % 2], 16)
                sp.dma_start(ogin[:r, n % 2, :], gvog_d[at0:at0 + r, 1024:2048]).then_inc(po_in[n % 2], 16)
            barrier(sp, 9)
            load_gates(gst2, 1024, part_d, pst2, base=U_PG)
            barrier(sp, 10)

            sp.wait_ge(mg_lo, KC)
            sp.dma_start(res[:, 0:8, :], h_d[0:SEQ, :].rearrange("(t p) c -> p t c", p=P)).then_inc(res_in, 16)
            sp.dma_start(res[0:80, 8, :], h_d[SEQ:T, :]).then_inc(res_in, 16)
            sp.dma_start(lg2[:, :], ln_p[2:3, :].broadcast_to((P, D))).then_inc(ln2_in, 16)
            sp.dma_start(lb2[:, :], ln_p[3:4, :].broadcast_to((P, D))).then_inc(ln2_in, 16)
            load_units(41, 45)
            barrier(sp, 11)
            with sp.Fori(0, (N_UNITS - 45) // 2) as i:
                for s in range(2):
                    load_unit(2 * i + 45 + s, 1 - s, 2 * i + 44 + s)
            barrier(sp, 12)
            sp.dma_start(lg2[:, :], ln_p[4:5, :].broadcast_to((P, D))).then_inc(ln2_in, 16)
            sp.dma_start(lb2[:, :], ln_p[5:6, :].broadcast_to((P, D))).then_inc(ln2_in, 16)
            for t in range(NT):
                sp.wait_ge(l_ok, NT + t + 1)
                if t < 8:
                    sp.dma_start(y_p[P * t:P * t + P, :], res[:, t, :]).then_inc(misc_out, 16)
                else:
                    sp.dma_start(y_s, res[META:80, t, :]).then_inc(misc_out, 16)
            sp.wait_ge(misc_out, 16 * (6 + 9))

        @block.tensor
        def _(pe):
            def unit_f(s, ready, free):
                pe.wait_ge(w_split, ready)
                for c in range(2):
                    if free[c] is not None:
                        pe.wait_ge(evac, free[c])
                    for n in range(3):
                        out = ps[:, 3 * c + n, 0:N3]
                        cols = slice(N3 * n, N3 * n + N3)
                        for k in range(KC):
                            at0 = (KC * c + k) * P
                            hi, lo = w_hi[:, s, at0:at0 + P], w_lo[:, s, at0:at0 + P]
                            pe.matmul(out, hi, xt_hi[:, k, cols], start=k == 0, stop=False)
                            pe.matmul(out, hi, xt_lo[:, k, cols], start=False, stop=False)
                            last = pe.matmul(out, lo, xt_hi[:, k, cols], start=False, stop=k == KC - 1)
                    last.then_inc(unit_done if c else half_done, 1)

            def unit_n(s, ready, free, wait=None):
                pe.wait_ge(w_split, ready)
                for t in range(NT):
                    pe.wait_ge(evac, free + t)
                    r = rows_of(t)
                    out = ps[:r, t % 3, 0:256]
                    cols = slice(P * t, P * t + r)
                    for k in range(KC):
                        w = slice(256 * k, 256 * k + 256)
                        pe.matmul(out, xt_hi[:, k, cols], w_hi[:, s, w], start=k == 0, stop=False)
                        pe.matmul(out, xt_lo[:, k, cols], w_hi[:, s, w], start=False, stop=False)
                        last = pe.matmul(out, xt_hi[:, k, cols], w_lo[:, s, w], start=False, stop=k == KC - 1)
                    last.then_inc(unit_done if t == NT - 1 else half_done, 1)

            def transpose_tile(src, r, bank, done):
                for k in range(KC):
                    last = pe.transpose(flat[:, 512 * bank + P * k:512 * bank + P * k + r],
                                        src[:r, P * k:P * k + P], ident[:r, :r])
                last.then_inc(done, 1)

            pe.wait_ge(consts, 7)
            for t in range(NT):
                pe.wait_ge(h_ready, t + 1)
                if t >= 2:
                    pe.wait_ge(lo_ok, t - 1)
                transpose_tile(hbuf[:, t % 2, :], rows_of(t), 2 * (t % 2), tr_ok)
            pe.wait_ge(lo_ok, NT)
            barrier(pe, 1)

            for u in range(4):
                unit_f(u % 2, u + 1, [2 * u + c - 1 if 2 * u + c >= 2 else None for c in range(2)])
            for t in range(NT):
                r = rows_of(t)
                if t >= 2:
                    pe.wait_ge(kn_ok, t - 1)
                for c in range(3):
                    last = pe.transpose(ps[:r, 6 + t % 2, P * c:P * c + P], kT3[:, c, P * t:P * t + r], ident[:, :])
                last.then_inc(kn_tr, 1)

            pe.wait_ge(ks_ok, 1)
            pe.wait_ge(kn_ok, NT)
            pe.wait_ge(evac, 8)
            for i in range(1, 8):
                _, w, np_ = keys_of(i)
                pe.wait_ge(q_lo_ok, i)
                for h in range(IH):
                    g = IH * (i - 1) + h
                    if g >= 2:
                        pe.wait_ge(ix_relu, g - 1)
                    for p in range(np_):
                        out, keys = ps[:, 4 * (g % 2) + p, 0:w], kiS[:, w * p:w * p + w]
                        pe.matmul(out, qhi[:, h, :], keys, start=True, stop=False)
                        last = pe.matmul(out, qlo[:, h, :], keys, start=False, stop=True)
                    last.then_inc(ix_mm, 1)
            barrier(pe, 2)

            pe.wait_ge(sx_in, 16 * 16)
            pe.wait_ge(wb_ok, 1)
            width = [512] * 4 + [DS]
            for b in range(DB):
                def tr(grp):
                    gg = 4 * b + grp
                    if gg >= 2:
                        pe.wait_ge(kx_ev, 5 * ((gg - 2) // 4) + 2 + (gg - 2) % 4)
                    for j in range(4):
                        last = pe.transpose(ps[0:HD, gg % 2, P * j:P * j + P], kxraw[:, b % 2, 4 * grp + j, :], ident[:, :])
                    last.then_inc(kx_tr, 1)

                def sc(p):
                    q = 5 * b + p
                    pe.wait_ge(kx_ev, 5 * b + min(2 + p, 5))
                    if q >= 2:
                        pe.wait_ge(s_relu, q - 1)
                    pe.matmul(ps[0:HD, 2 + q % 2, 0:width[p]], qiS[:, b, :, :].rearrange("p h t -> p (h t)"),
                              kxT[:, 512 * p:512 * p + width[p]], start=True, stop=True).then_inc(s_mm, 1)

                def ws(p):
                    q = 5 * b + p
                    pe.wait_ge(s_relu, q + 1)
                    if q >= 2:
                        pe.wait_ge(i_ev, q - 1)
                    pe.matmul(ps[0:DS, 4 + q % 2, 0:width[p]], wb[:, b, :], relu2[:, q % 2, 0:width[p]],
                              start=True, stop=True).then_inc(i_mm, 1)

                pe.wait_ge(kx_in[b % 2], 256 * (b // 2 + 1))
                tr(0); tr(1); sc(0); tr(2); sc(1); ws(0); tr(3)
                sc(2); ws(1); sc(3); ws(2); sc(4); ws(3); ws(4)
            barrier(pe, 3)

            with pe.Fori(0, 4) as i:
                for s in range(2):
                    e0 = evacs_before(U_Q) + 2 * s
                    unit_f(s, 2 * i + (U_Q + s + 1), [4 * i + (e0 + c - 1) for c in range(2)])
            pe.wait_ge(evac, evacs_before(U_N))
            unit_n(0, U_N + 1, evacs_before(U_N) - 2)
            with pe.Fori(0, 4) as i:
                for s in range(2):
                    unit_n(1 - s, 2 * i + (U_N + s + 2), 18 * i + (evacs_before(U_N + 1 + s) - 2))
            pe.wait_ge(evac, evacs_before(U_GATE))
            with pe.Fori(0, 4) as i:
                for s in range(2):
                    e0 = evacs_before(U_GATE) + 2 * s
                    unit_f(1 - s, 2 * i + (U_GATE + s + 1), [4 * i + (e0 + c - 1) for c in range(2)])
            pe.wait_ge(evac, evacs_before(U_PA))
            barrier(pe, 4)

            pe.wait_ge(c_ks_ok, NKV)
            B = 0
            for i in range(NT):
                r = rows_of(i)
                L, w, np_ = keys_of(i)
                score = 3 if np_ == 3 else 2
                banks = [6] if np_ == 3 else [4, 5, 6]
                chunks = [(0, META)] + ([(META + P * j, P) for j in range(i + 1)] if i < 8 else [])
                mask = masks[:r, mask_at(i):mask_at(i) + w * np_] if i < 8 else tri16[:r, :]

                def qk(hh, n, g):
                    if hh >= 2:
                        pe.wait_ge(exp_ok, hh - 1)
                    for p in range(np_):
                        out, keys = ps[:r, score * (hh % 2) + p, 0:w], kS[:, n, w * p:w * p + w]
                        pe.matmul(out, qh2[:, g, :r], keys, start=True, stop=False)
                        pe.matmul(out, ql2[:, g, :r], keys, start=False, stop=False)
                        last = pe.matmul(out, identb[:r, :r], mask[:, w * p:w * p + w], start=False, stop=True)
                    last.then_inc(qk_ok, 1)

                def pv(hh, n):
                    nonlocal B
                    batches = [chunks[j:j + 4] for j in range(0, len(chunks), 4)]
                    pe.wait_ge(exp_ok, hh + 1)
                    first = B

                    def tr(j):
                        bank = banks[(first + j) % len(banks)]
                        before = first + j - len(banks) + 1
                        if before > 0:
                            pe.wait_ge(pt_v, (before + 1) // 2)
                            if before // 2:
                                pe.wait_ge(pt_a, before // 2)
                        for m, (at0, wid) in enumerate(batches[j]):
                            last = pe.transpose(ps[:wid, bank, P * m:P * m + r], pP[:r, hh % 2, at0:at0 + wid], ident[:r, :r])
                        last.then_inc(pt_tr, 1)

                    def av(j):
                        bb_ = first + j
                        pe.wait_ge(pt_a if bb_ % 2 else pt_v, bb_ // 2 + 1)
                        if j == 0 and hh:
                            pe.wait_ge(o_ev, hh)
                        for m, (at0, wid) in enumerate(batches[j]):
                            vt = 8 if at0 == 0 else (at0 - META) // P
                            last = pe.matmul(ps[:r, 7, 0:HD], ptb[:wid, bb_ % 2, P * m:P * m + r],
                                             vnat[:wid, vt, HD * n:HD * n + HD],
                                             start=at0 == 0, stop=at0 == chunks[-1][0])
                        last.then_inc(pv_ok, 1)

                    tr(0)
                    for j in range(len(batches)):
                        if j + 1 < len(batches):
                            tr(j + 1)
                        av(j)
                    B += len(batches)

                if i in (7, 8):
                    pe.wait_ge(pt_v, (B + 1) // 2)
                    pe.wait_ge(pt_a, B // 2)
                    pe.wait_ge(exp_ok, NH * i)
                if i:
                    pe.wait_ge(lo_ok, NT + i)
                order = [(n, g) for n in range(NKV) for g in range(G)]
                for m, (n, g) in enumerate(order):
                    if g == 0:
                        pe.wait_ge(cq_lo, NKV * i + n + 1)
                    qk(NH * i + m, n, g)
                    if m:
                        pv(NH * i + m - 1, order[m - 1][0])
                pv(NH * i + NH - 1, NKV - 1)
                pe.wait_ge(o_ev, NH * (i + 1))
                transpose_tile(attn, r, 0, att_tr)
            pe.wait_ge(lo_ok, 2 * NT)
            barrier(pe, 5)

            pe.wait_ge(d_cst, 16 * 16)
            pe.wait_ge(d_set, 2)
            pb = 0
            for b in range(DB):
                def ktr(gg):
                    pe.wait_ge(kg_in[gg % 3], 64 * (gg // 3 + 1))
                    if gg:
                        pe.wait_ge(kt_a, gg)
                        pe.wait_ge(kt_v, gg)
                    for j in range(2):
                        for m in range(4):
                            last = pe.transpose(ps[:, 5 + j, P * m:P * m + P], kpg[:, gg % 3, m, P * j:P * j + P], ident[:, :])
                    last.then_inc(kt_tr, 1)

                def scores(p, keys, wid):
                    out = ps[:, p, 0:wid]
                    for j in range(2):
                        pe.matmul(out, qblk[:, j, b, :], keys(j), start=j == 0, stop=False)
                    return pe.matmul(out, esel[:, b, :, :].rearrange("p h t -> p (h t)"),
                                     maskS[:, 512 * p:512 * p + wid], start=False, stop=True)

                if b:
                    pe.wait_ge(d_exp, b)
                    pe.wait_ge(d_oev, b)
                    pe.wait_ge(d_pa, 2 * b)
                    pe.wait_ge(d_pv, 3 * b)
                ktr(4 * b)
                for grp in range(4):
                    gg = 4 * b + grp
                    if grp < 3:
                        ktr(gg + 1)
                    pe.wait_ge(kt_a, gg + 1)
                    pe.wait_ge(kt_v, gg + 1)
                    scores(grp, lambda j: kt[:, gg % 2, j, :], 512).then_inc(kt_qk, 1)
                scores(4, lambda j: kT3[:, j, TP + DS * b:TP + DS * b + DS], DS).then_inc(d_qk, 1)
                pe.wait_ge(d_p, b + 1)
                pe.wait_ge(vn_in[b % 2], 16 * (b // 2 + 1))

                def ptr(j):
                    n = 5 * b + j
                    if j >= 2:
                        pe.wait_ge(d_pa if j % 2 else d_pv, 2 * b + (j - 2) // 2 + 1 if j % 2 else 3 * b + (j - 2) // 2 + 1)
                    if j < 4:
                        for m in range(4):
                            last = pe.transpose(ps[:, 5 + j % 2, P * m:P * m + P],
                                                pS[:, 512 * j + P * m:512 * j + P * m + P], ident[:, :])
                    else:
                        last = pe.transpose(ps[:DS, 5 + j % 2, 0:P], pS[:, PAST:NK], ident[:, :])
                    last.then_inc(d_ptr, 1)

                def av(j):
                    pe.wait_ge(d_pa if j % 2 else d_pv, 2 * b + j // 2 + 1 if j % 2 else 3 * b + j // 2 + 1)
                    if j < 4:
                        pe.wait_ge(vg_in[j], 64 * (b + 1))
                    wid = P if j < 4 else DS
                    for m in range(4 if j < 4 else 1):
                        for jj in range(2):
                            v = vpg[:, j, m, P * jj:P * jj + P] if j < 4 else vnew[:, b % 2, P * jj:P * jj + P]
                            last = pe.matmul(ps[:, 7 if jj else 4, 0:HD], v,
                                             ptS[:wid, j % 2, P * m + HD * jj:P * m + HD * jj + HD],
                                             start=j == 0 and m == 0, stop=j == 4)
                    last.then_inc(d_o if j == 4 else s_done, 1)

                ptr(0)
                for j in range(5):
                    if j < 4:
                        ptr(j + 1)
                    av(j)
            barrier(pe, 6)

            for u in range(U_PA, U_PG):
                e0 = evacs_before(u)
                unit_f(u % 2, u + 1, [e0 + c - 1 for c in range(2)])
            pe.wait_ge(evac, evacs_before(U_PG))
            barrier(pe, 7)

            pe.wait_ge(ga_set, 48)
            for h in range(GH):
                if h:
                    pe.wait_ge(ga_head, h)
                for n in range(3):
                    last = pe.matmul(ps[:, n, 0:N3], wa2[:, DK * h:DK * h + DK], a1T[:, N3 * n:N3 * n + N3],
                                     start=True, stop=True)
                last.then_inc(ga_lg, 1)
                pe.wait_ge(ga_ready, h + 1)
                order = [OT[8]] + OT[:8] + [OT[9]]

                def intra(n):
                    i, at0, r = order[n]
                    e = 10 * h + n
                    if e >= 2:
                        pe.wait_ge(ga_am, e - 1)
                        pe.wait_ge(ga_kn, e - 1)
                    if n in (0, 9):
                        pe.matmul(ps[:r, e % 2, 0:r], kd[:, at0:at0 + r], gq[:, at0:at0 + r], start=True, stop=True)
                    else:
                        for c in range(2):
                            cols = slice(at0 + CH * c, at0 + CH * c + CH)
                            pe.matmul(ps[CH * c:CH * c + CH, e % 2, 0:CH], kd[:, cols], gq[:, cols], start=True, stop=True)
                    pe.transpose(ps[:r, 2 + e % 2, 0:DK], gk[:, at0:at0 + r], ident[:, :]).then_inc(ga_at, 1)

                intra(0)
                for n in range(10):
                    i, at0, r = order[n]
                    e = 10 * h + n
                    if n < 9:
                        intra(n + 1)
                    pe.wait_ge(ga_am, e + 1)
                    pe.wait_ge(ga_kn, e + 1)
                    if n == 9:
                        pe.wait_ge(ga_q, h + 1)
                        pe.wait_ge(ga_oe, e)
                        out = ps[:TS, 6, 0:DV]
                        pe.matmul(out, at[:TS, e % 2, :], gvs[:, :], start=True, stop=False)
                        for b in range(DB):
                            last = pe.matmul(out, qdm[:, TS * b:TS * b + TS], s0[:, b, :], start=False, stop=b == DB - 1)
                        last.then_inc(ga_o, 1)
                        for half in range(4):
                            pe.wait_ge(ga_s, 26 * h + 17 + 2 * max(half - 1, 0))
                            for m in range(2):
                                b = 2 * half + m
                                last = pe.matmul(ps[:, 4 + half % 2, DV * m:DV * m + DV], kem[:, b, :], gvs[:, :],
                                                 start=True, stop=True)
                            last.then_inc(ga_u, 1)
                        continue
                    if n:
                        pe.wait_ge(ga_s, 26 * h + 2 * (n - 1) + 1)
                    elif h:
                        pe.wait_ge(ga_s, 26 * h)
                    if n == 0:
                        pe.matmul(ps[:, 4, 0:DV], ken[:r, e % 2, :], gv[:r, 8, :], start=True, stop=True).then_inc(ga_u, 1)
                    else:
                        for c in range(2):
                            rows = slice(CH * c, CH * c + CH)
                            last = pe.matmul(ps[:, 4 + c, 0:DV], ken[rows, e % 2, :],
                                             gv[rows, i, :], start=True, stop=True)
                        last.then_inc(ga_u, 1)
                    if e:
                        pe.wait_ge(ga_oe, e)
                    if n == 0:
                        pe.matmul(ps[:r, 6, 0:DV], at[:r, e % 2, 0:r], gv[:r, 8, :], start=True, stop=True).then_inc(ga_o, 1)
                    else:
                        for c in range(2):
                            rows = slice(CH * c, CH * c + CH)
                            pe.matmul(ps[rows, 6, 0:DV], at[rows, e % 2, :], gv[rows, i, :], start=True, stop=False)
                            chunk = 2 * (n - 1) + c
                            pe.wait_ge(ga_s, 26 * h + chunk + 1)
                            last = pe.matmul(ps[rows, 6, 0:DV], gq[:, at0 + CH * c:at0 + CH * c + CH],
                                             sx[:, chunk % 4, :], start=False, stop=True)
                        last.then_inc(ga_o, 1)
            barrier(pe, 8)
            for n, (i, at0, r) in enumerate(OT):
                pe.wait_ge(po_ok, n + 1)
                if n >= 2:
                    pe.wait_ge(po_lo, n - 1)
                transpose_tile(oin[:, n % 2, :], r, 2 * (n % 2), po_tr)
            pe.wait_ge(po_lo, 10)
            barrier(pe, 9)

            for u in range(U_PG, U_O):
                e0 = evacs_before(u)
                unit_f(u % 2, u + 1, [e0 + c - 1 for c in range(2)])
            pe.wait_ge(evac, evacs_before(U_O))
            barrier(pe, 10)
            pe.wait_ge(mg_lo, KC)
            for u in range(U_O, U_FF):
                unit_n(u % 2, u + 1, evacs_before(u) - 2)
            for t in range(NT):
                if t == 0:
                    pe.wait_ge(evac, evacs_before(U_FF))
                else:
                    if t >= 2:
                        pe.wait_ge(l_lo, t - 1)
                pe.wait_ge(l_ok, t + 1)
                transpose_tile(res[:, t, :], rows_of(t), 2 * (t % 2), l_tr)
            pe.wait_ge(l_lo, NT)
            barrier(pe, 11)

            def up(s, ready, free):
                pe.wait_ge(w_split, ready)
                for c in range(2):
                    if free is not None:
                        pe.wait_ge(f_relu, free + c)
                    for n in range(3):
                        out = ps[:, 3 * c + n, 0:N3]
                        cols = slice(N3 * n, N3 * n + N3)
                        for k in range(KC):
                            at0 = (KC * c + k) * P
                            hi, lo = w_hi[:, s, at0:at0 + P], w_lo[:, s, at0:at0 + P]
                            pe.matmul(out, hi, xt_hi[:, k, cols], start=k == 0, stop=False)
                            pe.matmul(out, hi, xt_lo[:, k, cols], start=False, stop=False)
                            last = pe.matmul(out, lo, xt_hi[:, k, cols], start=False, stop=k == KC - 1)
                    last.then_inc(unit_done if c else half_done, 1)

            def down(s, a, ready, hidden, adds):
                pe.wait_ge(w_split, ready)
                pe.wait_ge(f_lo, hidden)
                for m in range(2 * NT):
                    t, hf = m // 2, m % 2
                    r = rows_of(t)
                    if adds is not None:
                        pe.wait_ge(f_add, adds + m - 1)
                    elif m >= 2:
                        pe.wait_ge(f_add, m - 1)
                    out = ps[:r, 6 + m % 2, :]
                    for k in range(2):
                        cols = slice(P * t, P * t + r)
                        w = slice(1024 * k + 512 * hf, 1024 * k + 512 * hf + 512)
                        pe.matmul(out, a_hi[:, a, k, cols], w_hi[:, s, w], start=k == 0, stop=False)
                        pe.matmul(out, a_lo[:, a, k, cols], w_hi[:, s, w], start=False, stop=False)
                        last = pe.matmul(out, a_hi[:, a, k, cols], w_lo[:, s, w], start=False, stop=k == 1)
                    last.then_inc(unit_done if m == 2 * NT - 1 else f_half, 1)

            up(1, U_FF + 1, None)
            up(0, U_FF + 2, 1)
            down(1, 0, U_FF + 3, 2, None)
            with pe.Fori(0, (FB - 2) // 2) as i:
                for o in range(2):
                    up(0, 4 * i + (U_FF + 4 + 2 * o), 4 * i + (2 * o + 3))
                    down(1, 1 - o, 4 * i + (U_FF + 5 + 2 * o), 4 * i + (4 + 2 * o), 36 * i + 18 * (o + 1))
            down(0, 1, N_UNITS, 2 * FB, 18 * (FB - 1))
            barrier(pe, 12)

        @block.scalar
        def _(act):
            def chunk_ready(c, halves, units):
                act.wait_ge(unit_done if c else half_done, units if c else halves)

            def to_dram(e, dst, src, done):
                act.wait_ge(evac, e)
                act.dma_start(dst, src).then_inc(done, 16)

            for t in range(NT + 1):
                if t < NT:
                    r = rows_of(t)
                    act.wait_ge(var_ok, t + 1)
                    act.activation(small[:r, 2 + t % 2:3 + t % 2], small[:r, t % 2:t % 2 + 1], ACT.Sqrt).then_inc(std_ok, 1)
                if t:
                    r = rows_of(t - 1)
                    act.wait_ge(tr_ok, t)
                    src = flat[:, 1024 * ((t - 1) % 2):1024 * ((t - 1) % 2) + 1024].rearrange("p (k n) -> p k n", n=P)
                    act.activation(xt_hi[:, :, P * (t - 1):P * (t - 1) + r], src[:, :, :r], ACT.Copy).then_inc(hi_ok, 1)
            barrier(act, 1)

            for e in range(8):
                u, c = e // 2, e % 2
                chunk_ready(c, u + 1, u + 1)
                dst = kT3[:, e, :] if e < 4 else stg[:, c, :]
                if e >= 6:
                    act.wait_ge(st_out[c], 16)
                act.activation(dst.rearrange("p (n m) -> p n m", m=N3), ps[:, 3 * c:3 * c + 3, 0:N3], ACT.Copy).then_inc(evac, 1)
                if e >= 4:
                    to_dram(e + 1, qiT_d[P * (e - 4):P * (e - 4) + P, :], dst, st_out[c])
            act.wait_ge(ks_in, 64)
            act.activation(kiS[:, 0:TP], relu[:, 1, 0:TP], ACT.Copy).then_inc(ks_hi, 1)
            act.wait_ge(ks_ok, 1)
            for i in range(1, 8):
                _, w, np_ = keys_of(i)
                act.wait_ge(q_in[i % 2], 32 * ((i + 1) // 2 if i % 2 else i // 2))
                if i > 1:
                    act.wait_ge(ix_mm, IH * (i - 1))
                act.activation(qhi[:, :, :], qraw[:, i % 2, :, :], ACT.Copy).then_inc(q_hi_ok, 1)
                for h in range(IH):
                    g = IH * (i - 1) + h
                    act.wait_ge(ix_mm, g + 1)
                    if g >= 2:
                        act.wait_ge(ix_acc, g - 1)
                    act.activation(relu[:, g % 2, 0:w * np_].rearrange("p (n m) -> p n m", m=w),
                                   ps[:, 4 * (g % 2):4 * (g % 2) + np_, 0:w], ACT.Relu,
                                   scale=HD ** -0.5).then_inc(ix_relu, 1)
            barrier(act, 2)
            width = [512] * 4 + [DS]
            for q in range(5 * DB):
                w = width[q % 5]
                act.wait_ge(s_mm, q + 1)
                if q >= 2:
                    act.wait_ge(i_mm, q - 1)
                act.activation(relu2[:, q % 2, 0:w], ps[0:HD, 2 + q % 2, 0:w], ACT.Relu, scale=HD ** -0.5).then_inc(s_relu, 1)
            barrier(act, 3)

            def f_out(i, u0, per, n_before, dst, func):
                for s in range(2):
                    for c in range(2):
                        u = u0 + s
                        e = 4 * i + (evacs_before(u) + c)
                        chunk_ready(c, 2 * i + (halves_before(u) + 1), 2 * i + (u + 1))
                        act.wait_ge(st_out[c], 32 * i + 16 * (n_before + s))
                        act.activation(stg[:, c, :].rearrange("p (n m) -> p n m", m=N3),
                                       ps[:, 3 * c:3 * c + 3, 0:N3], func).then_inc(evac, 1)
                        rows = dst[bass.ds(512 * i + P * (2 * s + c), P), :]
                        to_dram(e + 1, rows, stg[:, c, :], st_out[c])

            with act.Fori(0, 4) as i:
                f_out(i, U_Q, 0, 2, qT_d, ACT.Copy)
            for t in range(NT):
                r = rows_of(t)
                if t == NT - 1:
                    act.wait_ge(unit_done, U_N + 1)
                else:
                    act.wait_ge(half_done, halves_before(U_N) + t + 1)
                act.activation(vnat[:r, t, :], ps[:r, t % 3, 0:256], ACT.Copy).then_inc(evac, 1)

            def n_out(u, i, first):
                for t in range(NT):
                    r, s = rows_of(t), t % 3
                    if t == NT - 1:
                        act.wait_ge(unit_done, 2 * i + (u + 1))
                    else:
                        act.wait_ge(half_done, 16 * i + (halves_before(u) + t + 1))
                    n = 3 * (u - U_N - 1) + t // 3
                    if n or not first:
                        act.wait_ge(nst_out[s], 96 * i + 16 * n)
                    act.activation(nst[:r, s, :], ps[:r, s, 0:256], ACT.Copy).then_inc(evac, 1)
                    e = 18 * i + (evacs_before(u) + t + 1)
                    col = 512 * i + 256 * (u - U_N - 1)
                    to_dram(e, gvog_d[P * t:P * t + r, bass.ds(col, 256)], nst[:r, s, :], nst_out[s])

            n_out(U_N + 1, 0, True)
            n_out(U_N + 2, 0, True)
            with act.Fori(1, 4) as i:
                n_out(U_N + 1, i, False)
                n_out(U_N + 2, i, False)
            with act.Fori(0, 4) as i:
                f_out(i, U_GATE, 0, 10, gate_d, ACT.Sigmoid)
            for c in range(2):
                act.wait_ge(st_out[c], 16 * 18)
            for s in range(3):
                act.wait_ge(nst_out[s], 16 * 24)
            barrier(act, 4)

            for n in range(NKV):
                act.wait_ge(c_ks_in[n % 2], 64 * (n // 2 + 1))
                act.activation(kS[:, n, 0:TP], pP[:, n % 2, 0:TP], ACT.Copy).then_inc(c_ks_hi, 1)
            act.wait_ge(c_ks_ok, NKV)
            B = 0
            for i in range(NT):
                r = rows_of(i)
                L, w, np_ = keys_of(i)
                score = 3 if np_ == 3 else 2
                banks = [6] if np_ == 3 else [4, 5, 6]
                n_chunks = 1 + (i + 1 if i < 8 else 0)
                sizes = [min(4, n_chunks - j) for j in range(0, n_chunks, 4)]

                def q_split(n):
                    j = NKV * i + n
                    act.wait_ge(cq_in[j % 2], 32 * (j // 2 + 1))
                    if j:
                        act.wait_ge(qk_ok, G * j)
                    act.activation(qh2[:, :, :r], qraw2[:, j % 2, :, :r], ACT.Copy).then_inc(cq_hi, 1)

                def exp(hh):
                    act.wait_ge(mx_ok, hh + 1)
                    if hh >= 2:
                        act.wait_ge(pt_tr, tr_before(hh - 1))
                    act.activation(pP[:r, hh % 2, 0:w * np_].rearrange("p (n m) -> p n m", m=w),
                                   ps[:r, score * (hh % 2):score * (hh % 2) + np_, 0:w], ACT.Exp,
                                   bias=mx[:r, 2 + hh % 2:3 + hh % 2], scale=HD ** -0.5,
                                   accum_out=rsum[:r, hh % NH:hh % NH + 1])
                    act.drain().then_inc(exp_ok, 1)

                def evac_p(hh):
                    nonlocal B
                    for j, size in enumerate(sizes):
                        if B % 2:
                            act.wait_ge(pt_tr, B + 1)
                            if B >= 2:
                                act.wait_ge(pv_ok, B - 1)
                            evac_pt(act.activation, B, j, size, banks, r, n_chunks)
                        B += 1

                def evac_pt(op, bt, j, size, banks, r, n_chunks):
                    bank = banks[bt % len(banks)]
                    lo = 0
                    if j == 0:
                        last = op(ptb[:META, bt % 2, 0:r], ps[:META, bank, 0:r], ACT.Copy)
                        lo = 1
                    if size > lo:
                        last = op(ptb[:, bt % 2, :].rearrange("p (m q) -> p m q", q=P)[:, lo:size, :r],
                                  ps[:, bank, :].rearrange("p (m q) -> p m q", q=P)[:, lo:size, :r], ACT.Copy)
                    last.then_inc(pt_a, 1)

                q_split(0)
                for m in range(NH):
                    exp(NH * i + m)
                    if m % G == G - 1 and m < NH - 1:
                        q_split(m // G + 1)
                    if m:
                        evac_p(NH * i + m - 1)
                evac_p(NH * i + NH - 1)
                act.wait_ge(att_tr, i + 1)
                cols = slice(P * i, P * i + (r if i < 8 else META))
                src = flat[:, 0:1024].rearrange("p (k n) -> p k n", n=P)
                act.activation(xt_hi[:, :, cols], src[:, :, :(r if i < 8 else META)], ACT.Copy).then_inc(hi_ok, 1)
            barrier(act, 5)

            for b in range(DB):
                for grp in range(4):
                    gg = 4 * b + grp
                    act.wait_ge(kt_tr, gg + 1)
                    if gg >= 2:
                        act.wait_ge(kt_qk, gg - 1)
                    act.activation(kt[:, gg % 2, 1, :], ps[:, 6, :], ACT.Copy).then_inc(kt_a, 1)
                act.wait_ge(d_mx, b + 1)
                if b:
                    act.wait_ge(d_ptr, 5 * b)
                act.activation(pS[:, :], flat[:, 0:NK], ACT.Exp, bias=mx[:, 1:2], scale=HD ** -0.5,
                               accum_out=rsum[:, 0:1])
                act.drain().then_inc(d_exp, 1)
                for j in (1, 3):
                    act.wait_ge(d_ptr, 5 * b + j + 1)
                    if j == 3:
                        act.wait_ge(s_done, 4 * b + 2)
                    elif b:
                        act.wait_ge(d_o, b)
                    act.activation(ptS[:, 1, :], ps[:, 6, :], ACT.Copy).then_inc(d_pa, 1)
            act.wait_ge(d_att, 16 * 16)
            act.activation(xt_hi[:, :, TP:T], attT[:, :, :], ACT.Copy).then_inc(hi_ok, 1)
            barrier(act, 6)

            for m in range(KC):
                to_dram(evacs_before(U_PA) + m + 1, part_d[P * m:P * m + P, :], pst[:, m % 2, :], st_out[m % 2])
            for c in range(2):
                act.wait_ge(st_out[c], 16 * 22)
            barrier(act, 7)

            act.wait_ge(ga_set, 48)
            for h in range(GH):
                act.wait_ge(ga_lg, h + 1)
                act.activation(zz[:, :].rearrange("p (n m) -> p n m", m=N3), ps[:, 0:3, 0:N3], ACT.Identity,
                               bias=ba[:, h:h + 1]).then_inc(ga_z, 1)
                act.wait_ge(ga_step, 4 * h + 1)
                act.activation(kd[:, :], kd[:, :], ACT.Exp)
                act.drain()
                act.activation(kd[:, :], kd[:, :], ACT.Ln, bias=1.0).then_inc(ga_e, 1)
                act.wait_ge(ga_step, 4 * h + 2)
                act.activation(zz[:, :], bb[:, :], ACT.Exp, scale=1.0 / TAU).then_inc(ga_e, 1)
                act.wait_ge(ga_step, 4 * h + 3)
                act.activation(zz[:, :], bb[:, :], ACT.Exp, scale=-1.0 / TAU).then_inc(ga_e, 1)
                act.wait_ge(ga_step, 4 * h + 4)
                act.activation(zz[:, :], zz[:, :], ACT.Exp, scale=1.0 / TAU).then_inc(ga_e, 1)
                order = [OT[8]] + OT[:8] + [OT[9]]
                for n in range(11):
                    if n < 10:
                        i, at0, r = order[n]
                        e = 10 * h + n
                        act.wait_ge(ga_at, e + 1)
                        if e >= 2:
                            act.wait_ge(ga_o, e - 1)
                            act.wait_ge(ga_u, 13 * h + n - 1 if n >= 2 else 13 * h)
                        act.activation(ken[:r, e % 2, :], ps[:r, 2 + e % 2, 0:DK], ACT.Copy).then_inc(ga_kn, 1)
                    if n:
                        i, at0, r = order[n - 1]
                        e = 10 * h + n - 1
                        act.wait_ge(ga_o, e + 1)
                        if e >= 2:
                            act.wait_ge(ga_oo[e % 2], 16 * (e // 2))
                        act.activation(zz[:r, 0:DV], ps[:r, 6, 0:DV], ACT.Square, accum_out=ssq[:r, i, h:h + 1])
                        act.activation(ostg[:r, e % 2, :], ps[:r, 6, 0:DV], ACT.Copy).then_inc(ga_oe, 1)
            barrier(act, 8)

            act.wait_ge(po_v, 1)
            act.activation(ssq[:, :, :], ssq[:, :, :], ACT.Sqrt).then_inc(po_sd, 1)
            for n in range(11):
                if n < 10:
                    i, at0, r = OT[n]
                    act.wait_ge(po_in[n % 2], 32 * (n // 2 + 1))
                    act.activation(ogin[:r, n % 2, :], ogin[:r, n % 2, :], ACT.Silu).then_inc(po_sl, 1)
                if n:
                    i, at0, r = OT[n - 1]
                    act.wait_ge(po_tr, n)
                    src = flat[:, 1024 * ((n - 1) % 2):1024 * ((n - 1) % 2) + 1024].rearrange("p (k n) -> p k n", n=P)
                    act.activation(xt_hi[:, :, at0:at0 + r], src[:, :, :r], ACT.Copy).then_inc(po_hi, 1)
            barrier(act, 9)
            barrier(act, 10)
            for c in range(KC):
                act.activation(xt_hi[:, c, :], merged[:, c, :], ACT.Copy).then_inc(mg_hi, 1)

            for t in range(NT + 1):
                if t < NT:
                    r = rows_of(t)
                    act.wait_ge(l_var, t + 1)
                    act.activation(small[:r, 2 + t % 2:3 + t % 2], small[:r, t % 2:t % 2 + 1], ACT.Sqrt).then_inc(l_std, 1)
                if t:
                    r = rows_of(t - 1)
                    act.wait_ge(l_tr, t)
                    src = flat[:, 1024 * ((t - 1) % 2):1024 * ((t - 1) % 2) + 1024].rearrange("p (k n) -> p k n", n=P)
                    act.activation(xt_hi[:, :, P * (t - 1):P * (t - 1) + r], src[:, :, :r], ACT.Copy).then_inc(l_hi, 1)
            barrier(act, 11)

            def hidden(a, halves, units, lows, squares, used):
                for c in range(2):
                    chunk_ready(c, halves, units)
                    if lows is not None:
                        act.wait_ge(f_lo, lows + c)
                    act.activation(rl[:, c, :].rearrange("p (n m) -> p n m", m=N3), ps[:, 3 * c:3 * c + 3, 0:N3],
                                   ACT.Relu).then_inc(f_relu, 1)
                    act.wait_ge(f_sq, squares + c)
                    if used is not None:
                        act.wait_ge(unit_done, used)
                    act.activation(a_hi[:, a, c, :], rl[:, c, :], ACT.Copy).then_inc(f_hi, 1)

            hb = halves_before(U_FF)
            hidden(0, hb + 1, U_FF + 1, None, 1, None)
            hidden(1, hb + 2, U_FF + 2, 1, 3, None)
            with act.Fori(0, (FB - 2) // 2) as i:
                for o in range(2):
                    hidden(o, 2 * i + (hb + 3 + o), 4 * i + (U_FF + 4 + 2 * o), 4 * i + (3 + 2 * o),
                           4 * i + (5 + 2 * o), 4 * i + (U_FF + 3 + 2 * o))
            barrier(act, 12)
            for t in range(NT):
                r = rows_of(t)
                act.wait_ge(l_var, NT + t + 1)
                act.activation(small[:r, 2 + t % 2:3 + t % 2], small[:r, t % 2:t % 2 + 1], ACT.Sqrt).then_inc(l_std, 1)

        @block.vector
        def _(dve):
            def norm_stats(x, r, t, st, m, ok):
                for half in range(2):
                    dve.bn_stats(st[:r, t % 2, half, :], x[:r, 512 * half:512 * half + 512])
                dve.drain()
                dve.bn_aggr(m[:r, t % 2, :], st[:r, t % 2, :, :])
                dve.drain()
                dve.tensor_scalar(small[:r, t % 2:t % 2 + 1], m[:r, t % 2, 1:2], EPS, None, ALU.add).then_inc(ok, 1)

            def norm_apply(y, x, r, t, m, g, b, free, ok):
                dve.reciprocal(small[:r, 4 + t % 2:5 + t % 2], small[:r, 2 + t % 2:3 + t % 2])
                dve.drain()
                ins = dve.tensor_scalar(y[:r, :], x[:r, :], m[:r, t % 2, 0:1], small[:r, 4 + t % 2:5 + t % 2],
                                        ALU.subtract, ALU.mult)
                if free is not None:
                    ins.then_inc(free, 1)
                dve.drain()
                dve.tensor_tensor(y[:r, :], y[:r, :], g[:r, :], ALU.mult)
                dve.drain()
                dve.tensor_tensor(y[:r, :], y[:r, :], b[:r, :], ALU.add).then_inc(ok, 1)

            def lo_part(cols, slot, ok):
                n = cols.stop - cols.start
                src = flat[:, 1024 * slot:1024 * slot + 1024].rearrange("p (k n) -> p k n", n=P)
                dve.tensor_tensor(xt_lo[:, :, cols], src[:, :, :n], xt_hi[:, :, cols].bitcast(F32),
                                  ALU.subtract).then_inc(ok, 1)

            dve.wait_ge(x_in[0], 16)
            norm_stats(xin[:, 0, :], rows_of(0), 0, stats, mv, var_ok)
            dve.wait_ge(ln_in, 48)
            for t in range(NT + 1):
                if t + 1 < NT:
                    dve.wait_ge(x_in[(t + 1) % 2], 16 * ((t + 1) // 2 + 1))
                    norm_stats(xin[:, (t + 1) % 2, :], rows_of(t + 1), t + 1, stats, mv, var_ok)
                if t < NT:
                    dve.wait_ge(std_ok, t + 1)
                    if t >= 2:
                        dve.wait_ge(h_out[t % 2], 16 * (t // 2))
                        dve.wait_ge(tr_ok, t - 1)
                    norm_apply(hbuf[:, t % 2, :], xin[:, t % 2, :], rows_of(t), t, mv, lg, lb, x_free, h_ready)
                if t:
                    dve.wait_ge(hi_ok, t)
                    lo_part(slice(P * (t - 1), P * (t - 1) + rows_of(t - 1)), (t - 1) % 2, lo_ok)
            dve.memset(ssq[:, :, :], 0.0)
            dve.wait_ge(consts, 7)
            dve.tensor_reduce(delta[:, :], d8[:, :, :].rearrange("p i j -> p j i"), AX.X, ALU.add)
            dve.tensor_reduce(bsel[:, :], d8[:, :, :], AX.X, ALU.add)
            for t in range(DS):
                dve.memset(m8[:TS, t:t + 1], float(t))
            dve.drain()
            dve.tensor_tensor(triS[:, :], delta[:, :], m8[:TS, :], ALU.mult)
            dve.drain()
            dve.tensor_reduce(small[:TS, 8:9], triS[:, :], AX.X, ALU.add)
            dve.drain()
            dve.tensor_scalar(triS[:, :], m8[:TS, :], small[:TS, 8:9], NEG, ALU.is_gt, ALU.mult)
            barrier(dve, 1)

            dve.memset(kiS[:, TP:1056].bitcast(F32), 0.0)
            for t in range(NT):
                r = rows_of(t)
                dve.wait_ge(kn_tr, t + 1)
                if t >= 2:
                    dve.wait_ge(kn_out[t % 2], 32 * (t // 2))
                dve.tensor_scalar(winat[:r, t, :], ps[:r, 6 + t % 2, 256 + HD:256 + HD + IH], IH ** -0.5, None, ALU.mult)
                dve.tensor_copy(relu[:r, t % 2, 0:384], ps[:r, 6 + t % 2, 0:384]).then_inc(kn_ok, 1)
            dve.wait_ge(ks_hi, 1)
            lower = slice(HD, P)
            dve.tensor_tensor(kiS[lower, 0:TP], relu[lower, 1, 0:TP], kiS[lower, 0:TP].bitcast(F32),
                              ALU.subtract).then_inc(ks_ok, 1)
            for i in range(1, 8):
                L, w, np_ = keys_of(i)
                acc = isc[:, mask_at(i):mask_at(i) + L]
                dve.wait_ge(q_hi_ok, i)
                dve.tensor_tensor(qlo[:, :, :], qraw[:, i % 2, :, :], qhi[:, :, :].bitcast(F32),
                                  ALU.subtract).then_inc(q_lo_ok, 1)
                for h in range(IH):
                    g = IH * (i - 1) + h
                    dve.wait_ge(ix_relu, g + 1)
                    if h == 0:
                        dve.tensor_scalar(acc, relu[:, g % 2, 0:L], winat[:, i, 0:1], None, ALU.mult).then_inc(ix_acc, 1)
                    else:
                        dve.wait_ge(ix_acc, g)
                        dve.scalar_tensor_tensor(acc, relu[:, g % 2, 0:L], winat[:, i, h:h + 1], acc,
                                                 ALU.mult, ALU.add).then_inc(ix_acc, 1)
                dve.drain()
                dve.tensor_tensor(acc[:, L - P:L], acc[:, L - P:L], tri[:, :], ALU.add)
            barrier(dve, 2)

            dve.wait_ge(sx_in, 16 * 16)
            for b in range(DB):
                dve.tensor_scalar(wb[:, b, :], delta[:, :], wsel[:, b:b + 1], IH ** -0.5, ALU.mult, ALU.mult)
            dve.drain().then_inc(wb_ok, 1)
            width = [512] * 4 + [DS]
            for b in range(DB):
                def ev(grp):
                    gg = 4 * b + grp
                    dve.wait_ge(kx_tr, gg + 1)
                    dve.tensor_copy(kxT[:, 512 * grp:512 * grp + 512], ps[0:HD, gg % 2, :]).then_inc(kx_ev, 1)

                def ib_ev(p):
                    q = 5 * b + p
                    dve.wait_ge(i_mm, q + 1)
                    dve.tensor_copy(ib[:, 512 * p:512 * p + width[p]], ps[0:DS, 4 + q % 2, 0:width[p]]).then_inc(i_ev, 1)

                if b:
                    dve.wait_ge(s_mm, 5 * b)
                dve.tensor_copy(kxT[:, PAST:NK], kT3[0:HD, 2, TP + DS * b:TP + DS * b + DS]).then_inc(kx_ev, 1)
                ev(0); ev(1); ev(2)
                if b:
                    dve.wait_ge(ib_out, 16 * b)
                ib_ev(0); ev(3); ib_ev(1); ib_ev(2); ib_ev(3); ib_ev(4)
            dve.wait_ge(ib_out, 16 * DB)
            dve.tensor_tensor(iscS[:, PAST:NK], iscS[:, PAST:NK], triS[:, :], ALU.add)
            barrier(dve, 3)

            def top_k(scores, r):
                with dve.Fori(0, TOPK // 8):
                    dve.drain()
                    dve.max(m8[:r, :], scores)
                    dve.drain()
                    dve.match_replace(scores, m8[:r, :], scores, TAKEN)
                dve.drain()

            dve.memset(masks[:, 0:META], 0.0)
            dve.tensor_copy(masks[:, META:META + P], tri[:, :])
            dve.memset(masks[:, mask_at(7) + TP:IW], NEG)
            for i in range(1, 8):
                L, w, np_ = keys_of(i)
                part = isc[:, mask_at(i):mask_at(i) + L]
                top_k(part, P)
                mk = masks[:, mask_at(i):mask_at(i) + L]
                dve.tensor_scalar(mk, part, -2e38, NEG, ALU.is_gt, ALU.mult)
                dve.drain()
                dve.tensor_tensor(mk[:, L - P:L], mk[:, L - P:L], tri[:, :], ALU.add)
            top_k(iscS[:, :], TS)
            dve.tensor_scalar(maskS[:, :], iscS[:, :], -2e38, NEG, ALU.is_gt, ALU.mult)
            dve.drain()
            dve.tensor_tensor(maskS[:, PAST:NK], maskS[:, PAST:NK], triS[:, :], ALU.add)
            barrier(dve, 4)

            for n in range(NKV):
                dve.memset(kS[:, n, TP:1056].bitcast(F32), 0.0)
                dve.wait_ge(c_ks_hi, n + 1)
                dve.tensor_tensor(kS[lower, n, 0:TP], pP[lower, n % 2, 0:TP], kS[lower, n, 0:TP].bitcast(F32),
                                  ALU.subtract).then_inc(c_ks_ok, 1)
            B = 0
            for i in range(NT):
                r = rows_of(i)
                L, w, np_ = keys_of(i)
                score = 3 if np_ == 3 else 2
                banks = [6] if np_ == 3 else [4, 5, 6]
                n_chunks = 1 + (i + 1 if i < 8 else 0)
                sizes = [min(4, n_chunks - j) for j in range(0, n_chunks, 4)]

                def q_split(n):
                    j = NKV * i + n
                    dve.wait_ge(cq_hi, j + 1)
                    dve.tensor_tensor(ql2[:, :, :r], qraw2[:, j % 2, :, :r], qh2[:, :, :r].bitcast(F32),
                                      ALU.subtract).then_inc(cq_lo, 1)

                def row_max(hh):
                    dve.wait_ge(qk_ok, hh + 1)
                    s = hh % 2
                    dve.tensor_reduce(mx[:r, s:s + 1], ps[:r, score * s:score * s + np_, 0:w], AX.XY, ALU.max)
                    dve.drain()
                    dve.tensor_scalar(mx[:r, 2 + s:3 + s], mx[:r, s:s + 1], -HD ** -0.5, None, ALU.mult).then_inc(mx_ok, 1)

                def evac_p(hh):
                    nonlocal B
                    for j, size in enumerate(sizes):
                        if B % 2 == 0:
                            dve.wait_ge(pt_tr, B + 1)
                            if B >= 2:
                                dve.wait_ge(pv_ok, B - 1)
                            bank, first = banks[B % len(banks)], 0
                            if j == 0:
                                last = dve.tensor_copy(ptb[:META, B % 2, 0:r], ps[:META, bank, 0:r])
                                first = 1
                            if size > first:
                                last = dve.tensor_copy(
                                    ptb[:, B % 2, :].rearrange("p (m q) -> p m q", q=P)[:, first:size, :r],
                                    ps[:, bank, :].rearrange("p (m q) -> p m q", q=P)[:, first:size, :r])
                            last.then_inc(pt_v, 1)
                        B += 1

                def scale(hh):
                    m = hh % NH
                    dve.wait_ge(exp_ok, hh + 1)
                    inv = small[:r, 12 + m % 2:13 + m % 2]
                    dve.reciprocal(inv, rsum[:r, m:m + 1])
                    dve.drain()
                    if m == 0 and i:
                        dve.wait_ge(att_tr, i)
                    dve.wait_ge(pv_ok, B)
                    dve.tensor_scalar(attn[:r, HD * m:HD * m + HD], ps[:r, 7, 0:HD], inv, None,
                                      ALU.mult).then_inc(o_ev, 1)

                q_split(0)
                for m in range(NH):
                    row_max(NH * i + m)
                    if m % G == G - 1 and m < NH - 1:
                        q_split(m // G + 1)
                    if m:
                        evac_p(NH * i + m - 1)
                        scale(NH * i + m - 1)
                evac_p(NH * i + NH - 1)
                scale(NH * i + NH - 1)
                dve.wait_ge(hi_ok, NT + i + 1)
                lo_part(slice(P * i, P * i + (r if i < 8 else META)), 0, lo_ok)
            barrier(dve, 5)

            dve.memset(qblk[:, :, :, :], 0.0)
            dve.drain().then_inc(d_set, 1)
            for b in range(DB):
                dve.tensor_scalar(esel[:, b, :, :], delta[:, None, :].broadcast_to((TS, NH, DS)), bsel[:, b:b + 1],
                                  None, ALU.mult)
            dve.drain().then_inc(d_set, 1)
            for b in range(DB):
                for grp in range(4):
                    gg = 4 * b + grp
                    dve.wait_ge(kt_tr, gg + 1)
                    if gg >= 2:
                        dve.wait_ge(kt_qk, gg - 1)
                    dve.tensor_copy(kt[:, gg % 2, 0, :], ps[:, 5, :]).then_inc(kt_v, 1)
                dve.wait_ge(d_qk, b + 1)
                dve.tensor_reduce(mx[:, 0:1], flat[:, 0:NK], AX.X, ALU.max)
                dve.drain()
                dve.tensor_scalar(mx[:, 1:2], mx[:, 0:1], -HD ** -0.5, None, ALU.mult).then_inc(d_mx, 1)
                dve.wait_ge(d_exp, b + 1)
                dve.reciprocal(small[:, 9:10], rsum[:, 0:1])
                dve.drain()
                dve.tensor_scalar(pS[:, :], pS[:, :], small[:, 9:10], None, ALU.mult).then_inc(d_p, 1)
                for j in (0, 2, 4):
                    dve.wait_ge(d_ptr, 5 * b + j + 1)
                    if j:
                        dve.wait_ge(s_done, 4 * b + j - 1)
                    wid, n = (P, 512) if j < 4 else (DS, P)
                    dve.tensor_copy(ptS[:wid, 0, 0:n], ps[:wid, 5, 0:n]).then_inc(d_pv, 1)
                dve.wait_ge(d_o, b + 1)
                for jj in range(2):
                    for n2 in range(2):
                        rows = slice(HD * n2, HD * n2 + HD)
                        last = dve.tensor_copy(attS[rows, jj, :, b, :],
                                               ps[rows, 7 if jj else 4, 32 * n2:32 * n2 + 32].rearrange("p (g t) -> p g t", t=DS))
                last.then_inc(d_oev, 1)
            dve.wait_ge(hi_ok, 2 * NT + 1)
            dve.tensor_tensor(xt_lo[:, :, TP:T], attT[:, :, :], xt_hi[:, :, TP:T].bitcast(F32), ALU.subtract)
            barrier(dve, 6)

            def gated(m, base, g, dst, add=None, per=16, n0=0):
                e = evacs_before(base) + m
                u = base + m // 2
                if m % 2:
                    dve.wait_ge(unit_done, u + 1)
                else:
                    dve.wait_ge(half_done, halves_before(u) + 1)
                dve.wait_ge(g_in[m % 2], n0 + per * (m // 2 + 1))
                v = lambda a: a.rearrange("p (n m) -> p n m", m=N3)
                ins = dve.tensor_tensor(v(dst), ps[:, 3 * (m % 2):3 * (m % 2) + 3, 0:N3], v(g[:, m % 2, :]), ALU.mult)
                if add is not None:
                    dve.drain()
                    ins = dve.tensor_tensor(dst, dst, add[:, m % 2, :], ALU.add)
                ins.then_inc(evac, 1)

            for m in range(KC):
                if m >= 2:
                    dve.wait_ge(st_out[m % 2], 16 * (18 + m // 2))
                gated(m, U_PA, gst, pst[:, m % 2, :])
            barrier(dve, 7)

            dve.memset(reset[:, :], 1.0)
            dve.memset(qdm[:, :], 0.0)
            dve.drain()
            dve.memset(reset[:, 0:SEQ].rearrange("p (c n) -> p c n", n=CH)[:, :, 0:1], 0.0)
            dve.memset(reset[:, SEQ:SEQ + 1], 0.0)
            dve.memset(reset[:, TP:T].rearrange("p (c n) -> p c n", n=DS)[:, :, 0:1], 0.0)
            dve.tensor_tensor(bd64[:, :].rearrange("p (b t) -> p b t", t=DS),
                              causal[:TS, :].rearrange("p (b t) -> p b t", t=DS),
                              bsel[:, :].unsqueeze(2).broadcast_to((TS, DB, DS)), ALU.mult)
            segs = [(0, SEQ, CH), (SEQ, TP, META), (TP, T, DS)]
            for h in range(GH):
                dve.wait_ge(ga_z, h + 1)
                dve.scalar_tensor_tensor(kd[:, :], zz[:, :], -1.0, zz[:, :], ALU.mult, ALU.min).then_inc(ga_step, 1)
                dve.wait_ge(ga_e, 4 * h + 1)
                dve.scalar_tensor_tensor(zz[:, :], zz[:, :], 0.0, kd[:, :], ALU.min, ALU.subtract)
                dve.drain()
                dve.tensor_tensor_scan(bb[:, :], reset[:, :], zz[:, :], 0.0, ALU.mult, ALU.add).then_inc(ga_step, 1)
                dve.wait_ge(ga_in, 96 * (h + 1))
                dve.wait_ge(ga_e, 4 * h + 2)
                dve.scalar_tensor_tensor(gq[:, :], gq[:, :], DK ** -0.5, zz[:, :], ALU.mult, ALU.mult)
                for (a, z, n), at0 in zip(segs, (0, 16, 17)):
                    k = (z - a) // n
                    dve.tensor_copy(dec[:, at0:at0 + k].unsqueeze(2),
                                    zz[:, a:z].rearrange("p (c n) -> p c n", n=n)[:, :, n - 1:n])
                dve.drain().then_inc(ga_step, 1)
                dve.wait_ge(ga_e, 4 * h + 3)
                dve.tensor_tensor(kd[:, :], gk[:, :], zz[:, :], ALU.mult)
                dve.drain()
                for a, z, n in segs:
                    v = bb[:, a:z].rearrange("p (c n) -> p c n", n=n)
                    dve.tensor_tensor(zz[:, a:z].rearrange("p (c n) -> p c n", n=n),
                                      v[:, :, n - 1:n].broadcast_to((P, (z - a) // n, n)), v, ALU.subtract)
                dve.drain().then_inc(ga_step, 1)
                dve.wait_ge(ga_e, 4 * h + 4)
                dve.tensor_tensor(gk[:, :], gk[:, :], zz[:, :], ALU.mult)
                dve.tensor_copy(qdm[:, :].rearrange("p (b c) -> p b c", c=72)[:, :, 0:DS],
                                gq[:, TP:T].rearrange("p (b t) -> p b t", t=DS))
                dve.drain().then_inc(ga_ready, 1)
                order = [OT[8]] + OT[:8] + [OT[9]]
                if h:
                    dve.wait_ge(ga_so, 32 * h)
                for n in range(11):
                    if n < 10:
                        i, at0, r = order[n]
                        e = 10 * h + n
                        dve.wait_ge(ga_at, e + 1)
                        if e >= 2:
                            dve.wait_ge(ga_o, e - 1)
                        wid = META if n == 0 else CH
                        m = bd64 if n == 9 else causal
                        dve.tensor_tensor(at[:r, e % 2, 0:wid], ps[:r, e % 2, 0:wid], m[:r, 0:wid], ALU.mult).then_inc(ga_am, 1)
                    if n == 0:
                        continue
                    nn = n - 1
                    e = 10 * h + nn
                    if nn == 0:
                        dve.wait_ge(ga_u, 13 * h + 1)
                        dve.tensor_copy(sx[:, 0, :], ps[:, 4, 0:DV]).then_inc(ga_s, 1)
                    elif nn < 9:
                        dve.wait_ge(ga_u, 13 * h + nn + 1)
                        for c in range(2):
                            chunk = 2 * (nn - 1) + c
                            dve.wait_ge(ga_s, 26 * h + chunk + 1)
                            if chunk >= 3:
                                dve.wait_ge(ga_o, 10 * h + (chunk - 3) // 2 + 2)
                            dve.scalar_tensor_tensor(sx[:, (chunk + 1) % 4, :], sx[:, chunk % 4, :],
                                                     dec[:, chunk:chunk + 1],
                                                     ps[:, 4 + c, 0:DV], ALU.mult, ALU.add).then_inc(ga_s, 1)
                i, at0, r = order[9]
                dve.wait_ge(ga_kn, 10 * h + 10)
                dve.tensor_tensor(kem[:, :, :], ken[:TS, (10 * h + 9) % 2, :][:, None, :].broadcast_to((TS, DB, DK)),
                                  bsel[:, :].unsqueeze(2).broadcast_to((TS, DB, DK)), ALU.mult).then_inc(ga_q, 1)
                dve.wait_ge(ga_o, 10 * h + 10)
                for b in range(DB):
                    if b % 2 == 0:
                        dve.wait_ge(ga_u, 13 * h + 9 + b // 2 + 1)
                    dve.scalar_tensor_tensor(s0[:, b, :], s0[:, b, :], dec[:, 17 + b:18 + b],
                                             ps[:, 4 + (b // 2) % 2, DV * (b % 2):DV * (b % 2) + DV],
                                             ALU.mult, ALU.add).then_inc(ga_s, 1)
                dve.drain().then_inc(ga_s, 1)
                dve.wait_ge(ga_oe, 10 * h + 10)
                dve.drain().then_inc(ga_head, 1)
            barrier(dve, 8)

            dve.memset(small[:, 10:11], 0.0)
            dve.tensor_scalar(ssq[:, :, :], ssq[:, :, :], 1.0 / DV, EPS, ALU.mult, ALU.add).then_inc(po_v, 1)
            dve.wait_ge(po_sd, 1)
            dve.reciprocal(ssq[:, :, :], ssq[:, :, :])
            dve.wait_ge(po_set, 16)
            dve.drain()
            for n in range(11):
                if n < 10:
                    i, at0, r = OT[n]
                    dve.wait_ge(po_in[n % 2], 32 * (n // 2 + 1))
                    o = oin[:r, n % 2, :].rearrange("p (h v) -> p h v", v=DV)
                    for h in range(GH):
                        dve.scalar_tensor_tensor(o[:, h, :], o[:, h, :], ssq[:r, i, h:h + 1], gnb[:r, :], ALU.mult, ALU.mult)
                    dve.wait_ge(po_sl, n + 1)
                    dve.drain()
                    dve.tensor_tensor(oin[:r, n % 2, :], oin[:r, n % 2, :], ogin[:r, n % 2, :], ALU.mult).then_inc(po_ok, 1)
                if n:
                    i, at0, r = OT[n - 1]
                    dve.wait_ge(po_hi, n)
                    lo_part(slice(at0, at0 + r), (n - 1) % 2, po_lo)
            barrier(dve, 9)
            for m in range(KC):
                gated(m, U_PG, gst2, merged[:, m, :], pst2, 32, 64)
            barrier(dve, 10)
            for c in range(KC):
                dve.wait_ge(mg_hi, c + 1)
                dve.tensor_tensor(xt_lo[:, c, :], merged[:, c, :], xt_hi[:, c, :].bitcast(F32), ALU.subtract).then_inc(mg_lo, 1)

            dve.wait_ge(res_in, 32)
            for u in range(U_O, U_FF):
                for t in range(NT):
                    r = rows_of(t)
                    if t == NT - 1:
                        dve.wait_ge(unit_done, u + 1)
                    else:
                        dve.wait_ge(half_done, halves_before(u) + t + 1)
                    dst = res[:r, t, 256 * (u - U_O):256 * (u - U_O) + 256]
                    dve.scalar_tensor_tensor(dst, dst, ALPHA, ps[:r, t % 3, 0:256], ALU.mult, ALU.add).then_inc(evac, 1)
            dve.drain()

            def norm(first, ok0, write_xt):
                norm_stats(res[:, 0, :], P, 0, stats2, mv2, l_var)
                dve.wait_ge(ln2_in, first)
                for t in range(NT + 1):
                    if t + 1 < NT:
                        norm_stats(res[:, t + 1, :], rows_of(t + 1), t + 1, stats2, mv2, l_var)
                    if t < NT:
                        dve.wait_ge(l_std, ok0 + t + 1)
                        norm_apply(res[:, t, :], res[:, t, :], rows_of(t), t, mv2, lg2, lb2, None, l_ok)
                    if t and write_xt:
                        dve.wait_ge(l_hi, t)
                        lo_part(slice(P * (t - 1), P * (t - 1) + rows_of(t - 1)), (t - 1) % 2, l_lo)

            norm(32, 0, True)
            barrier(dve, 11)

            def square(c, relus):
                dve.wait_ge(f_relu, relus + c)
                dve.tensor_tensor(rl[:, c, :], rl[:, c, :], rl[:, c, :], ALU.mult).then_inc(f_sq, 1)

            def low(c, a, his):
                dve.wait_ge(f_hi, his + c)
                dve.tensor_tensor(a_lo[:, a, c, :], rl[:, c, :], a_hi[:, a, c, :].bitcast(F32), ALU.subtract).then_inc(f_lo, 1)

            def sums(m0, m1, halves, units, first=False):
                for m in range(m0, m1):
                    t, hf = m // 2, m % 2
                    r = rows_of(t)
                    if m == 2 * NT - 1:
                        dve.wait_ge(unit_done, units)
                    else:
                        dve.wait_ge(f_half, halves + m)
                    dst = res[:r, t, 512 * hf:512 * hf + 512]
                    if first:
                        dve.scalar_tensor_tensor(dst, dst, ALPHA, ps[:r, 6 + m % 2, :], ALU.mult, ALU.add).then_inc(f_add, 1)
                    else:
                        dve.tensor_tensor(dst, dst, ps[:r, 6 + m % 2, :], ALU.add).then_inc(f_add, 1)

            for j in range(2):
                for c in range(2):
                    square(c, 2 * j + 1)
                    low(c, j, 2 * j + 1)
            sums(0, 18, 1, U_FF + 3, True)
            with dve.Fori(0, (FB - 2) // 2) as i:
                for o in range(2):
                    n = 4 * i + (5 + 2 * o)
                    square(0, n)
                    low(0, o, n)
                    hv, uv = 34 * i + 17 * (o + 1) + 1, 4 * i + (U_FF + 5 + 2 * o)
                    square(1, n)
                    sums(0, 2, hv, uv)
                    low(1, o, n)
                    sums(2, 18, hv, uv)
            sums(0, 18, 17 * (FB - 1) + 1, N_UNITS)
            barrier(dve, 12)
            norm(64, NT, False)


def tr_before(hh):
    n = 0
    for i in range(NT):
        chunks = 1 + (i + 1 if i < 8 else 0)
        n += -(-chunks // 4) * max(0, min(NH, hh - NH * i))
    return n


def _units(inp):
    def f_unit(w, c0, c1):
        parts = [w[:, c:c + P].reshape(KC, P, P).transpose(1, 0, 2) for c in (c0, c1)]
        return np.concatenate(parts, axis=1).reshape(P, UNIT)

    def n_unit(w, c0):
        return w[:, c0:c0 + 256].reshape(KC, P, 256).transpose(1, 0, 2).reshape(P, UNIT)

    w, wa, wg, wo = inp["w_in"][0], inp["w_proj_attn"][0], inp["w_proj_gla"][0], inp["w_out"][0]
    up, down = inp["w_ff_up"][0], inp["w_ff_down"][0]
    us = [f_unit(w, C_K, C_K + P), f_unit(w, C_KI, C_A1)]
    us += [f_unit(w, C_QI + 256 * j, C_QI + 256 * j + P) for j in range(2)]
    us += [f_unit(w, C_Q + 256 * j, C_Q + 256 * j + P) for j in range(4)]
    us += [f_unit(w, c + 256 * j, c + 256 * j + P) for c in (C_GQ, C_GK) for j in range(2)]
    us += [n_unit(w, C_V)]
    us += [n_unit(w, c + 256 * j) for c in (C_GV, C_OG) for j in range(4)]
    us += [f_unit(w, C_GT + 256 * j, C_GT + 256 * j + P) for j in range(8)]
    us += [f_unit(m, 256 * j, 256 * j + P) for m in (wa, wg) for j in range(4)]
    us += [n_unit(wo, 256 * j) for j in range(4)]
    ups = [f_unit(up, 256 * j, 256 * j + P) for j in range(FB)]
    downs = [down[256 * j:256 * j + 256].reshape(2, P, D).transpose(1, 0, 2).reshape(P, UNIT) for j in range(FB)]
    us += [ups[0]]
    for j in range(1, FB):
        us += [ups[j], downs[j - 1]]
    return np.stack(us + [downs[FB - 1]])


def kernel(**inputs):
    import concourse.bacc as bacc
    from concourse.bass_utils import run_bass_kernel_spmd

    inp = {k: np.asarray(v) for k, v in inputs.items()}
    f = np.ascontiguousarray
    pool = inp["cache_k"].shape[1]
    arrays = {
        "x_all": f(np.concatenate([inp["x_prompt"][0], inp["meta_tokens"], inp["x_sample"].reshape(TS, D)])),
        "cache_k": f(inp["cache_k"][0].reshape(pool, PAGE, NKV * HD)),
        "cache_v": f(inp["cache_v"][0].reshape(pool, PAGE, NKV * HD)),
        "cache_kidx": f(inp["cache_kidx"][0]),
        "state": f(inp["state_gla"][0]),
        "page_table": f(inp["page_table"].reshape(1, DB * NPG)),
        "ln_p": f(np.stack([inp["ln_in_g"], inp["ln_in_b"], inp["ln1_g"][0], inp["ln1_b"][0],
                            inp["ln2_g"][0], inp["ln2_b"][0]])),
        "w_stream": f(_units(inp)),
        "w_a2": f(inp["w_gla_a2"][0]),
        "b_a": f(inp["b_gla_a"][0]),
        "gnorm": f(inp["gla_norm_g"]),
    }
    outs = [("y_p", (SEQ, D)), ("y_s", (TS, D)), ("k_p", (TP, 256)), ("v_p", (TP, 256)), ("ki_p", (TP, HD)),
            ("st_p", (GH, DK, DV)), ("k_s", (TS, 256)), ("v_s", (TS, 256)), ("ki_s", (TS, HD)),
            ("st_s", (DB, GH, DK, DV))]
    nc = bacc.Bacc("TRN2", target_bir_lowering=False, num_devices=1)
    ins = [nc.dram_tensor(n, a.shape, mybir.dt.from_np(a.dtype), kind="ExternalInput").ap() for n, a in arrays.items()]
    out_aps = [nc.dram_tensor(n, s, F32, kind="ExternalOutput").ap() for n, s in outs]
    build(nc, *ins, out_aps)
    r = run_bass_kernel_spmd(nc, [arrays], core_ids=[0]).results[0]
    return (r["y_p"].reshape(1, SEQ, D), r["y_s"].reshape(DB, DS, D),
            r["k_p"].reshape(1, 1, TP, NKV, HD), r["v_p"].reshape(1, 1, TP, NKV, HD), r["ki_p"].reshape(1, 1, TP, HD),
            r["st_p"].reshape(1, 1, GH, DK, DV), r["k_s"].reshape(1, DB, DS, NKV, HD),
            r["v_s"].reshape(1, DB, DS, NKV, HD), r["ki_s"].reshape(1, DB, DS, HD),
            r["st_s"].reshape(1, DB, GH, DK, DV))
```

```python
from contextlib import ExitStack

import numpy as np
import concourse.bass as bass
from concourse import mybir

F32 = mybir.dt.float32
F32R = mybir.dt.float32r
BF16 = mybir.dt.bfloat16
I32 = mybir.dt.int32
ALU = mybir.AluOpType
ACT = mybir.ActivationFunctionType
AX = mybir.AxisListType

P = 128
D = 1024
KC = D // P
SEQ, META, DB, DS = 1024, 16, 8, 8
TP = SEQ + META
TS = DB * DS
T = TP + TS
NT = -(-T // P)
N3 = T // 3
HD, NH, NKV, G = 64, 16, 4, 4
IH = 8
PAST, PAGE, NPG = 2048, 128, 16
NK = PAST + DS
TOPK = 256
GH, DK, DV, CH = 4, 128, 256, 64
RANK = 16
DFF = 4096
FB = DFF // 256
EPS = 1e-5
ALPHA = 2 ** 0.25
TAU = 16.0
NEG = -1e30
TAKEN = -3e38

UNIT = 2048
C_Q, C_K, C_V, C_QI, C_KI, C_GQ, C_GK, C_GV, C_OG, C_A1, C_GT = (
    0, 1024, 1280, 1536, 2048, 2120, 2632, 3144, 4168, 5192, 5208)
U_F1, U_Q, U_N, U_GATE, U_PA, U_PG, U_O, U_FF = 0, 4, 12, 21, 29, 33, 37, 41
N_UNITS = U_FF + 2 * FB


def is_natural(u):
    return U_N <= u < U_GATE or U_O <= u < U_FF


def is_filler(u):
    return U_N < u < U_PG


N_FILL = 8 * NT + 8 * 6


F_EARLY = 7 * NT


def fills_by(hh):
    return F_EARLY + (hh + 1) * (N_FILL - F_EARLY) // (NH * NT)


def fill_unit(f):
    if f < 8 * NT:
        return U_N + 1 + f // NT, f % NT, f % NT == NT - 1
    return U_GATE + (f - 8 * NT) // 6, (f - 8 * NT) % 6, (f - 8 * NT) % 6 == 5


def fill_count(f):
    return sum(not fill_unit(j)[2] for j in range(f + 1))


def fill_unit_start(u):
    return NT * (u - U_N - 1) if u <= U_GATE else 8 * NT + 6 * (u - U_GATE)


def batches_of(i):
    return -(-(1 + (i + 1 if i < 8 else 0)) // 4)


def batches_before(hh, parity):
    return sum((batches_of(h // NH) + 1 - parity) // 2 for h in range(hh))


def halves_before(u):
    return sum((NT - 1 if is_natural(v) else 1) * (not is_filler(v)) for v in range(min(u, U_FF))) + max(u - U_FF, 0)


def evacs_before(u):
    return sum((NT if is_natural(v) else 2) * (not is_filler(v)) for v in range(u))


def rows_of(t):
    return min(P, T - t * P)


def pieces(n):
    k = -(-n // 512)
    w = -(-n // k)
    return n, w + w % 2, k


def keys_of(i):
    return pieces(META if i == NT - 1 else META + P * (i + 1))


def mask_at(i):
    return sum(keys_of(j)[1] * keys_of(j)[2] for j in range(i))


def build(nc, x_all, cache_k, cache_v, cache_kidx, state, page_table, ln_p, w_stream, w_a2, b_a,
          gnorm, outs):
    (y_p, y_s, k_p, v_p, ki_p, st_p, k_s, v_s, ki_s, st_s) = outs
    top = ExitStack()
    with top:
        def alloc(stack, name, shape, dt=F32):
            return stack.enter_context(nc.sbuf_tensor(name, shape, dt))

        def sb(name, shape, dt=F32):
            return alloc(top, name, shape, dt)

        def region(*specs):
            with ExitStack() as st:
                return [alloc(st, *s) for s in specs]

        def sem(name):
            return top.enter_context(nc.semaphore(name))

        def dram(name, shape):
            return nc.dram_tensor(name, shape, F32).ap()

        h_d = dram("h_d", (T, D))
        qiT_d = dram("qiT_d", (IH * HD, T))
        qT_d = dram("qT_d", (2048, T))
        gvog_d = dram("gvog_d", (T, 2048))
        gate_d = dram("gate_d", (2048, T))
        part_d = dram("part_d", (D, T))
        o_d = dram("o_d", (T, D))
        a1_d = dram("a1_d", (RANK, T))
        wi_d = dram("wi_d", (IH, TS))
        vs_d = dram("vs_d", (TS, NKV * HD))
        att_d = dram("att_d", (TP, D))

        ps = top.enter_context(nc.psum_tensor("ps", [P, 8, 512], F32))
        flat = ps[:, :, :].rearrange("p b n -> p (b n)")

        ident = sb("ident", [P, P])
        identb = sb("identb", [P, P], BF16)
        raw = sb("raw", [P, 2, UNIT])
        w_hi = sb("w_hi", [P, 2, UNIT], F32R)
        w_lo = sb("w_lo", [P, 2, UNIT], F32R)
        xt_hi = sb("xt_hi", [P, KC, T], F32R)
        xt_lo = sb("xt_lo", [P, KC, T], F32R)
        small = sb("small", [P, 16])
        tri = sb("tri", [P, P])
        tri16 = sb("tri16", [P, META], BF16)
        causal = sb("causal", [P, CH])
        d8 = sb("d8", [TS, DB, DS])
        delta = sb("delta", [TS, DS])
        bsel = sb("bsel", [TS, DB])
        triS = sb("triS", [TS, DS])
        pt_sb = sb("pt_sb", [1, P], I32)
        m8 = sb("m8", [P, 8])
        mx = sb("mx", [P, 4])
        rsum = sb("rsum", [P, NH])
        ssq = sb("ssq", [P, 10, GH])
        pool_go = sb("pool_go", [P, 2])

        xin, hbuf, lg, lb, stats, mv = region(
            ("xin", [P, 2, D]), ("hbuf", [P, 2, D]), ("lg", [P, D]), ("lb", [P, D]),
            ("stats", [P, 2, 2, 6]), ("mv", [P, 2, 2]))
        with ExitStack() as att:
            kT3 = alloc(att, "kT3", [P, 4, T])
            winat = alloc(att, "winat", [P, NT, IH])
            IW = mask_at(8)
            with ExitStack() as b_st:
                stg = alloc(b_st, "stg", [P, 2, T])
                isc = alloc(b_st, "isc", [P, IW])
                iscS = alloc(b_st, "iscS", [TS, NK])
                kiS, qraw, qhi, qlo, relu = region(
                    ("kiS", [P, 1056], F32R), ("qraw", [P, 2, IH, P]), ("qhi", [P, IH, P], F32R),
                    ("qlo", [P, IH, P], F32R), ("relu", [P, 2, 1056]))
                kxraw, kxT, relu2, ib, qiS, wsel, wb = region(
                    ("kxraw", [P, 2, NPG, HD]), ("kxT", [HD, NK]), ("relu2", [HD, 2, 512]),
                    ("ib", [DS, NK]), ("qiS", [HD, DB, IH, DS]), ("wsel", [HD, DB]),
                    ("wb", [HD, DB, DS]))
                maskS = alloc(b_st, "maskS", [TS, NK], BF16)
                kt, pS, qblk, esel, oS, attT = region(
                    ("kt", [P, 2, 2, 512]), ("pS", [P, NK]),
                    ("qblk", [P, 2, DB, P]), ("esel", [TS, DB, NH, DS], BF16),
                    ("oS", [P, 2, HD]), ("attT", [P, KC, TS]))
                masks = alloc(b_st, "masks", [P, IW], BF16)
                vnat = alloc(b_st, "vnat", [P, NT, NKV * HD])
                eqb, cut, bit, cand, low_m, take, cnt, need = region(
                    ("eqb", [P, NK], BF16), ("cut", [P, 8], I32), ("bit", [P, 8], I32), ("cand", [P, 8], I32),
                    ("low_m", [P, 8], I32), ("take", [P, 8], I32), ("cnt", [P, 8]), ("need", [P, 8]))
                attn, qraw2 = region(("attn", [P, D]), ("qraw2", [P, 2, G, P]))
            kS, pP, ptb = region(
                ("kS", [P, NKV, 1056], F32R), ("pP", [P, 2, 1056]), ("ptb", [P, 3, 512]))
            with ExitStack() as c_st:
                alloc(c_st, "kS_place", [P, NKV * 1056 + 2 * 1056 + 1536])
                qh2, ql2 = region(("qh2", [P, G, P], F32R), ("ql2", [P, G, P], F32R))
            kpg, vpg, vnew, ptS = region(
                ("kpg", [P, 3, 4, 256]), ("vpg", [P, 4, 4, 256]), ("vnew", [DS, 2, 256]),
                ("ptS", [P, 2, 512]))
        gq, gk, kd, zz, bb, a1T, reset, gv, gvs, s0, sx, kem, qdm, at, ken, wa2, ba, dec, bd64, ostg, gst = region(
            ("gq", [P, T]), ("gk", [P, T]), ("kd", [P, T]), ("zz", [P, T]), ("bb", [P, T]),
            ("a1T", [RANK, T]), ("reset", [P, T], BF16), ("gv", [P, NT, DV]), ("gvs", [TS, DV]),
            ("s0", [P, DB, DV]), ("sx", [P, 4, DV]), ("kem", [TS, DB, DK]), ("qdm", [P, 576]),
            ("at", [P, 2, CH]), ("ken", [P, 2, DK]), ("wa2", [RANK, 512]), ("ba", [P, GH]),
            ("dec", [P, 25]), ("bd64", [TS, CH]), ("ostg", [P, 2, DV]), ("gst", [P, 2, T]))
        oin, ogin, gnb = region(("oin", [P, 2, D]), ("ogin", [P, 2, D]), ("gnb", [P, DV]))
        gst2, pst2, merged = region(("gst2", [P, 2, T]), ("pst2", [P, 2, T]), ("merged", [P, KC, T]))
        res = sb("res", [P, NT, D])
        lg2, lb2, stats2, mv2 = region(
            ("lg2", [P, D]), ("lb2", [P, D]), ("stats2", [P, 2, 2, 6]), ("mv2", [P, 2, 2]))
        a_hi, a_lo, rl = region(
            ("a_hi", [P, 2, 2, T], F32R), ("a_lo", [P, 2, 2, T], F32R), ("rl", [P, 2, T]))

        raw_in = [sem("raw_in0"), sem("raw_in1")]
        w_split = sem("w_split")
        half_done, unit_done = sem("half_done"), sem("unit_done")
        evac = sem("evac")
        stage = sem("stage")
        consts = sem("consts")
        ln_in = sem("ln_in")
        x_in = [sem("x_in0"), sem("x_in1")]
        x_free, var_ok, std_ok, h_ready = sem("x_free"), sem("var_ok"), sem("std_ok"), sem("h_ready")
        h_out = [sem("h_out0"), sem("h_out1")]
        tr_ok, hi_ok, lo_ok = sem("tr_ok"), sem("hi_ok"), sem("lo_ok")
        st_out = [sem("st_out0"), sem("st_out1")]
        fill_mm, fill_ev = sem("fill_mm"), sem("fill_ev")
        fst_out = [sem(f"fst_out{i}") for i in range(3)]
        att_out = [sem("att_out0"), sem("att_out1")]
        al_in = [sem("al_in0"), sem("al_in1")]
        g_sig = sem("g_sig")
        kn_tr, kn_ok = sem("kn_tr"), sem("kn_ok")
        kn_out = [sem("kn_out0"), sem("kn_out1")]
        ks_in, ks_hi, ks_ok, pads = sem("ks_in"), sem("ks_hi"), sem("ks_ok"), sem("pads")
        q_in = [sem("q_in0"), sem("q_in1")]
        q_hi_ok, q_lo_ok = sem("q_hi_ok"), sem("q_lo_ok")
        ix_mm, ix_relu, ix_acc = sem("ix_mm"), sem("ix_relu"), sem("ix_acc")
        sx_in, wb_ok = sem("sx_in"), sem("wb_ok")
        kx_in = [sem("kx_in0"), sem("kx_in1")]
        kx_tr, kx_ev, s_mm, s_relu, i_mm, i_ev, ib_out = (
            sem(n) for n in ("kx_tr", "kx_ev", "s_mm", "s_relu", "i_mm", "i_ev", "ib_out"))
        misc_out = sem("misc_out")
        c_ks_hi, c_ks_ok = sem("c_ks_hi"), sem("c_ks_ok")
        c_ks_in = [sem("c_ks_in0"), sem("c_ks_in1")]
        cq_in = [sem("cq_in0"), sem("cq_in1")]
        cq_hi, cq_lo = sem("cq_hi"), sem("cq_lo")
        qk_ok, mx_ok, exp_ok = sem("qk_ok"), sem("mx_ok"), sem("exp_ok")
        fill_at = kT3[:, 2, :].rearrange("p (s n) -> p s n", s=3)
        pt_tr, pt_a, pt_v, pv_ok, o_ev, att_tr = (
            sem(n) for n in ("pt_tr", "pt_a", "pt_v", "pv_ok", "o_ev", "att_tr"))
        d_set, d_cst = sem("d_set"), sem("d_cst")
        kg_in = [sem(f"kg_in{i}") for i in range(3)]
        vg_in = [sem(f"vg_in{i}") for i in range(4)]
        vn_in = [sem("vn_in0"), sem("vn_in1")]
        kt_tr, kt_a, kt_v, kt_qk = sem("kt_tr"), sem("kt_a"), sem("kt_v"), sem("kt_qk")
        d_qk, d_mx, d_exp, d_p, d_ptr, d_pa, d_pv, d_o, d_oev = (
            sem(n) for n in ("d_qk", "d_mx", "d_exp", "d_p", "d_ptr", "d_pa", "d_pv", "d_o", "d_oev"))
        d_oc, d_ot = sem("d_oc"), sem("d_ot")
        g_in = [sem("g_in0"), sem("g_in1")]
        s_done = sem("s_done")
        ga_set, ga_in, ga_z, ga_step, ga_e, ga_ready = (
            sem(n) for n in ("ga_set", "ga_in", "ga_z", "ga_step", "ga_e", "ga_ready"))
        ga_lg, ga_at, ga_am, ga_kn, ga_u, ga_s, ga_o, ga_oe, ga_head = (
            sem(n) for n in ("ga_lg", "ga_at", "ga_am", "ga_kn", "ga_u", "ga_s", "ga_o", "ga_oe", "ga_head"))
        ga_so, ga_q = sem("ga_so"), sem("ga_q")
        pa_mm, pa_ev, pa_out = sem("pa_mm"), sem("pa_ev"), sem("pa_out")
        ga_oo = [sem("ga_oo0"), sem("ga_oo1")]
        po_in = [sem("po_in0"), sem("po_in1")]
        po_set, po_v, po_sd, po_sl, po_ok, po_tr, po_hi, po_lo = (
            sem(n) for n in ("po_set", "po_v", "po_sd", "po_sl", "po_ok", "po_tr", "po_hi", "po_lo"))
        mg_hi, mg_lo, res_in = sem("mg_hi"), sem("mg_lo"), sem("res_in")
        l_var, l_std, l_ok, l_tr, l_hi, l_lo = (
            sem(n) for n in ("l_var", "l_std", "l_ok", "l_tr", "l_hi", "l_lo"))
        ln2_in = sem("ln2_in")
        f_relu, f_sq, f_hi, f_lo, f_half, f_add = (
            sem(n) for n in ("f_relu", "f_sq", "f_hi", "f_lo", "f_half", "f_add"))

        def barrier(eng, n):
            eng.drain().then_inc(stage, 1)
            eng.wait_ge(stage, 4 * n)

        OT = [(i, P * i, P) for i in range(8)] + [(8, SEQ, META), (9, TP, TS)]

        def load_pages(eng, dst, cache, b, grp, done):
            for j in range(4):
                at0 = NPG * b + 4 * grp + j
                page = eng.value_load(pt_sb[0:1, at0:at0 + 1], min_val=0, max_val=159)
                eng.dma_start(dst[:, j, :], cache[bass.ds(page, 1), :, :].rearrange(
                    "a p d -> (a p) d")).then_inc(done, 16)

        block = top.enter_context(nc.Block())

        @block.gpsimd
        def _(pool):
            for tile, v in ((ident[:, :], 0.0), (identb[:, :], 0.0), (tri[:, :], 0.0), (tri16[:, :], 0.0),
                            (causal[:, :], 1.0), (d8[:, :, :], 0.0), (pool_go[:, :], 0.0)):
                pool.memset(tile, v)
            pool.drain()
            selects = [
                (ident[:, :], ALU.not_equal, 1.0, [[-1, P]], 1),
                (identb[:, :], ALU.not_equal, 1.0, [[-1, P]], 1),
                (tri[:, :], ALU.is_ge, NEG, [[-1, P]], 1),
                (tri16[:, :], ALU.is_ge, NEG, [[-1, META]], 1),
                (causal[0:CH, :], ALU.is_ge, 0.0, [[1, CH]], -1),
                (causal[CH:P, :], ALU.is_ge, 0.0, [[1, CH]], -1),
                (d8[:, :, :], ALU.not_equal, 1.0, [[-DS, DB], [-1, DS]], 1)]
            for n, (tile, compare, fill, pattern, mult) in enumerate(selects):
                if n:
                    pool.wait_ge(consts, n)
                pool.affine_select(out=tile, in_=tile, compare_op=compare, fill=fill, base=0,
                                   pattern=pattern, channel_multiplier=mult).then_inc(consts, 1)
            pool.wait_ge(consts, 7)

            def split(s, landed, used):
                pool.wait_ge(raw_in[s], landed)
                if used is not None:
                    pool.wait_ge(unit_done, used)
                pool.tensor_tensor(pool_go[:, 0:1], pool_go[:, 1:2], pool_go[:, 1:2], ALU.mult)
                pool.tensor_copy(w_hi[:, s, :], raw[:, s, :])
                pool.drain()
                pool.tensor_tensor(w_lo[:, s, :], raw[:, s, :], w_hi[:, s, :].bitcast(F32),
                                   ALU.subtract).then_inc(w_split, 1)

            split(0, 16, None)
            split(1, 16, None)
            with pool.Fori(1, N_UNITS // 2) as i:
                for s in range(2):
                    split(s, 16 * i + 16, 2 * i + s - 1)
            split(0, 16 * (N_UNITS // 2) + 16, N_UNITS - 2)

        @block.sync
        def _(sp):
            def load_unit(u, s, landed_before=None):
                if landed_before is not None:
                    sp.wait_ge(w_split, landed_before)
                src = w_stream[u, :, :] if isinstance(u, int) else \
                    w_stream[bass.ds(u, 1), :, :].rearrange("u p n -> (u p) n")
                sp.dma_start(raw[:, s, :], src).then_inc(raw_in[s], 16)

            def load_units(u0, u1):
                for u in range(u0, u1):
                    load_unit(u, u % 2, u - 1 if u >= 2 else None)

            sp.dma_start(xin[:, 0, :], x_all[0:P, :]).then_inc(x_in[0], 16)
            sp.dma_start(xin[:, 1, :], x_all[P:2 * P, :]).then_inc(x_in[1], 16)
            sp.dma_start(lg[:, :], ln_p[0:1, :].broadcast_to((P, D))).then_inc(ln_in, 16)
            sp.dma_start(lb[:, :], ln_p[1:2, :].broadcast_to((P, D))).then_inc(ln_in, 16)
            sp.dma_start(pt_sb[:, :], page_table).then_inc(ln_in, 16)
            load_units(0, 2)
            for t in range(NT):
                r = rows_of(t)
                sp.wait_ge(h_ready, t + 1)
                sp.dma_start(h_d[P * t:P * t + r, :], hbuf[:r, t % 2, :]).then_inc(h_out[t % 2], 16)
                if t + 2 < NT:
                    sp.wait_ge(x_free, t + 1)
                    r = rows_of(t + 2)
                    sp.dma_start(xin[:r, t % 2, :], x_all[P * (t + 2):P * (t + 2) + r, :]).then_inc(x_in[t % 2], 16)
            sp.wait_ge(h_out[0], 16 * 5)
            sp.wait_ge(h_out[1], 16 * 4)
            sp.wait_ge(ln_in, 48)
            load_units(2, 4)
            barrier(sp, 1)

            sp.wait_ge(evac, 4)
            sp.dma_start(a1_d, kT3[:RANK, 3, :]).then_inc(misc_out, 16)
            sp.dma_start(wi_d, kT3[HD:HD + IH, 2, TP:T]).then_inc(misc_out, 16)
            for t in range(NT):
                sp.wait_ge(kn_ok, t + 1)
                src, s = relu[:, t % 2, 0:384], kn_out[t % 2]
                if t < 8:
                    at0 = META + P * t
                    sp.dma_start(k_p[at0:at0 + P, :], src[:, 0:256]).then_inc(s, 16)
                    sp.dma_start(ki_p[at0:at0 + P, :], src[:, 256:320]).then_inc(s, 16)
                else:
                    sp.dma_start(k_p[0:META, :], src[0:META, 0:256]).then_inc(s, 16)
                    sp.dma_start(ki_p[0:META, :], src[0:META, 256:320]).then_inc(s, 16)
                    sp.dma_start(k_s, src[META:80, 0:256]).then_inc(s, 16)
                    sp.dma_start(ki_s, src[META:80, 256:320]).then_inc(s, 16)
            sp.wait_ge(kn_out[0], 32 * 4 + 64)
            sp.wait_ge(kn_out[1], 32 * 4)

            def dup_keys(dst, src_rows, done):
                for half in range(2):
                    d = dst[HD * half:HD * half + HD, :]
                    sp.dma_start(d[:, 0:META], src_rows[:, SEQ:TP]).then_inc(done, 16)
                    sp.dma_start(d[:, META:TP], src_rows[:, 0:SEQ]).then_inc(done, 16)

            dup_keys(relu[:, 1, :], kT3[0:HD, 2, :], ks_in)

            sp.wait_ge(st_out[0], 32)
            sp.wait_ge(st_out[1], 32)
            qi_v = qiT_d.rearrange("(h d) t -> d h t", d=HD)
            for i in range(1, 8):
                if i >= 3:
                    sp.wait_ge(q_lo_ok, i - 2)
                for half in range(2):
                    sp.dma_start(qraw[HD * half:HD * half + HD, i % 2, :, :],
                                 qi_v[:, :, P * i:P * i + P]).then_inc(q_in[i % 2], 16)
            load_units(4, 6)
            barrier(sp, 2)

            sp.wait_ge(misc_out, 32)
            for h in range(IH):
                sp.dma_start(qiS[:, :, h, :], qiT_d[HD * h:HD * h + HD, TP:T].rearrange(
                    "d (b t) -> d b t", t=DS)).then_inc(sx_in, 16)
                sp.dma_start(wsel[DS * h:DS * h + DS, :], wi_d[h, :].rearrange(
                    "(b t) -> t b", t=DS), allow_slow_non_contiguous=True).then_inc(sx_in, 16)
            for b in range(DB):
                if b >= 2:
                    sp.wait_ge(kx_tr, 4 * (b - 1))
                for pg in range(NPG):
                    page = sp.value_load(pt_sb[0:1, NPG * b + pg:NPG * b + pg + 1], min_val=0, max_val=159)
                    sp.dma_start(kxraw[:, b % 2, pg, :], cache_kidx[bass.ds(page, 1), :, :].rearrange(
                        "a p d -> (a p) d")).then_inc(kx_in[b % 2], 16)
                if b >= 1:
                    sp.wait_ge(i_ev, 5 * b)
                    sp.dma_start(iscS[DS * (b - 1):DS * b, :], ib[:, :]).then_inc(ib_out, 16)
            sp.wait_ge(i_ev, 5 * DB)
            sp.dma_start(iscS[DS * (DB - 1):DS * DB, :], ib[:, :]).then_inc(ib_out, 16)
            barrier(sp, 3)

            load_units(6, 12)
            load_units(12, 17)
            sp.wait_ge(evac, evacs_before(U_N + 1))
            sp.dma_start(v_p[META:TP, :].rearrange("(t p) c -> p t c", p=P), vnat[:, 0:8, :]).then_inc(misc_out, 16)
            sp.dma_start(v_p[0:META, :], vnat[0:META, 8, :]).then_inc(misc_out, 16)
            sp.dma_start(v_s, vnat[META:80, 8, :]).then_inc(misc_out, 16)
            sp.dma_start(vs_d, vnat[META:80, 8, :]).then_inc(misc_out, 16)
            load_units(17, U_N + 5 + F_EARLY // NT)
            barrier(sp, 4)

            for n in range(NKV):
                if n >= 2:
                    sp.wait_ge(c_ks_ok, n - 1)
                dup_keys(pP[:, n % 2, :], kT3[HD * (n % 2):HD * (n % 2) + HD, n // 2, :], c_ks_in[n % 2])
            q_v = qT_d[0:1024, :].rearrange("(h d) t -> d h t", d=HD)
            u = U_N + 5 + F_EARLY // NT

            def store_half(hh):
                i, half = hh // NH, hh % NH // 8
                r = P if i < 8 else META
                at0 = P * i
                sp.wait_ge(o_ev, hh + 1)
                sp.dma_start(att_d[at0:at0 + r, 512 * half:512 * half + 512],
                             attn[:r, 512 * half:512 * half + 512]).then_inc(att_out[half], 16)

            for i in range(NT):
                r = rows_of(i)
                for n in range(NKV):
                    j = NKV * i + n
                    if j >= 2:
                        sp.wait_ge(cq_lo, j - 1)
                    for half in range(2):
                        sp.dma_start(qraw2[HD * half:HD * half + HD, j % 2, :, :r],
                                     q_v[:, G * n:G * n + G, P * i:P * i + r]).then_inc(cq_in[j % 2], 16)
                    if j >= 3 and j % 2:
                        store_half(4 * (j - 1) - 1)
                    while u < U_PA + 4 and fill_unit_start(u - 3) < fills_by(4 * (j - 1)):
                        load_unit(u, u % 2, u - 1)
                        u += 1
            store_half(NH * NT - 1)
            load_units(u, U_PA + 4)
            for half in range(2):
                sp.wait_ge(att_out[half], 16 * NT)
            barrier(sp, 5)

            def load_att(i):
                r = P if i < 8 else META
                sp.dma_start(kT3[:r, 2 + i % 2, 0:D], att_d[P * i:P * i + r, :]).then_inc(al_in[i % 2], 16)

            def load_k(gg):
                if gg >= 3:
                    sp.wait_ge(kt_tr, gg - 2)
                load_pages(sp, kpg[:, gg % 3, :, :], cache_k, gg // 4, gg % 4, kg_in[gg % 3])

            for gg in range(3):
                load_k(gg)
            sp.wait_ge(d_set, 1)
            sp.wait_ge(misc_out, 16 * 6)
            for j in range(2):
                for n2 in range(2):
                    for g in range(G):
                        head = G * (2 * j + n2) + g
                        sp.dma_start(
                            qblk[HD * n2:HD * n2 + HD, j, :, DS * head:DS * head + DS],
                            qT_d[HD * head:HD * head + HD, TP:T].rearrange("d (b t) -> d b t", t=DS)
                        ).then_inc(d_cst, 16)
            load_att(0)
            load_att(1)
            for b in range(DB):
                load_k(4 * b + 3)
                if b >= 1 and b + 1 < NT:
                    sp.wait_ge(att_tr, b)
                    load_att(b + 1)
                if b + 1 < DB:
                    load_k(4 * b + 4)
                if b >= 2:
                    sp.wait_ge(d_o, b - 1)
                sp.dma_start(vnew[:, b % 2, :], vs_d[DS * b:DS * b + DS, :]).then_inc(vn_in[b % 2], 16)
                for grp in range(2, 4):
                    if b >= 1:
                        sp.wait_ge(s_done, 4 * (b - 1) + grp + 1)
                    load_pages(sp, vpg[:, grp, :, :], cache_v, b, grp, vg_in[grp])
                if b + 1 < DB:
                    load_k(4 * b + 5)
                    load_k(4 * b + 6)
            barrier(sp, 6)

            def load_gates(dst, first, src2=None, dst2=None, base=0):
                for m in range(KC):
                    if m >= 2:
                        sp.wait_ge(evac, evacs_before(base) + m - 1)
                    sp.dma_start(dst[:, m % 2, :], gate_d[first + P * m:first + P * m + P, :]).then_inc(g_in[m % 2], 16)
                    if src2 is not None:
                        sp.dma_start(dst2[:, m % 2, :], src2[P * m:P * m + P, :]).then_inc(g_in[m % 2], 16)
                    if m % 2 == 1:
                        load_units(base + 4 + m // 2, base + 5 + m // 2)

            def load_head_gates(h):
                for c in range(2):
                    at0 = P * (2 * h + c)
                    sp.dma_start(gst[:, c, :], gate_d[at0:at0 + P, :]).then_inc(g_in[c], 16)

            load_head_gates(0)
            sp.dma_start(a1T[:, :], a1_d).then_inc(ga_set, 16)
            sp.dma_start(wa2[:, :], w_a2).then_inc(ga_set, 16)
            sp.dma_start(ba[:, :], b_a.rearrange("(h p) -> p h", p=P), allow_slow_non_contiguous=True).then_inc(ga_set, 16)
            for h in range(GH):
                if h:
                    sp.wait_ge(ga_head, h)
                    sp.wait_ge(ga_so, 32 * h)
                sp.dma_start(gq[:, :], qT_d[1024 + DK * h:1024 + DK * h + DK, :]).then_inc(ga_in, 16)
                sp.dma_start(gk[:, :], qT_d[1536 + DK * h:1536 + DK * h + DK, :]).then_inc(ga_in, 16)
                cols = gvog_d[:, DV * h:DV * h + DV]
                sp.dma_start(gv[:, 0:8, :], cols[0:SEQ, :].rearrange("(t p) c -> p t c", p=P)).then_inc(ga_in, 16)
                sp.dma_start(gv[0:META, 8, :], cols[SEQ:TP, :]).then_inc(ga_in, 16)
                sp.dma_start(gvs[:, :], cols[TP:T, :]).then_inc(ga_in, 16)
                sp.dma_start(s0[:, :, :], state[:, h, :, :].rearrange("b p v -> p b v")).then_inc(ga_in, 16)
                for n, (i, at0, r) in enumerate([OT[8]] + OT[:8] + [OT[9]]):
                    e = 10 * h + n
                    sp.wait_ge(ga_oe, e + 1)
                    sp.dma_start(o_d[at0:at0 + r, DV * h:DV * h + DV], ostg[:r, e % 2, :]).then_inc(ga_oo[e % 2], 16)
                    if n == 0:
                        sp.wait_ge(pa_ev, 6 * (h + 1))
                        for c in range(2):
                            at0 = P * (2 * h + c)
                            sp.dma_start(part_d[at0:at0 + P, :], gst[:, c, :]).then_inc(pa_out, 16)
                        load_unit(U_PG + h, (U_PG + h) % 2, U_PG + h - 1)
                    if n == 3 and h + 1 < GH:
                        sp.wait_ge(pa_out, 32 * (h + 1))
                        load_head_gates(h + 1)
                sp.wait_ge(ga_s, 26 * (h + 1))
                sp.dma_start(st_p[h, :, :], sx[:, 0, :]).then_inc(ga_so, 16)
                sp.dma_start(st_s[:, h, :, :].rearrange("b p v -> p b v"), s0[:, :, :]).then_inc(ga_so, 16)
            sp.wait_ge(ga_so, 32 * GH)
            sp.wait_ge(pa_out, 32 * GH)
            sp.wait_ge(ga_oo[0], 16 * 20)
            sp.wait_ge(ga_oo[1], 16 * 20)
            barrier(sp, 7)

            sp.dma_start(gnb[:, :], gnorm.broadcast_to((P, DV))).then_inc(po_set, 16)
            for n, (i, at0, r) in enumerate(OT):
                if n >= 2:
                    sp.wait_ge(po_tr, n - 1)
                sp.dma_start(oin[:r, n % 2, :], o_d[at0:at0 + r, :]).then_inc(po_in[n % 2], 16)
                sp.dma_start(ogin[:r, n % 2, :], gvog_d[at0:at0 + r, 1024:2048]).then_inc(po_in[n % 2], 16)
            barrier(sp, 8)
            load_gates(gst2, 1024, part_d, pst2, base=U_PG)
            barrier(sp, 9)

            sp.wait_ge(mg_lo, KC)
            sp.dma_start(res[:, 0:8, :], h_d[0:SEQ, :].rearrange("(t p) c -> p t c", p=P)).then_inc(res_in, 16)
            sp.dma_start(res[0:80, 8, :], h_d[SEQ:T, :]).then_inc(res_in, 16)
            sp.dma_start(lg2[:, :], ln_p[2:3, :].broadcast_to((P, D))).then_inc(ln2_in, 16)
            sp.dma_start(lb2[:, :], ln_p[3:4, :].broadcast_to((P, D))).then_inc(ln2_in, 16)
            load_units(41, 45)
            barrier(sp, 10)
            with sp.Fori(0, (N_UNITS - 45) // 2) as i:
                for s in range(2):
                    load_unit(2 * i + 45 + s, 1 - s, 2 * i + 44 + s)
            barrier(sp, 11)
            sp.dma_start(lg2[:, :], ln_p[4:5, :].broadcast_to((P, D))).then_inc(ln2_in, 16)
            sp.dma_start(lb2[:, :], ln_p[5:6, :].broadcast_to((P, D))).then_inc(ln2_in, 16)
            for t in range(NT):
                sp.wait_ge(l_ok, NT + t + 1)
                if t < 8:
                    sp.dma_start(y_p[P * t:P * t + P, :], res[:, t, :]).then_inc(misc_out, 16)
                else:
                    sp.dma_start(y_s, res[META:80, t, :]).then_inc(misc_out, 16)
            sp.wait_ge(misc_out, 16 * (6 + 9))

        @block.tensor
        def _(pe):
            def unit_f(s, ready, free):
                pe.wait_ge(w_split, ready)
                for c in range(2):
                    if free[c] is not None:
                        pe.wait_ge(evac, free[c])
                    for n in range(3):
                        out = ps[:, 3 * c + n, 0:N3]
                        cols = slice(N3 * n, N3 * n + N3)
                        for k in range(KC):
                            at0 = (KC * c + k) * P
                            hi, lo = w_hi[:, s, at0:at0 + P], w_lo[:, s, at0:at0 + P]
                            pe.matmul(out, hi, xt_hi[:, k, cols], start=k == 0, stop=False)
                            pe.matmul(out, hi, xt_lo[:, k, cols], start=False, stop=False)
                            last = pe.matmul(out, lo, xt_hi[:, k, cols], start=False, stop=k == KC - 1)
                    last.then_inc(unit_done if c else half_done, 1)

            def unit_n(s, ready, free, wait=None):
                pe.wait_ge(w_split, ready)
                for t in range(NT):
                    pe.wait_ge(evac, free + t)
                    r = rows_of(t)
                    out = ps[:r, t % 3, 0:256]
                    cols = slice(P * t, P * t + r)
                    for k in range(KC):
                        w = slice(256 * k, 256 * k + 256)
                        pe.matmul(out, xt_hi[:, k, cols], w_hi[:, s, w], start=k == 0, stop=False)
                        pe.matmul(out, xt_lo[:, k, cols], w_hi[:, s, w], start=False, stop=False)
                        last = pe.matmul(out, xt_hi[:, k, cols], w_lo[:, s, w], start=False, stop=k == KC - 1)
                    last.then_inc(unit_done if t == NT - 1 else half_done, 1)

            def transpose_tile(src, r, bank, done):
                for k in range(KC):
                    last = pe.transpose(flat[:, 512 * bank + P * k:512 * bank + P * k + r],
                                        src[:r, P * k:P * k + P], ident[:r, :r])
                last.then_inc(done, 1)

            pe.wait_ge(consts, 7)
            for t in range(NT):
                pe.wait_ge(h_ready, t + 1)
                if t >= 2:
                    pe.wait_ge(lo_ok, t - 1)
                transpose_tile(hbuf[:, t % 2, :], rows_of(t), 2 * (t % 2), tr_ok)
            pe.wait_ge(lo_ok, NT)
            barrier(pe, 1)

            for u in range(4):
                unit_f(u % 2, u + 1, [2 * u + c - 1 if 2 * u + c >= 2 else None for c in range(2)])
            for t in range(NT):
                r = rows_of(t)
                if t >= 2:
                    pe.wait_ge(kn_ok, t - 1)
                for c in range(3):
                    last = pe.transpose(ps[:r, 6 + t % 2, P * c:P * c + P], kT3[:, c, P * t:P * t + r], ident[:, :])
                last.then_inc(kn_tr, 1)

            pe.wait_ge(ks_ok, 1)
            pe.wait_ge(kn_ok, NT)
            pe.wait_ge(evac, 8)
            for i in range(1, 8):
                _, w, np_ = keys_of(i)
                pe.wait_ge(q_lo_ok, i)
                for h in range(IH):
                    g = IH * (i - 1) + h
                    if g >= 2:
                        pe.wait_ge(ix_relu, g - 1)
                    for p in range(np_):
                        out, keys = ps[:, 4 * (g % 2) + p, 0:w], kiS[:, w * p:w * p + w]
                        pe.matmul(out, qhi[:, h, :], keys, start=True, stop=False)
                        last = pe.matmul(out, qlo[:, h, :], keys, start=False, stop=True)
                    last.then_inc(ix_mm, 1)
            barrier(pe, 2)

            pe.wait_ge(sx_in, 16 * 16)
            pe.wait_ge(wb_ok, 1)
            width = [512] * 4 + [DS]
            for b in range(DB):
                def tr(grp):
                    gg = 4 * b + grp
                    if gg >= 2:
                        pe.wait_ge(kx_ev, 5 * ((gg - 2) // 4) + 2 + (gg - 2) % 4)
                    for j in range(4):
                        last = pe.transpose(ps[0:HD, gg % 2, P * j:P * j + P], kxraw[:, b % 2, 4 * grp + j, :], ident[:, :])
                    last.then_inc(kx_tr, 1)

                def sc(p):
                    q = 5 * b + p
                    pe.wait_ge(kx_ev, 5 * b + min(2 + p, 5))
                    if q >= 2:
                        pe.wait_ge(s_relu, q - 1)
                    pe.matmul(ps[0:HD, 2 + q % 2, 0:width[p]], qiS[:, b, :, :].rearrange("p h t -> p (h t)"),
                              kxT[:, 512 * p:512 * p + width[p]], start=True, stop=True).then_inc(s_mm, 1)

                def ws(p):
                    q = 5 * b + p
                    pe.wait_ge(s_relu, q + 1)
                    if q >= 2:
                        pe.wait_ge(i_ev, q - 1)
                    pe.matmul(ps[0:DS, 4 + q % 2, 0:width[p]], wb[:, b, :], relu2[:, q % 2, 0:width[p]],
                              start=True, stop=True).then_inc(i_mm, 1)

                pe.wait_ge(kx_in[b % 2], 256 * (b // 2 + 1))
                tr(0); tr(1); sc(0); tr(2); sc(1); ws(0); tr(3)
                sc(2); ws(1); sc(3); ws(2); sc(4); ws(3); ws(4)
            barrier(pe, 3)

            with pe.Fori(0, 4) as i:
                for s in range(2):
                    e0 = evacs_before(U_Q) + 2 * s
                    unit_f(s, 2 * i + (U_Q + s + 1), [4 * i + (e0 + c - 1) for c in range(2)])
            pe.wait_ge(evac, evacs_before(U_N))
            unit_n(0, U_N + 1, evacs_before(U_N) - 2)
            pe.wait_ge(evac, evacs_before(U_N + 1))

            def fill(f):
                u, m, last_one = fill_unit(f)
                s = u % 2
                if m == 0:
                    pe.wait_ge(w_split, u + 1)
                ahead = f < F_EARLY
                bank = 6 + f % 2 if ahead else 7
                if f - ahead > 0:
                    pe.wait_ge(fill_ev, f - ahead)
                if f < 8 * NT:
                    r = rows_of(m)
                    out, cols = ps[:r, bank, 0:256], slice(P * m, P * m + r)
                    for k in range(KC):
                        w = slice(256 * k, 256 * k + 256)
                        pe.matmul(out, xt_hi[:, k, cols], w_hi[:, s, w], start=k == 0, stop=False)
                        pe.matmul(out, xt_lo[:, k, cols], w_hi[:, s, w], start=False, stop=False)
                        last = pe.matmul(out, xt_hi[:, k, cols], w_lo[:, s, w], start=False, stop=k == KC - 1)
                else:
                    out, cols = ps[:, bank, 0:N3], slice(N3 * (m % 3), N3 * (m % 3) + N3)
                    for k in range(KC):
                        at0 = (KC * (m // 3) + k) * P
                        hi, lo = w_hi[:, s, at0:at0 + P], w_lo[:, s, at0:at0 + P]
                        pe.matmul(out, hi, xt_hi[:, k, cols], start=k == 0, stop=False)
                        pe.matmul(out, hi, xt_lo[:, k, cols], start=False, stop=False)
                        last = pe.matmul(out, lo, xt_hi[:, k, cols], start=False, stop=k == KC - 1)
                last.then_inc(unit_done if last_one else fill_mm, 1)

            for f in range(F_EARLY):
                fill(f)
            barrier(pe, 4)

            def qk(hh):
                i, n, g = hh // NH, hh % NH // G, hh % G
                r = rows_of(i)
                L, w, np_ = keys_of(i)
                if g == 0:
                    pe.wait_ge(cq_lo, hh // G + 1)
                free = hh if i == 7 or (i == 8 and hh % NH < 2) else hh - 1
                if free > 0:
                    pe.wait_ge(mx_ok, free)
                bank = 0 if np_ == 3 else 2 * (hh % 2)
                for p in range(np_):
                    out, keys = ps[:r, bank + p, 0:w], kS[:, n, w * p:w * p + w]
                    pe.matmul(out, qh2[:, g, :r], keys, start=True, stop=False)
                    last = pe.matmul(out, ql2[:, g, :r], keys, start=False, stop=True)
                last.then_inc(qk_ok, 1)

            def chunks_of(i):
                return [(0, META)] + ([(META + P * j, P) for j in range(i + 1)] if i < 8 else [])

            def tr(hh, j):
                i = hh // NH
                r = rows_of(i)
                if j == 0:
                    pe.wait_ge(exp_ok, hh + 1)
                if j == 2:
                    pe.wait_ge(pt_v, batches_before(hh, 0) + 1)
                for m, (at0, wid) in enumerate(chunks_of(i)[4 * j:4 * j + 4]):
                    last = pe.transpose(ps[:wid, 4 + j % 2, P * m:P * m + r], pP[:r, hh % 2, at0:at0 + wid], ident[:r, :r])
                last.then_inc(pt_tr, 1)

            def av(hh, j):
                i, n = hh // NH, hh % NH // G
                r = rows_of(i)
                chunks = chunks_of(i)
                pe.wait_ge(pt_a if j == 1 else pt_v, batches_before(hh, j % 2) + (2 if j == 2 else 1))
                if j == 0 and hh:
                    pe.wait_ge(o_ev, hh)
                for m, (at0, wid) in enumerate(chunks[4 * j:4 * j + 4]):
                    vt = 8 if at0 == 0 else (at0 - META) // P
                    last = pe.matmul(ps[:r, 6, 0:HD], ptb[:wid, j, P * m:P * m + r],
                                     vnat[:wid, vt, HD * n:HD * n + HD],
                                     start=at0 == 0, stop=at0 == chunks[-1][0])
                last.then_inc(pv_ok, 1)

            pe.wait_ge(c_ks_ok, NKV)
            f = F_EARLY
            qk(0)
            qk(1)
            for hh in range(NH * NT):
                nb = batches_of(hh // NH)
                for j in range(min(nb, 2)):
                    tr(hh, j)
                if hh + 2 < NH * NT:
                    qk(hh + 2)
                if f < fills_by(hh):
                    fill(f)
                    f += 1
                if nb == 3:
                    tr(hh, 2)
                for j in range(nb):
                    av(hh, j)
            barrier(pe, 5)

            def att_tile(i):
                pe.wait_ge(al_in[i % 2], 16 * (i // 2 + 1))
                transpose_tile(kT3[:, 2 + i % 2, 0:D], P if i < 8 else META, 5, att_tr)

            def ktr(gg):
                pe.wait_ge(kg_in[gg % 3], 64 * (gg // 3 + 1))
                if gg:
                    pe.wait_ge(kt_a, gg)
                    pe.wait_ge(kt_v, gg)
                for j in range(2):
                    for m in range(4):
                        last = pe.transpose(ps[:, 5 + j, P * m:P * m + P], kpg[:, gg % 3, m, P * j:P * j + P], ident[:, :])
                last.then_inc(kt_tr, 1)

            def o_transposed(b):
                pe.wait_ge(d_oc, b + 1)
                pe.transpose(ps[:, 4, 256:256 + P], oS[:, :, :].rearrange("p a d -> p (a d)"), ident[:, :]).then_inc(d_ot, 1)

            ktr(0)
            ktr(1)
            pe.wait_ge(d_cst, 16 * 16)
            pe.wait_ge(d_set, 2)
            for b in range(DB):
                def scores(p, keys, wid):
                    out = ps[:, p, 0:wid]
                    for j in range(2):
                        pe.matmul(out, qblk[:, j, b, :], keys(j), start=j == 0, stop=False)
                    return pe.matmul(out, esel[:, b, :, :].rearrange("p h t -> p (h t)"),
                                     maskS[:, 512 * p:512 * p + wid], start=False, stop=True)

                if b:
                    pe.wait_ge(d_exp, b)
                for grp in range(4):
                    gg = 4 * b + grp
                    pe.wait_ge(kt_a, gg + 1)
                    pe.wait_ge(kt_v, gg + 1)
                    scores(grp, lambda j: kt[:, gg % 2, j, :], 512).then_inc(kt_qk, 1)
                    if grp == 0 and b:
                        o_transposed(b - 1)
                        pe.wait_ge(d_pa, 2 * b)
                        pe.wait_ge(d_pv, 3 * b)
                    if grp < 2:
                        ktr(gg + 2)
                if b:
                    pe.wait_ge(d_oev, b)
                scores(4, lambda j: kT3[:, j, TP + DS * b:TP + DS * b + DS], DS).then_inc(d_qk, 1)
                att_tile(b)
                pe.wait_ge(lo_ok, NT + b + 1)
                if b + 1 < DB:
                    ktr(4 * b + 4)
                    ktr(4 * b + 5)
                    pe.wait_ge(kt_a, 4 * b + 6)
                    pe.wait_ge(kt_v, 4 * b + 6)
                pe.wait_ge(d_p, b + 1)
                pe.wait_ge(vn_in[b % 2], 16 * (b // 2 + 1))

                def ptr(j):
                    if j >= 2:
                        pe.wait_ge(d_pa if j % 2 else d_pv, 2 * b + (j - 2) // 2 + 1 if j % 2 else 3 * b + (j - 2) // 2 + 1)
                    if j < 4:
                        for m in range(4):
                            last = pe.transpose(ps[:, 5 + j % 2, P * m:P * m + P],
                                                pS[:, 512 * j + P * m:512 * j + P * m + P], ident[:, :])
                    else:
                        last = pe.transpose(ps[:DS, 5 + j % 2, 0:P], pS[:, PAST:NK], ident[:, :])
                    last.then_inc(d_ptr, 1)

                def av(j):
                    pe.wait_ge(d_pa if j % 2 else d_pv, 2 * b + j // 2 + 1 if j % 2 else 3 * b + j // 2 + 1)
                    if j < 4:
                        pe.wait_ge(vg_in[j], 64 * (b + 1))
                    wid = P if j < 4 else DS
                    for m in range(4 if j < 4 else 1):
                        last = pe.matmul(ps[:, 7, 0:NKV * HD], ptS[:wid, j % 2, P * m:P * m + P],
                                         vpg[:, j, m, :] if j < 4 else vnew[:, b % 2, :],
                                         start=j == 0 and m == 0, stop=j == 4)
                    last.then_inc(d_o if j == 4 else s_done, 1)

                ptr(0)
                for j in range(5):
                    if j < 4:
                        ptr(j + 1)
                    av(j)
            o_transposed(DB - 1)
            pe.wait_ge(d_pv, 3 * DB)
            pe.wait_ge(d_pa, 2 * DB)
            att_tile(8)
            barrier(pe, 6)

            pe.wait_ge(ga_set, 48)
            for h in range(GH):
                if h:
                    pe.wait_ge(ga_head, h)
                for n in range(3):
                    last = pe.matmul(ps[:, n, 0:N3], wa2[:, DK * h:DK * h + DK], a1T[:, N3 * n:N3 * n + N3],
                                     start=True, stop=True)
                last.then_inc(ga_lg, 1)
                s = (U_PA + h) % 2
                pe.wait_ge(w_split, U_PA + h + 1)
                for q in range(6):
                    if 6 * h + q >= 2:
                        pe.wait_ge(pa_ev, 6 * h + q - 1)
                    out, cols = ps[:, 5 + 2 * (q % 2), 0:N3], slice(N3 * (q % 3), N3 * (q % 3) + N3)
                    for k in range(KC):
                        at0 = (KC * (q // 3) + k) * P
                        hi, lo = w_hi[:, s, at0:at0 + P], w_lo[:, s, at0:at0 + P]
                        pe.matmul(out, hi, xt_hi[:, k, cols], start=k == 0, stop=False)
                        pe.matmul(out, hi, xt_lo[:, k, cols], start=False, stop=False)
                        last = pe.matmul(out, lo, xt_hi[:, k, cols], start=False, stop=k == KC - 1)
                    last.then_inc(unit_done if q == 5 else pa_mm, 1)
                pe.wait_ge(ga_ready, h + 1)
                order = [OT[8]] + OT[:8] + [OT[9]]

                def intra(n):
                    i, at0, r = order[n]
                    e = 10 * h + n
                    if e >= 2:
                        pe.wait_ge(ga_am, e - 1)
                        pe.wait_ge(ga_kn, e - 1)
                    if n in (0, 9):
                        pe.matmul(ps[:r, e % 2, 0:r], kd[:, at0:at0 + r], gq[:, at0:at0 + r], start=True, stop=True)
                    else:
                        for c in range(2):
                            cols = slice(at0 + CH * c, at0 + CH * c + CH)
                            pe.matmul(ps[CH * c:CH * c + CH, e % 2, 0:CH], kd[:, cols], gq[:, cols], start=True, stop=True)
                    pe.transpose(ps[:r, 2 + e % 2, 0:DK], gk[:, at0:at0 + r], ident[:, :]).then_inc(ga_at, 1)

                intra(0)
                for n in range(10):
                    i, at0, r = order[n]
                    e = 10 * h + n
                    if n < 9:
                        intra(n + 1)
                    pe.wait_ge(ga_am, e + 1)
                    pe.wait_ge(ga_kn, e + 1)
                    if n == 9:
                        pe.wait_ge(ga_q, h + 1)
                        pe.wait_ge(ga_oe, e)
                        out = ps[:TS, 6, 0:DV]
                        pe.matmul(out, at[:TS, e % 2, :], gvs[:, :], start=True, stop=False)
                        for b in range(DB):
                            last = pe.matmul(out, qdm[:, TS * b:TS * b + TS], s0[:, b, :], start=False, stop=b == DB - 1)
                        last.then_inc(ga_o, 1)
                        for half in range(4):
                            pe.wait_ge(ga_s, 26 * h + 17 + 2 * max(half - 1, 0))
                            for m in range(2):
                                b = 2 * half + m
                                last = pe.matmul(ps[:, 4 + half % 2, DV * m:DV * m + DV], kem[:, b, :], gvs[:, :],
                                                 start=True, stop=True)
                            last.then_inc(ga_u, 1)
                        continue
                    if n == 1:
                        pe.wait_ge(pa_ev, 6 * (h + 1))
                    if n:
                        pe.wait_ge(ga_s, 26 * h + 2 * (n - 1) + 1)
                    elif h:
                        pe.wait_ge(ga_s, 26 * h)
                    if n == 0:
                        pe.matmul(ps[:, 4, 0:DV], ken[:r, e % 2, :], gv[:r, 8, :], start=True, stop=True).then_inc(ga_u, 1)
                    else:
                        for c in range(2):
                            rows = slice(CH * c, CH * c + CH)
                            last = pe.matmul(ps[:, 4 + c, 0:DV], ken[rows, e % 2, :],
                                             gv[rows, i, :], start=True, stop=True)
                        last.then_inc(ga_u, 1)
                    if e:
                        pe.wait_ge(ga_oe, e)
                    if n == 0:
                        pe.matmul(ps[:r, 6, 0:DV], at[:r, e % 2, 0:r], gv[:r, 8, :], start=True, stop=True).then_inc(ga_o, 1)
                    else:
                        for c in range(2):
                            rows = slice(CH * c, CH * c + CH)
                            pe.matmul(ps[rows, 6, 0:DV], at[rows, e % 2, :], gv[rows, i, :], start=True, stop=False)
                            chunk = 2 * (n - 1) + c
                            pe.wait_ge(ga_s, 26 * h + chunk + 1)
                            last = pe.matmul(ps[rows, 6, 0:DV], gq[:, at0 + CH * c:at0 + CH * c + CH],
                                             sx[:, chunk % 4, :], start=False, stop=True)
                        last.then_inc(ga_o, 1)
            barrier(pe, 7)
            for n, (i, at0, r) in enumerate(OT):
                pe.wait_ge(po_ok, n + 1)
                if n >= 2:
                    pe.wait_ge(po_lo, n - 1)
                transpose_tile(oin[:, n % 2, :], r, 2 * (n % 2), po_tr)
            pe.wait_ge(po_lo, 10)
            barrier(pe, 8)

            for u in range(U_PG, U_O):
                e0 = evacs_before(u)
                unit_f(u % 2, u + 1, [e0 + c - 1 for c in range(2)])
            pe.wait_ge(evac, evacs_before(U_O))
            barrier(pe, 9)
            pe.wait_ge(mg_lo, KC)
            for u in range(U_O, U_FF):
                unit_n(u % 2, u + 1, evacs_before(u) - 2)
            for t in range(NT):
                if t == 0:
                    pe.wait_ge(evac, evacs_before(U_FF))
                else:
                    if t >= 2:
                        pe.wait_ge(l_lo, t - 1)
                pe.wait_ge(l_ok, t + 1)
                transpose_tile(res[:, t, :], rows_of(t), 2 * (t % 2), l_tr)
            pe.wait_ge(l_lo, NT)
            barrier(pe, 10)

            def up(s, ready, free):
                pe.wait_ge(w_split, ready)
                for c in range(2):
                    if free is not None:
                        pe.wait_ge(f_relu, free + c)
                    for n in range(3):
                        out = ps[:, 3 * c + n, 0:N3]
                        cols = slice(N3 * n, N3 * n + N3)
                        for k in range(KC):
                            at0 = (KC * c + k) * P
                            hi, lo = w_hi[:, s, at0:at0 + P], w_lo[:, s, at0:at0 + P]
                            pe.matmul(out, hi, xt_hi[:, k, cols], start=k == 0, stop=False)
                            pe.matmul(out, hi, xt_lo[:, k, cols], start=False, stop=False)
                            last = pe.matmul(out, lo, xt_hi[:, k, cols], start=False, stop=k == KC - 1)
                    last.then_inc(unit_done if c else half_done, 1)

            def down(s, a, ready, hidden, adds):
                pe.wait_ge(w_split, ready)
                pe.wait_ge(f_lo, hidden)
                for m in range(2 * NT):
                    t, hf = m // 2, m % 2
                    r = rows_of(t)
                    if adds is not None:
                        pe.wait_ge(f_add, adds + m - 1)
                    elif m >= 2:
                        pe.wait_ge(f_add, m - 1)
                    out = ps[:r, 6 + m % 2, :]
                    for k in range(2):
                        cols = slice(P * t, P * t + r)
                        w = slice(1024 * k + 512 * hf, 1024 * k + 512 * hf + 512)
                        pe.matmul(out, a_hi[:, a, k, cols], w_hi[:, s, w], start=k == 0, stop=False)
                        pe.matmul(out, a_lo[:, a, k, cols], w_hi[:, s, w], start=False, stop=False)
                        last = pe.matmul(out, a_hi[:, a, k, cols], w_lo[:, s, w], start=False, stop=k == 1)
                    last.then_inc(unit_done if m == 2 * NT - 1 else f_half, 1)

            up(1, U_FF + 1, None)
            up(0, U_FF + 2, 1)
            down(1, 0, U_FF + 3, 2, None)
            with pe.Fori(0, (FB - 2) // 2) as i:
                for o in range(2):
                    up(0, 4 * i + (U_FF + 4 + 2 * o), 4 * i + (2 * o + 3))
                    down(1, 1 - o, 4 * i + (U_FF + 5 + 2 * o), 4 * i + (4 + 2 * o), 36 * i + 18 * (o + 1))
            down(0, 1, N_UNITS, 2 * FB, 18 * (FB - 1))
            barrier(pe, 11)

        @block.scalar
        def _(act):
            def chunk_ready(c, halves, units):
                act.wait_ge(unit_done if c else half_done, units if c else halves)

            def to_dram(e, dst, src, done):
                act.wait_ge(evac, e)
                act.dma_start(dst, src).then_inc(done, 16)

            for t in range(NT + 1):
                if t < NT:
                    r = rows_of(t)
                    act.wait_ge(var_ok, t + 1)
                    act.activation(small[:r, 2 + t % 2:3 + t % 2], small[:r, t % 2:t % 2 + 1], ACT.Sqrt).then_inc(std_ok, 1)
                if t:
                    r = rows_of(t - 1)
                    act.wait_ge(tr_ok, t)
                    src = flat[:, 1024 * ((t - 1) % 2):1024 * ((t - 1) % 2) + 1024].rearrange("p (k n) -> p k n", n=P)
                    act.activation(xt_hi[:, :, P * (t - 1):P * (t - 1) + r], src[:, :, :r], ACT.Copy).then_inc(hi_ok, 1)
            barrier(act, 1)

            for e in range(8):
                u, c = e // 2, e % 2
                chunk_ready(c, u + 1, u + 1)
                dst = kT3[:, e, :] if e < 4 else stg[:, c, :]
                if e >= 6:
                    act.wait_ge(st_out[c], 16)
                act.activation(dst.rearrange("p (n m) -> p n m", m=N3), ps[:, 3 * c:3 * c + 3, 0:N3], ACT.Copy).then_inc(evac, 1)
                if e >= 4:
                    to_dram(e + 1, qiT_d[P * (e - 4):P * (e - 4) + P, :], dst, st_out[c])
            act.wait_ge(ks_in, 64)
            act.activation(kiS[:, 0:TP], relu[:, 1, 0:TP], ACT.Copy).then_inc(ks_hi, 1)
            act.wait_ge(ks_ok, 1)
            for i in range(1, 8):
                _, w, np_ = keys_of(i)
                act.wait_ge(q_in[i % 2], 32 * ((i + 1) // 2 if i % 2 else i // 2))
                if i > 1:
                    act.wait_ge(ix_mm, IH * (i - 1))
                act.activation(qhi[:, :, :], qraw[:, i % 2, :, :], ACT.Copy).then_inc(q_hi_ok, 1)
                for h in range(IH):
                    g = IH * (i - 1) + h
                    act.wait_ge(ix_mm, g + 1)
                    if g >= 2:
                        act.wait_ge(ix_acc, g - 1)
                    act.activation(relu[:, g % 2, 0:w * np_].rearrange("p (n m) -> p n m", m=w),
                                   ps[:, 4 * (g % 2):4 * (g % 2) + np_, 0:w], ACT.Relu,
                                   scale=HD ** -0.5).then_inc(ix_relu, 1)
            barrier(act, 2)
            width = [512] * 4 + [DS]
            for q in range(5 * DB):
                w = width[q % 5]
                act.wait_ge(s_mm, q + 1)
                if q >= 2:
                    act.wait_ge(i_mm, q - 1)
                act.activation(relu2[:, q % 2, 0:w], ps[0:HD, 2 + q % 2, 0:w], ACT.Relu, scale=HD ** -0.5).then_inc(s_relu, 1)
            barrier(act, 3)

            def f_out(i, u0, per, n_before, dst, func):
                for s in range(2):
                    for c in range(2):
                        u = u0 + s
                        e = 4 * i + (evacs_before(u) + c)
                        chunk_ready(c, 2 * i + (halves_before(u) + 1), 2 * i + (u + 1))
                        act.wait_ge(st_out[c], 32 * i + 16 * (n_before + s))
                        act.activation(stg[:, c, :].rearrange("p (n m) -> p n m", m=N3),
                                       ps[:, 3 * c:3 * c + 3, 0:N3], func).then_inc(evac, 1)
                        rows = dst[bass.ds(512 * i + P * (2 * s + c), P), :]
                        to_dram(e + 1, rows, stg[:, c, :], st_out[c])

            with act.Fori(0, 4) as i:
                f_out(i, U_Q, 0, 2, qT_d, ACT.Copy)
            for t in range(NT):
                r = rows_of(t)
                if t == NT - 1:
                    act.wait_ge(unit_done, U_N + 1)
                else:
                    act.wait_ge(half_done, halves_before(U_N) + t + 1)
                act.activation(vnat[:r, t, :], ps[:r, t % 3, 0:256], ACT.Copy).then_inc(evac, 1)

            for c in range(2):
                act.wait_ge(st_out[c], 16 * 10)

            def fill_out(f):
                u, m, last_one = fill_unit(f)
                if last_one:
                    act.wait_ge(unit_done, u + 1)
                else:
                    act.wait_ge(fill_mm, fill_count(f))
                s = f % 3
                if f >= 3:
                    act.wait_ge(fst_out[s], 16 * (f // 3))
                if f < 8 * NT:
                    r, wid = rows_of(m), 256
                    col = 256 * (u - U_N - 1)
                    dst = gvog_d[P * m:P * m + r, col:col + 256]
                else:
                    r, wid = P, N3
                    row = P * (2 * (u - U_GATE) + m // 3)
                    dst = gate_d[row:row + P, N3 * (m % 3):N3 * (m % 3) + N3]
                bank = 6 + f % 2 if f < F_EARLY else 7
                act.activation(fill_at[:r, s, 0:wid], ps[:r, bank, 0:wid], ACT.Copy).then_inc(fill_ev, 1)
                act.wait_ge(fill_ev, f + 1)
                act.dma_start(dst, fill_at[:r, s, 0:wid]).then_inc(fst_out[s], 16)

            for f in range(F_EARLY):
                fill_out(f)
            barrier(act, 4)

            for n in range(NKV):
                act.wait_ge(c_ks_in[n % 2], 64 * (n // 2 + 1))
                act.activation(kS[:, n, 0:TP], pP[:, n % 2, 0:TP], ACT.Copy).then_inc(c_ks_hi, 1)
            act.wait_ge(c_ks_ok, NKV)

            def q_split(j):
                r = rows_of(j // NKV)
                act.wait_ge(cq_in[j % 2], 32 * (j // 2 + 1))
                if j:
                    act.wait_ge(qk_ok, G * j)
                act.activation(qh2[:, :, :r], qraw2[:, j % 2, :, :r], ACT.Copy).then_inc(cq_hi, 1)

            def exp(hh):
                i = hh // NH
                r = rows_of(i)
                _, w, np_ = keys_of(i)
                act.wait_ge(mx_ok, hh + 1)
                part = pP[:r, hh % 2, 0:w * np_]
                act.activation(part, part, ACT.Exp, bias=mx[:r, hh % 2:hh % 2 + 1], scale=-1.0,
                               accum_out=rsum[:r, hh % NH:hh % NH + 1])
                act.drain().then_inc(exp_ok, 1)

            q_split(0)
            exp(0)
            f = F_EARLY
            for hh in range(NH * NT):
                i = hh // NH
                r = rows_of(i)
                if hh + 1 < NH * NT:
                    if hh % G == G - 2 and hh + 2 < NH * NT:
                        q_split((hh + 2) // G)
                    exp(hh + 1)
                if batches_of(i) > 1:
                    size = min(4, i + 2 - 4)
                    act.wait_ge(pt_tr, tr_before(hh) + 2)
                    act.activation(ptb[:, 1, 0:P * size], ps[:, 5, 0:P * size], ACT.Copy).then_inc(pt_a, 1)
                if f < fills_by(hh):
                    fill_out(f)
                    f += 1
            for s in range(3):
                act.wait_ge(fst_out[s], 16 * (N_FILL // 3))
            barrier(act, 5)

            def att_hi(i):
                r = P if i < 8 else META
                act.wait_ge(att_tr, i + 1)
                src = flat[:, 2560:3584].rearrange("p (k n) -> p k n", n=P)
                act.activation(xt_hi[:, :, P * i:P * i + r], src[:, :, :r], ACT.Copy).then_inc(hi_ok, 1)

            def kt_upper(gg):
                act.wait_ge(kt_tr, gg + 1)
                if gg >= 2:
                    act.wait_ge(kt_qk, gg - 1)
                act.activation(kt[:, gg % 2, 1, :], ps[:, 6, :], ACT.Copy).then_inc(kt_a, 1)

            def load_v(b, grp):
                if b >= 1:
                    act.wait_ge(s_done, 4 * (b - 1) + grp + 1)
                load_pages(act, vpg[:, grp, :, :], cache_v, b, grp, vg_in[grp])

            kt_upper(0)
            kt_upper(1)
            for b in range(DB):
                load_v(b, 0)
                kt_upper(4 * b + 2)
                kt_upper(4 * b + 3)
                load_v(b, 1)
                att_hi(b)
                act.wait_ge(d_mx, b + 1)
                if b:
                    act.wait_ge(d_ptr, 5 * b)
                act.activation(pS[:, :], flat[:, 0:NK], ACT.Exp, bias=mx[:, 1:2], scale=HD ** -0.5,
                               accum_out=rsum[:, 0:1])
                act.drain().then_inc(d_exp, 1)
                if b + 1 < DB:
                    kt_upper(4 * b + 4)
                    kt_upper(4 * b + 5)
                for j in (1, 3):
                    act.wait_ge(d_ptr, 5 * b + j + 1)
                    if j == 3:
                        act.wait_ge(s_done, 4 * b + 2)
                    elif b:
                        act.wait_ge(d_o, b)
                    act.activation(ptS[:, 1, :], ps[:, 6, :], ACT.Copy).then_inc(d_pa, 1)
            att_hi(8)
            act.wait_ge(d_oev, DB)
            act.activation(xt_hi[:, :, TP:T], attT[:, :, :], ACT.Copy).then_inc(hi_ok, 1)
            barrier(act, 6)

            def sigmoid(dst, m, per, n0):
                act.wait_ge(g_in[m % 2], n0 + per * (m // 2 + 1))
                act.activation(dst[:, m % 2, :], dst[:, m % 2, :], ACT.Sigmoid).then_inc(g_sig, 1)

            for c in range(2):
                sigmoid(gst, c, 16, 0)
            act.wait_ge(ga_set, 48)
            for h in range(GH):
                act.wait_ge(ga_lg, h + 1)
                act.activation(zz[:, :].rearrange("p (n m) -> p n m", m=N3), ps[:, 0:3, 0:N3], ACT.Identity,
                               bias=ba[:, h:h + 1]).then_inc(ga_z, 1)
                act.wait_ge(ga_step, 4 * h + 1)
                act.activation(kd[:, :], kd[:, :], ACT.Exp)
                act.drain()
                act.activation(kd[:, :], kd[:, :], ACT.Ln, bias=1.0).then_inc(ga_e, 1)
                act.wait_ge(ga_step, 4 * h + 2)
                act.activation(zz[:, :], bb[:, :], ACT.Exp, scale=1.0 / TAU).then_inc(ga_e, 1)
                act.wait_ge(ga_step, 4 * h + 3)
                act.activation(zz[:, :], bb[:, :], ACT.Exp, scale=-1.0 / TAU).then_inc(ga_e, 1)
                act.wait_ge(ga_step, 4 * h + 4)
                act.activation(zz[:, :], zz[:, :], ACT.Exp, scale=1.0 / TAU).then_inc(ga_e, 1)
                order = [OT[8]] + OT[:8] + [OT[9]]
                for n in range(11):
                    if n < 10:
                        i, at0, r = order[n]
                        e = 10 * h + n
                        act.wait_ge(ga_at, e + 1)
                        if e >= 2:
                            act.wait_ge(ga_o, e - 1)
                            act.wait_ge(ga_u, 13 * h + n - 1 if n >= 2 else 13 * h)
                        act.activation(ken[:r, e % 2, :], ps[:r, 2 + e % 2, 0:DK], ACT.Copy).then_inc(ga_kn, 1)
                    if n:
                        i, at0, r = order[n - 1]
                        e = 10 * h + n - 1
                        act.wait_ge(ga_o, e + 1)
                        if e >= 2:
                            act.wait_ge(ga_oo[e % 2], 16 * (e // 2))
                        act.activation(zz[:r, 0:DV], ps[:r, 6, 0:DV], ACT.Square, accum_out=ssq[:r, i, h:h + 1])
                        act.activation(ostg[:r, e % 2, :], ps[:r, 6, 0:DV], ACT.Copy).then_inc(ga_oe, 1)
                if h + 1 < GH:
                    for c in range(2):
                        sigmoid(gst, 2 * h + 2 + c, 16, 0)
            barrier(act, 7)

            act.wait_ge(po_v, 1)
            act.activation(ssq[:, :, :], ssq[:, :, :], ACT.Sqrt).then_inc(po_sd, 1)
            for n in range(11):
                if n < 10:
                    i, at0, r = OT[n]
                    act.wait_ge(po_in[n % 2], 32 * (n // 2 + 1))
                    act.activation(ogin[:r, n % 2, :], ogin[:r, n % 2, :], ACT.Silu).then_inc(po_sl, 1)
                if n:
                    i, at0, r = OT[n - 1]
                    act.wait_ge(po_tr, n)
                    src = flat[:, 1024 * ((n - 1) % 2):1024 * ((n - 1) % 2) + 1024].rearrange("p (k n) -> p k n", n=P)
                    act.activation(xt_hi[:, :, at0:at0 + r], src[:, :, :r], ACT.Copy).then_inc(po_hi, 1)
            barrier(act, 8)
            for m in range(KC):
                sigmoid(gst2, m, 32, 64)
            barrier(act, 9)
            for c in range(KC):
                act.activation(xt_hi[:, c, :], merged[:, c, :], ACT.Copy).then_inc(mg_hi, 1)

            for t in range(NT + 1):
                if t < NT:
                    r = rows_of(t)
                    act.wait_ge(l_var, t + 1)
                    act.activation(small[:r, 2 + t % 2:3 + t % 2], small[:r, t % 2:t % 2 + 1], ACT.Sqrt).then_inc(l_std, 1)
                if t:
                    r = rows_of(t - 1)
                    act.wait_ge(l_tr, t)
                    src = flat[:, 1024 * ((t - 1) % 2):1024 * ((t - 1) % 2) + 1024].rearrange("p (k n) -> p k n", n=P)
                    act.activation(xt_hi[:, :, P * (t - 1):P * (t - 1) + r], src[:, :, :r], ACT.Copy).then_inc(l_hi, 1)
            barrier(act, 10)

            def hidden(a, halves, units, lows, squares, used):
                for c in range(2):
                    chunk_ready(c, halves, units)
                    if lows is not None:
                        act.wait_ge(f_lo, lows + c)
                    act.activation(rl[:, c, :].rearrange("p (n m) -> p n m", m=N3), ps[:, 3 * c:3 * c + 3, 0:N3],
                                   ACT.Relu).then_inc(f_relu, 1)
                    act.wait_ge(f_sq, squares + c)
                    if used is not None:
                        act.wait_ge(unit_done, used)
                    act.activation(a_hi[:, a, c, :], rl[:, c, :], ACT.Copy).then_inc(f_hi, 1)

            hb = halves_before(U_FF)
            hidden(0, hb + 1, U_FF + 1, None, 1, None)
            hidden(1, hb + 2, U_FF + 2, 1, 3, None)
            with act.Fori(0, (FB - 2) // 2) as i:
                for o in range(2):
                    hidden(o, 2 * i + (hb + 3 + o), 4 * i + (U_FF + 4 + 2 * o), 4 * i + (3 + 2 * o),
                           4 * i + (5 + 2 * o), 4 * i + (U_FF + 3 + 2 * o))
            barrier(act, 11)
            for t in range(NT):
                r = rows_of(t)
                act.wait_ge(l_var, NT + t + 1)
                act.activation(small[:r, 2 + t % 2:3 + t % 2], small[:r, t % 2:t % 2 + 1], ACT.Sqrt).then_inc(l_std, 1)

        @block.vector
        def _(dve):
            def norm_stats(x, r, t, st, m, ok):
                for half in range(2):
                    dve.bn_stats(st[:r, t % 2, half, :], x[:r, 512 * half:512 * half + 512])
                dve.drain()
                dve.bn_aggr(m[:r, t % 2, :], st[:r, t % 2, :, :])
                dve.drain()
                dve.tensor_scalar(small[:r, t % 2:t % 2 + 1], m[:r, t % 2, 1:2], EPS, None, ALU.add).then_inc(ok, 1)

            def norm_apply(y, x, r, t, m, g, b, free, ok):
                dve.reciprocal(small[:r, 4 + t % 2:5 + t % 2], small[:r, 2 + t % 2:3 + t % 2])
                dve.drain()
                ins = dve.tensor_scalar(y[:r, :], x[:r, :], m[:r, t % 2, 0:1], small[:r, 4 + t % 2:5 + t % 2],
                                        ALU.subtract, ALU.mult)
                if free is not None:
                    ins.then_inc(free, 1)
                dve.drain()
                dve.tensor_tensor(y[:r, :], y[:r, :], g[:r, :], ALU.mult)
                dve.drain()
                dve.tensor_tensor(y[:r, :], y[:r, :], b[:r, :], ALU.add).then_inc(ok, 1)

            def lo_part(cols, slot, ok):
                n = cols.stop - cols.start
                src = flat[:, 1024 * slot:1024 * slot + 1024].rearrange("p (k n) -> p k n", n=P)
                dve.tensor_tensor(xt_lo[:, :, cols], src[:, :, :n], xt_hi[:, :, cols].bitcast(F32),
                                  ALU.subtract).then_inc(ok, 1)

            dve.wait_ge(x_in[0], 16)
            norm_stats(xin[:, 0, :], rows_of(0), 0, stats, mv, var_ok)
            dve.wait_ge(ln_in, 48)
            for t in range(NT + 1):
                if t + 1 < NT:
                    dve.wait_ge(x_in[(t + 1) % 2], 16 * ((t + 1) // 2 + 1))
                    norm_stats(xin[:, (t + 1) % 2, :], rows_of(t + 1), t + 1, stats, mv, var_ok)
                if t < NT:
                    dve.wait_ge(std_ok, t + 1)
                    if t >= 2:
                        dve.wait_ge(h_out[t % 2], 16 * (t // 2))
                        dve.wait_ge(tr_ok, t - 1)
                    norm_apply(hbuf[:, t % 2, :], xin[:, t % 2, :], rows_of(t), t, mv, lg, lb, x_free, h_ready)
                if t:
                    dve.wait_ge(hi_ok, t)
                    lo_part(slice(P * (t - 1), P * (t - 1) + rows_of(t - 1)), (t - 1) % 2, lo_ok)
            dve.memset(ssq[:, :, :], 0.0)
            dve.wait_ge(consts, 7)
            dve.tensor_reduce(delta[:, :], d8[:, :, :].rearrange("p i j -> p j i"), AX.X, ALU.add)
            dve.tensor_reduce(bsel[:, :], d8[:, :, :], AX.X, ALU.add)
            for t in range(DS):
                dve.memset(m8[:TS, t:t + 1], float(t))
            dve.drain()
            dve.tensor_tensor(triS[:, :], delta[:, :], m8[:TS, :], ALU.mult)
            dve.drain()
            dve.tensor_reduce(small[:TS, 8:9], triS[:, :], AX.X, ALU.add)
            dve.drain()
            dve.tensor_scalar(triS[:, :], m8[:TS, :], small[:TS, 8:9], NEG, ALU.is_gt, ALU.mult)
            barrier(dve, 1)

            dve.memset(kiS[:, TP:1056].bitcast(F32), 0.0)
            for t in range(NT):
                r = rows_of(t)
                dve.wait_ge(kn_tr, t + 1)
                if t >= 2:
                    dve.wait_ge(kn_out[t % 2], 32 * (t // 2))
                dve.tensor_scalar(winat[:r, t, :], ps[:r, 6 + t % 2, 256 + HD:256 + HD + IH], IH ** -0.5, None, ALU.mult)
                dve.tensor_copy(relu[:r, t % 2, 0:384], ps[:r, 6 + t % 2, 0:384]).then_inc(kn_ok, 1)
            dve.wait_ge(ks_hi, 1)
            lower = slice(HD, P)
            dve.tensor_tensor(kiS[lower, 0:TP], relu[lower, 1, 0:TP], kiS[lower, 0:TP].bitcast(F32),
                              ALU.subtract).then_inc(ks_ok, 1)
            for i in range(1, 8):
                L, w, np_ = keys_of(i)
                acc = isc[:, mask_at(i):mask_at(i) + L]
                dve.wait_ge(q_hi_ok, i)
                dve.tensor_tensor(qlo[:, :, :], qraw[:, i % 2, :, :], qhi[:, :, :].bitcast(F32),
                                  ALU.subtract).then_inc(q_lo_ok, 1)
                for h in range(IH):
                    g = IH * (i - 1) + h
                    dve.wait_ge(ix_relu, g + 1)
                    if h == 0:
                        dve.tensor_scalar(acc, relu[:, g % 2, 0:L], winat[:, i, 0:1], None, ALU.mult).then_inc(ix_acc, 1)
                    else:
                        dve.wait_ge(ix_acc, g)
                        dve.scalar_tensor_tensor(acc, relu[:, g % 2, 0:L], winat[:, i, h:h + 1], acc,
                                                 ALU.mult, ALU.add).then_inc(ix_acc, 1)
                dve.drain()
                dve.tensor_tensor(acc[:, L - P:L], acc[:, L - P:L], tri[:, :], ALU.add)
            barrier(dve, 2)

            dve.wait_ge(sx_in, 16 * 16)
            for b in range(DB):
                dve.tensor_scalar(wb[:, b, :], delta[:, :], wsel[:, b:b + 1], IH ** -0.5, ALU.mult, ALU.mult)
            dve.drain().then_inc(wb_ok, 1)
            width = [512] * 4 + [DS]
            for b in range(DB):
                def ev(grp):
                    gg = 4 * b + grp
                    dve.wait_ge(kx_tr, gg + 1)
                    dve.tensor_copy(kxT[:, 512 * grp:512 * grp + 512], ps[0:HD, gg % 2, :]).then_inc(kx_ev, 1)

                def ib_ev(p):
                    q = 5 * b + p
                    dve.wait_ge(i_mm, q + 1)
                    dve.tensor_copy(ib[:, 512 * p:512 * p + width[p]], ps[0:DS, 4 + q % 2, 0:width[p]]).then_inc(i_ev, 1)

                if b:
                    dve.wait_ge(s_mm, 5 * b)
                dve.tensor_copy(kxT[:, PAST:NK], kT3[0:HD, 2, TP + DS * b:TP + DS * b + DS]).then_inc(kx_ev, 1)
                ev(0); ev(1); ev(2)
                if b:
                    dve.wait_ge(ib_out, 16 * b)
                ib_ev(0); ev(3); ib_ev(1); ib_ev(2); ib_ev(3); ib_ev(4)
            dve.wait_ge(ib_out, 16 * DB)
            dve.tensor_tensor(iscS[:, PAST:NK], iscS[:, PAST:NK], triS[:, :], ALU.add)
            barrier(dve, 3)

            sets = [(isc[:, mask_at(i):mask_at(i) + keys_of(i)[0]], masks[:, mask_at(i):mask_at(i) + keys_of(i)[0]],
                     P, keys_of(i)[0]) for i in range(1, 8)] + [(iscS[:, :], maskS[:, :], TS, NK)]

            def as_float(dst, src):
                dve.tensor_scalar(low_m[:, :], src[:, :], 31, 0x7FFFFFFF, ALU.arith_shift_right, ALU.bitwise_and)
                dve.drain()
                dve.scalar_tensor_tensor(dst[:, :], low_m[:, :], -1, src[:, :], ALU.bitwise_xor, ALU.bitwise_xor)
                dve.drain()

            dve.memset(cut[:, :], 0)
            dve.memset(cnt[:, :], 0.0)
            dve.memset(bit[:, :], 1)
            dve.drain()
            dve.tensor_scalar(bit[:, :], bit[:, :], 31, None, ALU.logical_shift_left)
            with dve.Fori(0, 32):
                dve.drain()
                dve.tensor_tensor(cand[:, :], cut[:, :], bit[:, :], ALU.bitwise_or)
                dve.drain()
                as_float(take, cand)
                for j, (x, m, r, n) in enumerate(sets):
                    dve.tensor_scalar(m, x, take[:r, j:j + 1].bitcast(F32), None, ALU.is_ge, ALU.add,
                                      accum_out=cnt[:r, j:j + 1])
                dve.drain()
                dve.tensor_scalar(low_m[:, :], cnt[:, :], float(TOPK), -1.0, ALU.is_ge, ALU.mult)
                dve.drain()
                dve.tensor_tensor(low_m[:, :], low_m[:, :], bit[:, :], ALU.bitwise_and)
                dve.drain()
                dve.tensor_tensor(cut[:, :], cut[:, :], low_m[:, :], ALU.bitwise_or)
                dve.tensor_scalar(bit[:, :], bit[:, :], 1, None, ALU.logical_shift_right)
            dve.drain()
            as_float(take, cut)
            for j, (x, m, r, n) in enumerate(sets):
                dve.tensor_scalar(m, x, take[:r, j:j + 1].bitcast(F32), None, ALU.is_gt, ALU.add,
                                  accum_out=cnt[:r, j:j + 1])
            dve.drain()
            dve.tensor_scalar(need[:, :], cnt[:, :], -1.0, float(TOPK), ALU.mult, ALU.add)
            dve.drain()
            for j, (x, m, r, n) in enumerate(sets):
                eq = eqb[:r, 0:n]
                dve.tensor_scalar(eq, x, take[:r, j:j + 1].bitcast(F32), None, ALU.is_equal)
                dve.drain()
                dve.tensor_tensor_scan(x, eq, eq, 0.0, ALU.add, ALU.max)
                dve.drain()
                dve.scalar_tensor_tensor(eq, x, need[:r, j:j + 1], eq, ALU.is_le, ALU.mult)
                dve.drain()
                dve.tensor_tensor(m, m, eq, ALU.add)
                dve.drain()
                dve.tensor_scalar(m, m, 1.0, -NEG, ALU.subtract, ALU.mult)
                dve.drain()
                last, add = (m[:, n - P:n], tri[:, :]) if r == P else (m[:, PAST:NK], triS[:, :])
                dve.tensor_tensor(last, last, add, ALU.add)
            dve.memset(masks[:, 0:META], 0.0)
            dve.tensor_copy(masks[:, META:META + P], tri[:, :])
            dve.memset(masks[:, mask_at(7) + TP:IW], NEG)
            barrier(dve, 4)

            for n in range(NKV):
                dve.memset(kS[:, n, TP:1056].bitcast(F32), 0.0)
                dve.wait_ge(c_ks_hi, n + 1)
                dve.tensor_tensor(kS[lower, n, 0:TP], pP[lower, n % 2, 0:TP], kS[lower, n, 0:TP].bitcast(F32),
                                  ALU.subtract).then_inc(c_ks_ok, 1)

            def q_split(j):
                r = rows_of(j // NKV)
                dve.wait_ge(cq_hi, j + 1)
                dve.tensor_tensor(ql2[:, :, :r], qraw2[:, j % 2, :, :r], qh2[:, :, :r].bitcast(F32),
                                  ALU.subtract).then_inc(cq_lo, 1)

            def masked_max(hh):
                i = hh // NH
                r = rows_of(i)
                _, w, np_ = keys_of(i)
                bank = 0 if np_ == 3 else 2 * (hh % 2)
                mask = masks[:r, mask_at(i):mask_at(i) + w * np_] if i < 8 else tri16[:r, :]
                dve.wait_ge(qk_ok, hh + 1)
                if hh >= 2:
                    dve.wait_ge(pt_tr, tr_before(hh - 1))
                v = lambda a: a.rearrange("p (n m) -> p n m", m=w)
                dve.tensor_tensor_reduce(out=v(pP[:r, hh % 2, 0:w * np_]), in0=ps[:r, bank:bank + np_, 0:w],
                                         in1=v(mask), scale=-HD ** -0.5, scalar=3e38, op0=ALU.add, op1=ALU.min,
                                         accum_out=mx[:r, hh % 2:hh % 2 + 1]).then_inc(mx_ok, 1)

            def evac_p(hh, j):
                i = hh // NH
                r, size = rows_of(i), min(4, (i + 2 if i < 8 else 1) - 4 * j)
                dve.wait_ge(pt_tr, tr_before(hh) + j + 1)
                first = 0
                if j == 0:
                    last = dve.tensor_copy(ptb[:META, 0, 0:r], ps[:META, 4, 0:r])
                    first = 1
                if size > first:
                    last = dve.tensor_copy(ptb[:, j, P * first:P * size], ps[:, 4, P * first:P * size])
                last.then_inc(pt_v, 1)

            def scale(hh):
                i, m = hh // NH, hh % NH
                r = rows_of(i)
                inv = small[:r, 12 + m % 2:13 + m % 2]
                dve.wait_ge(exp_ok, hh + 1)
                dve.reciprocal(inv, rsum[:r, m:m + 1])
                dve.drain()
                if m % 8 == 0 and i:
                    dve.wait_ge(att_out[m // 8], 16 * i)
                dve.wait_ge(pv_ok, tr_before(hh + 1))
                dve.tensor_scalar(attn[:r, HD * m:HD * m + HD], ps[:r, 6, 0:HD], inv, None,
                                  ALU.mult).then_inc(o_ev, 1)

            q_split(0)
            masked_max(0)
            masked_max(1)
            for hh in range(NH * NT):
                if hh % G == G - 2 and hh + 2 < NH * NT:
                    q_split((hh + 2) // G)
                evac_p(hh, 0)
                if batches_of(hh // NH) == 3:
                    evac_p(hh, 2)
                if hh + 2 < NH * NT:
                    masked_max(hh + 2)
                scale(hh)
            barrier(dve, 5)

            dve.memset(qblk[:, :, :, :], 0.0)
            dve.drain().then_inc(d_set, 1)
            for b in range(DB):
                dve.tensor_scalar(esel[:, b, :, :], delta[:, None, :].broadcast_to((TS, NH, DS)), bsel[:, b:b + 1],
                                  None, ALU.mult)
            dve.drain().then_inc(d_set, 1)
            def att_lo(i):
                r = P if i < 8 else META
                cols = slice(P * i, P * i + r)
                dve.wait_ge(hi_ok, NT + i + 1)
                src = flat[:, 2560:3584].rearrange("p (k n) -> p k n", n=P)
                dve.tensor_tensor(xt_lo[:, :, cols], src[:, :, :r], xt_hi[:, :, cols].bitcast(F32),
                                  ALU.subtract).then_inc(lo_ok, 1)

            def kt_lower(gg):
                dve.wait_ge(kt_tr, gg + 1)
                if gg >= 2:
                    dve.wait_ge(kt_qk, gg - 1)
                dve.tensor_copy(kt[:, gg % 2, 0, :], ps[:, 5, :]).then_inc(kt_v, 1)

            def o_out(b):
                dve.wait_ge(d_ot, b + 1)
                for half in range(2):
                    rows = slice(HD * half, HD * half + HD)
                    src = ps[rows, 4, 256:256 + P].rearrange("p (c a t) -> p c a t", a=2, t=DS)
                    last = dve.tensor_copy(attT[rows, :, DS * b:DS * b + DS], src[:, :, half, :])
                last.then_inc(d_oev, 1)

            kt_lower(0)
            kt_lower(1)
            for b in range(DB):
                if b:
                    o_out(b - 1)
                kt_lower(4 * b + 2)
                kt_lower(4 * b + 3)
                dve.wait_ge(d_qk, b + 1)
                dve.tensor_reduce(mx[:, 0:1], flat[:, 0:NK], AX.X, ALU.max)
                dve.drain()
                dve.tensor_scalar(mx[:, 1:2], mx[:, 0:1], -HD ** -0.5, None, ALU.mult).then_inc(d_mx, 1)
                att_lo(b)
                if b + 1 < DB:
                    kt_lower(4 * b + 4)
                dve.wait_ge(d_exp, b + 1)
                dve.reciprocal(small[:, 9:10], rsum[:, 0:1])
                dve.drain()
                dve.tensor_scalar(pS[:, :], pS[:, :], small[:, 9:10], None, ALU.mult).then_inc(d_p, 1)
                if b + 1 < DB:
                    kt_lower(4 * b + 5)
                for j in (0, 2, 4):
                    dve.wait_ge(d_ptr, 5 * b + j + 1)
                    if j:
                        dve.wait_ge(s_done, 4 * b + j - 1)
                    wid, n = (P, 512) if j < 4 else (DS, P)
                    dve.tensor_copy(ptS[:wid, 0, 0:n], ps[:wid, 5, 0:n]).then_inc(d_pv, 1)
                dve.wait_ge(d_o, b + 1)
                for n in range(NKV):
                    rows = slice(32 * n, 32 * n + 32)
                    last = dve.tensor_copy(oS[rows, :, :], ps[rows, 7, HD * n:HD * n + HD][:, None, :].broadcast_to((32, 2, HD)))
                last.then_inc(d_oc, 1)
            o_out(DB - 1)
            att_lo(8)
            dve.wait_ge(hi_ok, 2 * NT + 1)
            dve.tensor_tensor(xt_lo[:, :, TP:T], attT[:, :, :], xt_hi[:, :, TP:T].bitcast(F32), ALU.subtract)
            barrier(dve, 6)

            def gated(m, base, g, dst, add=None, sig=0):
                e = evacs_before(base) + m
                u = base + m // 2
                if m % 2:
                    dve.wait_ge(unit_done, u + 1)
                else:
                    dve.wait_ge(half_done, halves_before(u) + 1)
                dve.wait_ge(g_sig, sig + m + 1)
                v = lambda a: a.rearrange("p (n m) -> p n m", m=N3)
                ins = dve.tensor_tensor(v(dst), ps[:, 3 * (m % 2):3 * (m % 2) + 3, 0:N3], v(g[:, m % 2, :]), ALU.mult)
                if add is not None:
                    dve.drain()
                    ins = dve.tensor_tensor(dst, dst, add[:, m % 2, :], ALU.add)
                ins.then_inc(evac, 1)

            def pa_gated(h, q):
                dve.wait_ge(unit_done if q == 5 else pa_mm, U_PA + h + 1 if q == 5 else 5 * h + q + 1)
                dve.wait_ge(g_sig, 2 * h + q // 3 + 1)
                part = gst[:, q // 3, N3 * (q % 3):N3 * (q % 3) + N3]
                dve.tensor_tensor(part, ps[:, 5 + 2 * (q % 2), 0:N3], part, ALU.mult).then_inc(pa_ev, 1)

            dve.memset(reset[:, :], 1.0)
            dve.memset(qdm[:, :], 0.0)
            dve.drain()
            dve.memset(reset[:, 0:SEQ].rearrange("p (c n) -> p c n", n=CH)[:, :, 0:1], 0.0)
            dve.memset(reset[:, SEQ:SEQ + 1], 0.0)
            dve.memset(reset[:, TP:T].rearrange("p (c n) -> p c n", n=DS)[:, :, 0:1], 0.0)
            dve.tensor_tensor(bd64[:, :].rearrange("p (b t) -> p b t", t=DS),
                              causal[:TS, :].rearrange("p (b t) -> p b t", t=DS),
                              bsel[:, :].unsqueeze(2).broadcast_to((TS, DB, DS)), ALU.mult)
            segs = [(0, SEQ, CH), (SEQ, TP, META), (TP, T, DS)]
            for h in range(GH):
                dve.wait_ge(ga_z, h + 1)
                dve.scalar_tensor_tensor(kd[:, :], zz[:, :], -1.0, zz[:, :], ALU.mult, ALU.min).then_inc(ga_step, 1)
                dve.wait_ge(ga_e, 4 * h + 1)
                dve.scalar_tensor_tensor(zz[:, :], zz[:, :], 0.0, kd[:, :], ALU.min, ALU.subtract)
                dve.drain()
                dve.tensor_tensor_scan(bb[:, :], reset[:, :], zz[:, :], 0.0, ALU.mult, ALU.add).then_inc(ga_step, 1)
                pa_gated(h, 0)
                dve.wait_ge(ga_in, 96 * (h + 1))
                dve.wait_ge(ga_e, 4 * h + 2)
                dve.scalar_tensor_tensor(gq[:, :], gq[:, :], DK ** -0.5, zz[:, :], ALU.mult, ALU.mult)
                for (a, z, n), at0 in zip(segs, (0, 16, 17)):
                    k = (z - a) // n
                    dve.tensor_copy(dec[:, at0:at0 + k].unsqueeze(2),
                                    zz[:, a:z].rearrange("p (c n) -> p c n", n=n)[:, :, n - 1:n])
                dve.drain().then_inc(ga_step, 1)
                pa_gated(h, 1)
                dve.wait_ge(ga_e, 4 * h + 3)
                dve.tensor_tensor(kd[:, :], gk[:, :], zz[:, :], ALU.mult)
                dve.drain()
                for a, z, n in segs:
                    v = bb[:, a:z].rearrange("p (c n) -> p c n", n=n)
                    dve.tensor_tensor(zz[:, a:z].rearrange("p (c n) -> p c n", n=n),
                                      v[:, :, n - 1:n].broadcast_to((P, (z - a) // n, n)), v, ALU.subtract)
                dve.drain().then_inc(ga_step, 1)
                pa_gated(h, 2)
                dve.wait_ge(ga_e, 4 * h + 4)
                dve.tensor_tensor(gk[:, :], gk[:, :], zz[:, :], ALU.mult)
                dve.tensor_copy(qdm[:, :].rearrange("p (b c) -> p b c", c=72)[:, :, 0:DS],
                                gq[:, TP:T].rearrange("p (b t) -> p b t", t=DS))
                dve.drain().then_inc(ga_ready, 1)
                for q in range(3, 6):
                    pa_gated(h, q)
                order = [OT[8]] + OT[:8] + [OT[9]]
                if h:
                    dve.wait_ge(ga_so, 32 * h)
                for n in range(11):
                    if n < 10:
                        i, at0, r = order[n]
                        e = 10 * h + n
                        dve.wait_ge(ga_at, e + 1)
                        if e >= 2:
                            dve.wait_ge(ga_o, e - 1)
                        wid = META if n == 0 else CH
                        m = bd64 if n == 9 else causal
                        dve.tensor_tensor(at[:r, e % 2, 0:wid], ps[:r, e % 2, 0:wid], m[:r, 0:wid], ALU.mult).then_inc(ga_am, 1)
                    if n == 0:
                        continue
                    nn = n - 1
                    e = 10 * h + nn
                    if nn == 0:
                        dve.wait_ge(ga_u, 13 * h + 1)
                        dve.tensor_copy(sx[:, 0, :], ps[:, 4, 0:DV]).then_inc(ga_s, 1)
                    elif nn < 9:
                        dve.wait_ge(ga_u, 13 * h + nn + 1)
                        for c in range(2):
                            chunk = 2 * (nn - 1) + c
                            dve.wait_ge(ga_s, 26 * h + chunk + 1)
                            if chunk >= 3:
                                dve.wait_ge(ga_o, 10 * h + (chunk - 3) // 2 + 2)
                            dve.scalar_tensor_tensor(sx[:, (chunk + 1) % 4, :], sx[:, chunk % 4, :],
                                                     dec[:, chunk:chunk + 1],
                                                     ps[:, 4 + c, 0:DV], ALU.mult, ALU.add).then_inc(ga_s, 1)
                i, at0, r = order[9]
                dve.wait_ge(ga_kn, 10 * h + 10)
                dve.tensor_tensor(kem[:, :, :], ken[:TS, (10 * h + 9) % 2, :][:, None, :].broadcast_to((TS, DB, DK)),
                                  bsel[:, :].unsqueeze(2).broadcast_to((TS, DB, DK)), ALU.mult).then_inc(ga_q, 1)
                dve.wait_ge(ga_o, 10 * h + 10)
                for b in range(DB):
                    if b % 2 == 0:
                        dve.wait_ge(ga_u, 13 * h + 9 + b // 2 + 1)
                    dve.scalar_tensor_tensor(s0[:, b, :], s0[:, b, :], dec[:, 17 + b:18 + b],
                                             ps[:, 4 + (b // 2) % 2, DV * (b % 2):DV * (b % 2) + DV],
                                             ALU.mult, ALU.add).then_inc(ga_s, 1)
                dve.drain().then_inc(ga_s, 1)
                dve.wait_ge(ga_oe, 10 * h + 10)
                dve.drain().then_inc(ga_head, 1)
            barrier(dve, 7)

            dve.memset(small[:, 10:11], 0.0)
            dve.tensor_scalar(ssq[:, :, :], ssq[:, :, :], 1.0 / DV, EPS, ALU.mult, ALU.add).then_inc(po_v, 1)
            dve.wait_ge(po_sd, 1)
            dve.reciprocal(ssq[:, :, :], ssq[:, :, :])
            dve.wait_ge(po_set, 16)
            dve.drain()
            for n in range(11):
                if n < 10:
                    i, at0, r = OT[n]
                    dve.wait_ge(po_in[n % 2], 32 * (n // 2 + 1))
                    o = oin[:r, n % 2, :].rearrange("p (h v) -> p h v", v=DV)
                    for h in range(GH):
                        dve.scalar_tensor_tensor(o[:, h, :], o[:, h, :], ssq[:r, i, h:h + 1], gnb[:r, :], ALU.mult, ALU.mult)
                    dve.wait_ge(po_sl, n + 1)
                    dve.drain()
                    dve.tensor_tensor(oin[:r, n % 2, :], oin[:r, n % 2, :], ogin[:r, n % 2, :], ALU.mult).then_inc(po_ok, 1)
                if n:
                    i, at0, r = OT[n - 1]
                    dve.wait_ge(po_hi, n)
                    lo_part(slice(at0, at0 + r), (n - 1) % 2, po_lo)
            barrier(dve, 8)
            for m in range(KC):
                gated(m, U_PG, gst2, merged[:, m, :], pst2, KC)
            barrier(dve, 9)
            for c in range(KC):
                dve.wait_ge(mg_hi, c + 1)
                dve.tensor_tensor(xt_lo[:, c, :], merged[:, c, :], xt_hi[:, c, :].bitcast(F32), ALU.subtract).then_inc(mg_lo, 1)

            dve.wait_ge(res_in, 32)
            for u in range(U_O, U_FF):
                for t in range(NT):
                    r = rows_of(t)
                    if t == NT - 1:
                        dve.wait_ge(unit_done, u + 1)
                    else:
                        dve.wait_ge(half_done, halves_before(u) + t + 1)
                    dst = res[:r, t, 256 * (u - U_O):256 * (u - U_O) + 256]
                    dve.scalar_tensor_tensor(dst, dst, ALPHA, ps[:r, t % 3, 0:256], ALU.mult, ALU.add).then_inc(evac, 1)
            dve.drain()

            def norm(first, ok0, write_xt):
                norm_stats(res[:, 0, :], P, 0, stats2, mv2, l_var)
                dve.wait_ge(ln2_in, first)
                for t in range(NT + 1):
                    if t + 1 < NT:
                        norm_stats(res[:, t + 1, :], rows_of(t + 1), t + 1, stats2, mv2, l_var)
                    if t < NT:
                        dve.wait_ge(l_std, ok0 + t + 1)
                        norm_apply(res[:, t, :], res[:, t, :], rows_of(t), t, mv2, lg2, lb2, None, l_ok)
                    if t and write_xt:
                        dve.wait_ge(l_hi, t)
                        lo_part(slice(P * (t - 1), P * (t - 1) + rows_of(t - 1)), (t - 1) % 2, l_lo)

            norm(32, 0, True)
            barrier(dve, 10)

            def square(c, relus):
                dve.wait_ge(f_relu, relus + c)
                dve.tensor_tensor(rl[:, c, :], rl[:, c, :], rl[:, c, :], ALU.mult).then_inc(f_sq, 1)

            def low(c, a, his):
                dve.wait_ge(f_hi, his + c)
                dve.tensor_tensor(a_lo[:, a, c, :], rl[:, c, :], a_hi[:, a, c, :].bitcast(F32), ALU.subtract).then_inc(f_lo, 1)

            def sums(m0, m1, halves, units, first=False):
                for m in range(m0, m1):
                    t, hf = m // 2, m % 2
                    r = rows_of(t)
                    if m == 2 * NT - 1:
                        dve.wait_ge(unit_done, units)
                    else:
                        dve.wait_ge(f_half, halves + m)
                    dst = res[:r, t, 512 * hf:512 * hf + 512]
                    if first:
                        dve.scalar_tensor_tensor(dst, dst, ALPHA, ps[:r, 6 + m % 2, :], ALU.mult, ALU.add).then_inc(f_add, 1)
                    else:
                        dve.tensor_tensor(dst, dst, ps[:r, 6 + m % 2, :], ALU.add).then_inc(f_add, 1)

            for j in range(2):
                for c in range(2):
                    square(c, 2 * j + 1)
                    low(c, j, 2 * j + 1)
            sums(0, 18, 1, U_FF + 3, True)
            with dve.Fori(0, (FB - 2) // 2) as i:
                for o in range(2):
                    n = 4 * i + (5 + 2 * o)
                    square(0, n)
                    low(0, o, n)
                    hv, uv = 34 * i + 17 * (o + 1) + 1, 4 * i + (U_FF + 5 + 2 * o)
                    square(1, n)
                    sums(0, 2, hv, uv)
                    low(1, o, n)
                    sums(2, 18, hv, uv)
            sums(0, 18, 17 * (FB - 1) + 1, N_UNITS)
            barrier(dve, 11)
            norm(64, NT, False)


def tr_before(hh):
    return sum(batches_of(h // NH) for h in range(hh))


def _units(inp):
    def f_unit(w, c0, c1):
        parts = [w[:, c:c + P].reshape(KC, P, P).transpose(1, 0, 2) for c in (c0, c1)]
        return np.concatenate(parts, axis=1).reshape(P, UNIT)

    def n_unit(w, c0):
        return w[:, c0:c0 + 256].reshape(KC, P, 256).transpose(1, 0, 2).reshape(P, UNIT)

    w, wa, wg, wo = inp["w_in"][0], inp["w_proj_attn"][0], inp["w_proj_gla"][0], inp["w_out"][0]
    up, down = inp["w_ff_up"][0], inp["w_ff_down"][0]
    us = [f_unit(w, C_K, C_K + P), f_unit(w, C_KI, C_A1)]
    us += [f_unit(w, C_QI + 256 * j, C_QI + 256 * j + P) for j in range(2)]
    us += [f_unit(w, C_Q + 256 * j, C_Q + 256 * j + P) for j in range(4)]
    us += [f_unit(w, c + 256 * j, c + 256 * j + P) for c in (C_GQ, C_GK) for j in range(2)]
    us += [n_unit(w, C_V)]
    us += [n_unit(w, c + 256 * j) for c in (C_GV, C_OG) for j in range(4)]
    us += [f_unit(w, C_GT + 256 * j, C_GT + 256 * j + P) for j in range(8)]
    us += [f_unit(m, 256 * j, 256 * j + P) for m in (wa, wg) for j in range(4)]
    us += [n_unit(wo, 256 * j) for j in range(4)]
    ups = [f_unit(up, 256 * j, 256 * j + P) for j in range(FB)]
    downs = [down[256 * j:256 * j + 256].reshape(2, P, D).transpose(1, 0, 2).reshape(P, UNIT) for j in range(FB)]
    us += [ups[0]]
    for j in range(1, FB):
        us += [ups[j], downs[j - 1]]
    return np.stack(us + [downs[FB - 1]])


def kernel(**inputs):
    import concourse.bacc as bacc
    from concourse.bass_utils import run_bass_kernel_spmd

    inp = {k: np.asarray(v) for k, v in inputs.items()}
    f = np.ascontiguousarray
    pool = inp["cache_k"].shape[1]
    arrays = {
        "x_all": f(np.concatenate([inp["x_prompt"][0], inp["meta_tokens"], inp["x_sample"].reshape(TS, D)])),
        "cache_k": f(inp["cache_k"][0].reshape(pool, PAGE, NKV * HD)),
        "cache_v": f(inp["cache_v"][0].reshape(pool, PAGE, NKV * HD)),
        "cache_kidx": f(inp["cache_kidx"][0]),
        "state": f(inp["state_gla"][0]),
        "page_table": f(inp["page_table"].reshape(1, DB * NPG)),
        "ln_p": f(np.stack([inp["ln_in_g"], inp["ln_in_b"], inp["ln1_g"][0], inp["ln1_b"][0],
                            inp["ln2_g"][0], inp["ln2_b"][0]])),
        "w_stream": f(_units(inp)),
        "w_a2": f(inp["w_gla_a2"][0]),
        "b_a": f(inp["b_gla_a"][0]),
        "gnorm": f(inp["gla_norm_g"]),
    }
    outs = [("y_p", (SEQ, D)), ("y_s", (TS, D)), ("k_p", (TP, 256)), ("v_p", (TP, 256)), ("ki_p", (TP, HD)),
            ("st_p", (GH, DK, DV)), ("k_s", (TS, 256)), ("v_s", (TS, 256)), ("ki_s", (TS, HD)),
            ("st_s", (DB, GH, DK, DV))]
    nc = bacc.Bacc("TRN2", target_bir_lowering=False, num_devices=1)
    ins = [nc.dram_tensor(n, a.shape, mybir.dt.from_np(a.dtype), kind="ExternalInput").ap() for n, a in arrays.items()]
    out_aps = [nc.dram_tensor(n, s, F32, kind="ExternalOutput").ap() for n, s in outs]
    build(nc, *ins, out_aps)
    r = run_bass_kernel_spmd(nc, [arrays], core_ids=[0]).results[0]
    return (r["y_p"].reshape(1, SEQ, D), r["y_s"].reshape(DB, DS, D),
            r["k_p"].reshape(1, 1, TP, NKV, HD), r["v_p"].reshape(1, 1, TP, NKV, HD), r["ki_p"].reshape(1, 1, TP, HD),
            r["st_p"].reshape(1, 1, GH, DK, DV), r["k_s"].reshape(1, DB, DS, NKV, HD),
            r["v_s"].reshape(1, DB, DS, NKV, HD), r["ki_s"].reshape(1, DB, DS, HD),
            r["st_s"].reshape(1, DB, GH, DK, DV))
```

```python
from contextlib import ExitStack

import numpy as np
import concourse.bass as bass
from concourse import mybir

F32 = mybir.dt.float32
F32R = mybir.dt.float32r
BF16 = mybir.dt.bfloat16
I32 = mybir.dt.int32
ALU = mybir.AluOpType
ACT = mybir.ActivationFunctionType
AX = mybir.AxisListType

P = 128
D = 1024
KC = D // P
SEQ, META, DB, DS = 1024, 16, 8, 8
TP = SEQ + META
TS = DB * DS
T = TP + TS
NT = -(-T // P)
N3 = T // 3
HD, NH, NKV, G = 64, 16, 4, 4
IH = 8
PAST, PAGE, NPG = 2048, 128, 16
NK = PAST + DS
TOPK = 256
GH, DK, DV, CH = 4, 128, 256, 64
RANK = 16
DFF = 4096
FB = DFF // 256
EPS = 1e-5
ALPHA = 2 ** 0.25
TAU = 16.0
NEG = -1e30
TAKEN = -3e38

UNIT = 2048
C_Q, C_K, C_V, C_QI, C_KI, C_GQ, C_GK, C_GV, C_OG, C_A1, C_GT = (
    0, 1024, 1280, 1536, 2048, 2120, 2632, 3144, 4168, 5192, 5208)
U_F1, U_Q, U_N, U_GATE, U_PA, U_PG, U_O, U_FF = 0, 4, 12, 21, 29, 33, 37, 41
N_UNITS = U_FF + 2 * FB


def is_natural(u):
    return U_N <= u < U_GATE or U_O <= u < U_FF


def is_filler(u):
    return U_N < u < U_PG


N_FILL = 8 * NT + 8 * 6


F_EARLY = 7 * NT


F_START = F_EARLY + 6


def fills_by(hh):
    if hh < 0:
        return F_EARLY
    between = N_FILL - F_START - 2 * NH
    mid = min(max(hh + 1 - NH, 0), NH * (NT - 2))
    return F_START + min(hh + 1, NH) + between * mid // (NH * (NT - 2)) + max(hh + 1 - NH * (NT - 1), 0)


def fill_unit(f):
    if f < 8 * NT:
        return U_N + 1 + f // NT, f % NT, f % NT == NT - 1
    return U_GATE + (f - 8 * NT) // 6, (f - 8 * NT) % 6, (f - 8 * NT) % 6 == 5


def fill_count(f):
    return sum(not fill_unit(j)[2] for j in range(f + 1))


def fill_unit_start(u):
    return NT * (u - U_N - 1) if u <= U_GATE else 8 * NT + 6 * (u - U_GATE)


def batches_of(i):
    return -(-(1 + (i + 1 if i < 8 else 0)) // 4)


def batches_before(hh, parity):
    return sum((batches_of(h // NH) + 1 - parity) // 2 for h in range(hh))


def halves_before(u):
    return sum((NT - 1 if is_natural(v) else 1) * (not is_filler(v)) for v in range(min(u, U_FF))) + max(u - U_FF, 0)


def evacs_before(u):
    return sum((NT if is_natural(v) else 2) * (not is_filler(v)) for v in range(u))


def rows_of(t):
    return min(P, T - t * P)


def pieces(n):
    k = -(-n // 512)
    w = -(-n // k)
    return n, w + w % 2, k


def keys_of(i):
    return pieces(META if i == NT - 1 else META + P * (i + 1))


def mask_at(i):
    return sum(keys_of(j)[1] * keys_of(j)[2] for j in range(i))


def build(nc, x_all, cache_k, cache_v, cache_kidx, state, page_table, ln_p, w_stream, w_a2, b_a,
          gnorm, outs):
    (y_p, y_s, k_p, v_p, ki_p, st_p, k_s, v_s, ki_s, st_s) = outs
    top = ExitStack()
    with top:
        def alloc(stack, name, shape, dt=F32):
            return stack.enter_context(nc.sbuf_tensor(name, shape, dt))

        def sb(name, shape, dt=F32):
            return alloc(top, name, shape, dt)

        def region(*specs):
            with ExitStack() as st:
                return [alloc(st, *s) for s in specs]

        def sem(name):
            return top.enter_context(nc.semaphore(name))

        def dram(name, shape):
            return nc.dram_tensor(name, shape, F32).ap()

        h_d = dram("h_d", (T, D))
        qiT_d = dram("qiT_d", (IH * HD, T))
        qT_d = dram("qT_d", (2048, T))
        gvog_d = dram("gvog_d", (T, 2048))
        gate_d = dram("gate_d", (2048, T))
        part_d = dram("part_d", (D, T))
        o_d = dram("o_d", (T, D))
        a1_d = dram("a1_d", (RANK, T))
        wi_d = dram("wi_d", (IH, TS))
        vs_d = dram("vs_d", (TS, NKV * HD))
        att_d = dram("att_d", (TP, D))

        ps = top.enter_context(nc.psum_tensor("ps", [P, 8, 512], F32))
        flat = ps[:, :, :].rearrange("p b n -> p (b n)")

        ident = sb("ident", [P, P])
        identb = sb("identb", [P, P], BF16)
        raw = sb("raw", [P, 2, UNIT])
        w_hi = sb("w_hi", [P, 2, UNIT], F32R)
        w_lo = sb("w_lo", [P, 2, UNIT], F32R)
        xt_hi = sb("xt_hi", [P, KC, T], F32R)
        xt_lo = sb("xt_lo", [P, KC, T], F32R)
        small = sb("small", [P, 16])
        tri = sb("tri", [P, P])
        tri16 = sb("tri16", [P, META], BF16)
        causal = sb("causal", [P, CH])
        d8 = sb("d8", [TS, DB, DS])
        delta = sb("delta", [TS, DS])
        bsel = sb("bsel", [TS, DB])
        triS = sb("triS", [TS, DS])
        pt_sb = sb("pt_sb", [1, P], I32)
        m8 = sb("m8", [P, 8])
        mx = sb("mx", [P, 4])
        rsum = sb("rsum", [P, NH])
        ssq = sb("ssq", [P, 10, GH])
        pool_go = sb("pool_go", [P, 2])
        stats = sb("stats", [P, 2, 2, 6])
        mv = sb("mv", [P, 2, 2])

        h_sb, lg, lb = region(("h_sb", [P, NT, D]), ("lg", [P, D]), ("lb", [P, D]))
        with ExitStack() as att:
            kT3 = alloc(att, "kT3", [P, 4, T])
            winat = alloc(att, "winat", [P, NT, IH])
            IW = mask_at(8)
            with ExitStack() as b_st:
                stg = alloc(b_st, "stg", [P, 2, T])
                isc = alloc(b_st, "isc", [P, IW])
                iscS = alloc(b_st, "iscS", [TS, NK])
                kiS, qraw, qhi, qlo, relu = region(
                    ("kiS", [P, 1056], F32R), ("qraw", [P, 2, IH, P]), ("qhi", [P, IH, P], F32R),
                    ("qlo", [P, IH, P], F32R), ("relu", [P, 2, 1056]))
                kxT, relu2, ib, wb, _, qiS, wsel = region(
                    ("kxT", [HD, NK]), ("relu2", [HD, 2, 512]), ("ib", [DS, NK]), ("wb", [HD, DB, DS]),
                    ("beside_relu", [P, 2112]), ("qiS", [HD, DB, IH, DS]), ("wsel", [HD, DB]))
                kxraw = [stg[:, b, 0:NPG * HD].rearrange("p (g d) -> p g d", d=HD) for b in range(2)]
                maskS = alloc(b_st, "maskS", [TS, NK], BF16)
                kt, pS, qblk, esel, oS, attT = region(
                    ("kt", [P, 2, 2, 512]), ("pS", [P, NK]),
                    ("qblk", [P, 2, DB, P]), ("esel", [TS, DB, NH, DS], BF16),
                    ("oS", [P, 2, HD]), ("attT", [P, KC, TS]))
                masks = alloc(b_st, "masks", [P, IW], BF16)
                vnat = alloc(b_st, "vnat", [P, NT, NKV * HD])
                eqb, cut, bit, cand, low_m, take, cnt, need = region(
                    ("eqb", [P, NK], BF16), ("cut", [P, 8], I32), ("bit", [P, 8], I32), ("cand", [P, 8], I32),
                    ("low_m", [P, 8], I32), ("take", [P, 8], I32), ("cnt", [P, 8]), ("need", [P, 8]))
                attn, qraw2 = region(("attn", [P, D]), ("qraw2", [P, 2, G, P]))
            kS, pP, ptb = region(
                ("kS", [P, NKV, 1056], F32R), ("pP", [P, 2, 1056]), ("ptb", [P, 1536]))
            with ExitStack() as c_st:
                alloc(c_st, "kS_place", [P, NKV * 1056 + 2 * 1056 + 1536])
                qh2, ql2 = region(("qh2", [P, G, P], F32R), ("ql2", [P, G, P], F32R))
            kpg, vpg, vnew, ptS = region(
                ("kpg", [P, 3, 4, 256]), ("vpg", [P, 4, 4, 256]), ("vnew", [DS, 2, 256]),
                ("ptS", [P, 2, 512]))
        gq, gk, kd, zz, bb, a1T, reset, gv, gvs, s0, sx, kem, qdm, at, ken, wa2, ba, dec, bd64, ostg, gst = region(
            ("gq", [P, T]), ("gk", [P, T]), ("kd", [P, T]), ("zz", [P, T]), ("bb", [P, T]),
            ("a1T", [RANK, T]), ("reset", [P, T], BF16), ("gv", [P, NT, DV]), ("gvs", [TS, DV]),
            ("s0", [P, DB, DV]), ("sx", [P, 4, DV]), ("kem", [TS, DB, DK]), ("qdm", [P, 576]),
            ("at", [P, 2, CH]), ("ken", [P, 2, DK]), ("wa2", [RANK, 512]), ("ba", [P, GH]),
            ("dec", [P, 25]), ("bd64", [TS, CH]), ("ostg", [P, 2, DV]), ("gst", [P, 2, T]))
        oin, ogin, gnb = region(("oin", [P, 4, D]), ("ogin", [P, 4, D]), ("gnb", [P, DV]))
        gst2, pst2, merged = region(("gst2", [P, 2, T]), ("pst2", [P, 2, T]), ("merged", [P, KC, T]))
        res = sb("res", [P, NT, D])
        lg2, lb2 = sb("lg2", [P, D]), sb("lb2", [P, D])
        a_hi, a_lo, rl = region(
            ("a_hi", [P, 2, 2, T], F32R), ("a_lo", [P, 2, 2, T], F32R), ("rl", [P, 2, T]))

        kraw = isc[:, mask_at(7):mask_at(7) + TP]
        knat = [isc[:, mask_at(6) + 384 * s:mask_at(6) + 384 * s + 384] for s in range(2)]

        raw_in = [sem("raw_in0"), sem("raw_in1")]
        w_split = sem("w_split")
        half_done, unit_done = sem("half_done"), sem("unit_done")
        evac = sem("evac")
        stage = sem("stage")
        consts = sem("consts")
        ln_in = sem("ln_in")
        x_in = [sem(f"x_in{i}") for i in range(5)]
        n_var, n_std, n_shift, n_z, n_g, n_h = (
            sem(n) for n in ("n_var", "n_std", "n_shift", "n_z", "n_g", "n_h"))
        h_out = sem("h_out")
        tr_ok, hi_ok, lo_ok = sem("tr_ok"), sem("hi_ok"), sem("lo_ok")
        st_out = [sem("st_out0"), sem("st_out1")]
        fill_mm, fill_ev = sem("fill_mm"), sem("fill_ev")
        fst_out = [sem(f"fst_out{i}") for i in range(3)]
        att_out = [sem("att_out0"), sem("att_out1")]
        al_in = [sem("al_in0"), sem("al_in1")]
        g_sig = sem("g_sig")
        kn_tr, kn_ok = sem("kn_tr"), sem("kn_ok")
        kn_out = [sem("kn_out0"), sem("kn_out1")]
        ks_in, ks_hi, ks_ok = sem("ks_in"), sem("ks_hi"), sem("ks_ok")
        q_in = [sem("q_in0"), sem("q_in1")]
        q_hi_ok, q_lo_ok = sem("q_hi_ok"), sem("q_lo_ok")
        ix_mm, ix_relu, ix_acc = sem("ix_mm"), sem("ix_relu"), sem("ix_acc")
        sx_in, wb_ok = sem("sx_in"), sem("wb_ok")
        kx_in = [sem("kx_in0"), sem("kx_in1")]
        kx_tr, kx_ev, s_mm, s_relu, i_mm, i_ev, ib_out = (
            sem(n) for n in ("kx_tr", "kx_ev", "s_mm", "s_relu", "i_mm", "i_ev", "ib_out"))
        misc_out = sem("misc_out")
        c_ks_hi, c_ks_ok = sem("c_ks_hi"), sem("c_ks_ok")
        c_ks_in = [sem("c_ks_in0"), sem("c_ks_in1")]
        cq_in = [sem("cq_in0"), sem("cq_in1")]
        cq_hi, cq_lo = sem("cq_hi"), sem("cq_lo")
        qk_ok, mx_ok, exp_ok = sem("qk_ok"), sem("mx_ok"), sem("exp_ok")
        fill_at = kT3[:, 2, :].rearrange("p (s n) -> p s n", s=3)

        def probs_t(hh, j):
            if j == 2:
                return ptb[:, 1024 + P * (hh % 2):1024 + P * (hh % 2) + P]
            return kT3[:, 3, 512 * j:512 * j + 512] if hh % 2 else ptb[:, 512 * j:512 * j + 512]

        pt_tr, pt_a, pt_v, pv_ok, o_ev, att_tr = (
            sem(n) for n in ("pt_tr", "pt_a", "pt_v", "pv_ok", "o_ev", "att_tr"))
        d_set, d_cst = sem("d_set"), sem("d_cst")
        kg_in = [sem(f"kg_in{i}") for i in range(3)]
        vg_in = [sem(f"vg_in{i}") for i in range(4)]
        vn_in = [sem("vn_in0"), sem("vn_in1")]
        kt_tr, kt_a, kt_v, kt_qk = sem("kt_tr"), sem("kt_a"), sem("kt_v"), sem("kt_qk")
        d_qk, d_mx, d_exp, d_p, d_ptr, d_pa, d_pv, d_o, d_oev = (
            sem(n) for n in ("d_qk", "d_mx", "d_exp", "d_p", "d_ptr", "d_pa", "d_pv", "d_o", "d_oev"))
        d_oc, d_ot = sem("d_oc"), sem("d_ot")
        g_in = [sem("g_in0"), sem("g_in1")]
        s_done = sem("s_done")
        ga_set, ga_in, ga_z, ga_step, ga_e, ga_ready = (
            sem(n) for n in ("ga_set", "ga_in", "ga_z", "ga_step", "ga_e", "ga_ready"))
        ga_lg, ga_at, ga_am, ga_kn, ga_u, ga_s, ga_o, ga_oe, ga_head = (
            sem(n) for n in ("ga_lg", "ga_at", "ga_am", "ga_kn", "ga_u", "ga_s", "ga_o", "ga_oe", "ga_head"))
        ga_so, ga_q = sem("ga_so"), sem("ga_q")
        pa_mm, pa_ev, pa_out = sem("pa_mm"), sem("pa_ev"), sem("pa_out")
        ga_oo = [sem("ga_oo0"), sem("ga_oo1")]
        po_in = [sem(f"po_in{i}") for i in range(4)]
        po_set, po_v, po_sd, po_sl, po_ok, po_tr, po_hi, po_lo = (
            sem(n) for n in ("po_set", "po_v", "po_sd", "po_sl", "po_ok", "po_tr", "po_hi", "po_lo"))
        mg_hi, mg_lo, res_in = sem("mg_hi"), sem("mg_lo"), sem("res_in")
        l_tr, l_hi, l_lo = sem("l_tr"), sem("l_hi"), sem("l_lo")
        ln2_in = sem("ln2_in")
        f_relu, f_sq, f_hi, f_lo, f_half, f_add = (
            sem(n) for n in ("f_relu", "f_sq", "f_hi", "f_lo", "f_half", "f_add"))

        def barrier(eng, n):
            eng.drain().then_inc(stage, 1)
            eng.wait_ge(stage, 4 * n)

        OT = [(i, P * i, P) for i in range(8)] + [(8, SEQ, META), (9, TP, TS)]

        def load_pages(eng, dst, cache, b, grp, done):
            for j in range(4):
                at0 = NPG * b + 4 * grp + j
                page = eng.value_load(pt_sb[0:1, at0:at0 + 1], min_val=0, max_val=159)
                eng.dma_start(dst[:, j, :], cache[bass.ds(page, 1), :, :].rearrange(
                    "a p d -> (a p) d")).then_inc(done, 16)

        block = top.enter_context(nc.Block())

        @block.gpsimd
        def _(pool):
            for tile, v in ((ident[:, :], 0.0), (identb[:, :], 0.0), (tri[:, :], 0.0), (tri16[:, :], 0.0),
                            (causal[:, :], 1.0), (d8[:, :, :], 0.0), (pool_go[:, :], 0.0)):
                pool.memset(tile, v)
            pool.drain()
            selects = [
                (ident[:, :], ALU.not_equal, 1.0, [[-1, P]], 1),
                (identb[:, :], ALU.not_equal, 1.0, [[-1, P]], 1),
                (tri[:, :], ALU.is_ge, NEG, [[-1, P]], 1),
                (tri16[:, :], ALU.is_ge, NEG, [[-1, META]], 1),
                (causal[0:CH, :], ALU.is_ge, 0.0, [[1, CH]], -1),
                (causal[CH:P, :], ALU.is_ge, 0.0, [[1, CH]], -1),
                (d8[:, :, :], ALU.not_equal, 1.0, [[-DS, DB], [-1, DS]], 1)]
            for n, (tile, compare, fill, pattern, mult) in enumerate(selects):
                if n:
                    pool.wait_ge(consts, n)
                pool.affine_select(out=tile, in_=tile, compare_op=compare, fill=fill, base=0,
                                   pattern=pattern, channel_multiplier=mult).then_inc(consts, 1)
            pool.wait_ge(consts, 7)

            def split(s, landed, used):
                pool.wait_ge(raw_in[s], landed)
                if used is not None:
                    pool.wait_ge(unit_done, used)
                pool.tensor_tensor(pool_go[:, 0:1], pool_go[:, 1:2], pool_go[:, 1:2], ALU.mult)
                pool.tensor_copy(w_hi[:, s, :], raw[:, s, :])
                pool.drain()
                pool.tensor_tensor(w_lo[:, s, :], raw[:, s, :], w_hi[:, s, :].bitcast(F32),
                                   ALU.subtract).then_inc(w_split, 1)

            def shift(which, x, b, tiles):
                for t in tiles:
                    r = rows_of(t)
                    pool.wait_ge(n_g, NT * which + t + 1)
                    pool.tensor_tensor(x[:r, t, :], x[:r, t, :], b[:r, :], ALU.add).then_inc(n_h, 1)

            def split_units(u0, u1):
                with pool.Fori(u0 // 2, u1 // 2) as i:
                    for s in range(2):
                        split(s, 16 * i + 16, 2 * i + s - 1)

            shift(0, h_sb, lb, range(4))
            split(0, 16, None)
            shift(0, h_sb, lb, range(4, NT))
            pool.wait_ge(n_h, NT)
            split(1, 16, None)
            split_units(2, U_FF - 1)
            for u in (U_FF - 1, U_FF):
                split(u % 2, 16 * (u // 2) + 16, u - 1)
            pool.wait_ge(w_split, U_FF + 1)
            shift(1, res, lb2, range(NT))
            pool.wait_ge(n_h, 2 * NT)
            for u in (U_FF + 1, U_FF + 2):
                split(u % 2, 16 * (u // 2) + 16, u - 1)
            split_units(U_FF + 3, N_UNITS - 1)
            split(0, 16 * (N_UNITS // 2) + 16, N_UNITS - 2)
            pool.wait_ge(w_split, N_UNITS)
            shift(2, res, lb2, range(NT))

        @block.sync
        def _(sp):
            def load_unit(u, s, landed_before=None):
                if landed_before is not None:
                    sp.wait_ge(w_split, landed_before)
                src = w_stream[u, :, :] if isinstance(u, int) else \
                    w_stream[bass.ds(u, 1), :, :].rearrange("u p n -> (u p) n")
                sp.dma_start(raw[:, s, :], src).then_inc(raw_in[s], 16)

            def load_units(u0, u1):
                for u in range(u0, u1):
                    load_unit(u, u % 2, u - 1 if u >= 2 else None)

            def load_x(t0, t1, n):
                sp.dma_start(h_sb[:, t0:t1, :], x_all[P * t0:P * t1, :].rearrange("(t p) c -> p t c", p=P)).then_inc(x_in[n], 16)

            load_x(0, 1, 0)
            load_x(1, 2, 1)
            sp.dma_start(lg[:, :], ln_p[0:1, :].broadcast_to((P, D))).then_inc(ln_in, 16)
            sp.dma_start(lb[:, :], ln_p[1:2, :].broadcast_to((P, D))).then_inc(ln_in, 16)
            sp.dma_start(pt_sb[:, :], page_table).then_inc(ln_in, 16)
            load_x(2, 5, 2)
            load_units(0, 1)
            load_x(5, 8, 3)
            sp.dma_start(h_sb[0:80, 8, :], x_all[SEQ:T, :]).then_inc(x_in[4], 16)
            load_units(1, 2)
            for t in range(NT):
                r = rows_of(t)
                sp.wait_ge(n_h, t + 1)
                sp.dma_start(h_d[P * t:P * t + r, :], h_sb[:r, t, :]).then_inc(h_out, 16)
            sp.wait_ge(h_out, 16 * NT)
            sp.wait_ge(ln_in, 48)
            load_units(2, 4)
            barrier(sp, 1)

            def dup_keys(dst, src_rows, done):
                for half in range(2):
                    d = dst[HD * half:HD * half + HD, :]
                    sp.dma_start(d[:, 0:META], src_rows[:, SEQ:TP]).then_inc(done, 16)
                    sp.dma_start(d[:, META:TP], src_rows[:, 0:SEQ]).then_inc(done, 16)

            sp.wait_ge(evac, 4)
            dup_keys(kraw, kT3[0:HD, 2, :], ks_in)
            sp.dma_start(a1_d, kT3[:RANK, 3, :]).then_inc(misc_out, 16)
            sp.dma_start(wi_d, kT3[HD:HD + IH, 2, TP:T]).then_inc(misc_out, 16)

            def load_qi(i):
                for half in range(2):
                    sp.dma_start(qraw[HD * half:HD * half + HD, i % 2, :, :],
                                 qiT_d.rearrange("(h d) t -> d h t", d=HD)[:, :, P * i:P * i + P]).then_inc(q_in[i % 2], 16)

            sp.wait_ge(st_out[0], 32)
            sp.wait_ge(st_out[1], 32)
            load_qi(1)
            load_qi(2)
            for t in range(NT):
                sp.wait_ge(kn_ok, t + 1)
                src, s = knat[t % 2], kn_out[t % 2]
                if t < 8:
                    at0 = META + P * t
                    sp.dma_start(k_p[at0:at0 + P, :], src[:, 0:256]).then_inc(s, 16)
                    sp.dma_start(ki_p[at0:at0 + P, :], src[:, 256:320]).then_inc(s, 16)
                else:
                    sp.dma_start(k_p[0:META, :], src[0:META, 0:256]).then_inc(s, 16)
                    sp.dma_start(ki_p[0:META, :], src[0:META, 256:320]).then_inc(s, 16)
                    sp.dma_start(k_s, src[META:80, 0:256]).then_inc(s, 16)
                    sp.dma_start(ki_s, src[META:80, 256:320]).then_inc(s, 16)
            for i in range(3, 8):
                sp.wait_ge(q_lo_ok, i - 2)
                load_qi(i)
            sp.wait_ge(kn_out[0], 32 * 4 + 64)
            sp.wait_ge(kn_out[1], 32 * 4)

            load_units(4, 6)

            def load_kx(b):
                for pg in range(NPG):
                    page = sp.value_load(pt_sb[0:1, NPG * b + pg:NPG * b + pg + 1], min_val=0, max_val=159)
                    sp.dma_start(kxraw[b % 2][:, pg, :], cache_kidx[bass.ds(page, 1), :, :].rearrange(
                        "a p d -> (a p) d")).then_inc(kx_in[b % 2], 16)

            sp.wait_ge(misc_out, 32)
            for h in range(IH):
                sp.dma_start(qiS[:, :, h, :], qiT_d[HD * h:HD * h + HD, TP:T].rearrange(
                    "d (b t) -> d b t", t=DS)).then_inc(sx_in, 16)
                sp.dma_start(wsel[DS * h:DS * h + DS, :], wi_d[h, :].rearrange(
                    "(b t) -> t b", t=DS), allow_slow_non_contiguous=True).then_inc(sx_in, 16)
            load_kx(0)
            load_kx(1)
            barrier(sp, 2)
            for b in range(1, DB):
                if b >= 2:
                    sp.wait_ge(kx_tr, 4 * (b - 1))
                    load_kx(b)
                sp.wait_ge(i_ev, 5 * b)
                sp.dma_start(iscS[DS * (b - 1):DS * b, :], ib[:, :]).then_inc(ib_out, 16)
            sp.wait_ge(i_ev, 5 * DB)
            sp.dma_start(iscS[DS * (DB - 1):DS * DB, :], ib[:, :]).then_inc(ib_out, 16)
            barrier(sp, 3)

            load_units(6, 12)
            load_units(12, 17)
            sp.wait_ge(evac, evacs_before(U_N + 1))
            sp.dma_start(v_p[META:TP, :].rearrange("(t p) c -> p t c", p=P), vnat[:, 0:8, :]).then_inc(misc_out, 16)
            sp.dma_start(v_p[0:META, :], vnat[0:META, 8, :]).then_inc(misc_out, 16)
            sp.dma_start(v_s, vnat[META:80, 8, :]).then_inc(misc_out, 16)
            sp.dma_start(vs_d, vnat[META:80, 8, :]).then_inc(misc_out, 16)
            load_units(17, U_N + 4 + F_EARLY // NT)
            barrier(sp, 4)

            for n in range(NKV):
                if n >= 2:
                    sp.wait_ge(c_ks_ok, n - 1)
                dup_keys(pP[:, n % 2, :], kT3[HD * (n % 2):HD * (n % 2) + HD, n // 2, :], c_ks_in[n % 2])
            q_v = qT_d[0:1024, :].rearrange("(h d) t -> d h t", d=HD)
            u = U_N + 4 + F_EARLY // NT

            def store_half(hh):
                i, half = hh // NH, hh % NH // 8
                r = P if i < 8 else META
                at0 = P * i
                sp.wait_ge(o_ev, hh + 1)
                sp.dma_start(att_d[at0:at0 + r, 512 * half:512 * half + 512],
                             attn[:r, 512 * half:512 * half + 512]).then_inc(att_out[half], 16)

            for i in range(NT):
                r = rows_of(i)
                for n in range(NKV):
                    j = NKV * i + n
                    if j >= 2:
                        sp.wait_ge(cq_lo, j - 1)
                    for half in range(2):
                        sp.dma_start(qraw2[HD * half:HD * half + HD, j % 2, :, :r],
                                     q_v[:, G * n:G * n + G, P * i:P * i + r]).then_inc(cq_in[j % 2], 16)
                    if j >= 3 and j % 2:
                        store_half(4 * (j - 1) - 1)
                    while u < U_PA + 3 and fill_unit_start(u - 3) < fills_by(4 * (j - 1)):
                        load_unit(u, u % 2, u - 1)
                        u += 1
            store_half(NH * NT - 1)
            load_units(u, U_PA + 3)
            for half in range(2):
                sp.wait_ge(att_out[half], 16 * NT)
            barrier(sp, 5)

            def load_att(i):
                r = P if i < 8 else META
                sp.dma_start(kT3[:r, 2 + i % 2, 0:D], att_d[P * i:P * i + r, :]).then_inc(al_in[i % 2], 16)

            def load_k(gg):
                if gg >= 3:
                    sp.wait_ge(kt_tr, gg - 2)
                load_pages(sp, kpg[:, gg % 3, :, :], cache_k, gg // 4, gg % 4, kg_in[gg % 3])

            for gg in range(3):
                load_k(gg)
            sp.wait_ge(d_set, 1)
            sp.wait_ge(misc_out, 16 * 6)
            for j in range(2):
                for n2 in range(2):
                    for g in range(G):
                        head = G * (2 * j + n2) + g
                        sp.dma_start(
                            qblk[HD * n2:HD * n2 + HD, j, :, DS * head:DS * head + DS],
                            qT_d[HD * head:HD * head + HD, TP:T].rearrange("d (b t) -> d b t", t=DS)
                        ).then_inc(d_cst, 16)
            load_att(0)
            load_att(1)
            load_unit(U_PA + 3, (U_PA + 3) % 2, U_PA + 2)
            for b in range(DB):
                load_k(4 * b + 3)
                if b >= 1 and b + 1 < NT:
                    sp.wait_ge(att_tr, b)
                    load_att(b + 1)
                if b + 1 < DB:
                    load_k(4 * b + 4)
                if b >= 2:
                    sp.wait_ge(d_o, b - 1)
                sp.dma_start(vnew[:, b % 2, :], vs_d[DS * b:DS * b + DS, :]).then_inc(vn_in[b % 2], 16)
                for grp in range(2, 4):
                    if b >= 1:
                        sp.wait_ge(s_done, 4 * (b - 1) + grp + 1)
                    load_pages(sp, vpg[:, grp, :, :], cache_v, b, grp, vg_in[grp])
                if b + 1 < DB:
                    load_k(4 * b + 5)
                    load_k(4 * b + 6)
            barrier(sp, 6)

            def load_gates(dst, first, src2, dst2, base):
                for m in range(KC):
                    if m >= 2:
                        sp.wait_ge(evac, evacs_before(base) + m - 1)
                    sp.dma_start(dst[:, m % 2, :], gate_d[first + P * m:first + P * m + P, :]).then_inc(g_in[m % 2], 16)
                    sp.dma_start(dst2[:, m % 2, :], src2[P * m:P * m + P, :]).then_inc(g_in[m % 2], 16)
                    if m % 2 == 1:
                        load_units(base + 4 + m // 2, base + 5 + m // 2)

            def load_head_gates(h):
                for c in range(2):
                    at0 = P * (2 * h + c)
                    sp.dma_start(gst[:, c, :], gate_d[at0:at0 + P, :]).then_inc(g_in[c], 16)

            load_head_gates(0)
            sp.dma_start(a1T[:, :], a1_d).then_inc(ga_set, 16)
            sp.dma_start(wa2[:, :], w_a2).then_inc(ga_set, 16)
            sp.dma_start(ba[:, :], b_a.rearrange("(h p) -> p h", p=P), allow_slow_non_contiguous=True).then_inc(ga_set, 16)
            for h in range(GH):
                if h:
                    sp.wait_ge(ga_head, h)
                    sp.wait_ge(ga_so, 32 * h)
                sp.dma_start(gq[:, :], qT_d[1024 + DK * h:1024 + DK * h + DK, :]).then_inc(ga_in, 16)
                sp.dma_start(gk[:, :], qT_d[1536 + DK * h:1536 + DK * h + DK, :]).then_inc(ga_in, 16)
                cols = gvog_d[:, DV * h:DV * h + DV]
                sp.dma_start(gv[:, 0:8, :], cols[0:SEQ, :].rearrange("(t p) c -> p t c", p=P)).then_inc(ga_in, 16)
                sp.dma_start(gv[0:META, 8, :], cols[SEQ:TP, :]).then_inc(ga_in, 16)
                sp.dma_start(gvs[:, :], cols[TP:T, :]).then_inc(ga_in, 16)
                sp.dma_start(s0[:, :, :], state[:, h, :, :].rearrange("b p v -> p b v")).then_inc(ga_in, 16)
                for n, (i, at0, r) in enumerate([OT[8]] + OT[:8] + [OT[9]]):
                    e = 10 * h + n
                    sp.wait_ge(ga_oe, e + 1)
                    sp.dma_start(o_d[at0:at0 + r, DV * h:DV * h + DV], ostg[:r, e % 2, :]).then_inc(ga_oo[e % 2], 16)
                    if n == 0:
                        sp.wait_ge(pa_ev, 6 * (h + 1))
                        for c in range(2):
                            at0 = P * (2 * h + c)
                            sp.dma_start(part_d[at0:at0 + P, :], gst[:, c, :]).then_inc(pa_out, 16)
                        load_unit(U_PG + h, (U_PG + h) % 2, U_PG + h - 1)
                    if n == 3 and h + 1 < GH:
                        sp.wait_ge(pa_out, 32 * (h + 1))
                        load_head_gates(h + 1)
                sp.wait_ge(ga_s, 26 * (h + 1))
                sp.dma_start(st_p[h, :, :], sx[:, 0, :]).then_inc(ga_so, 16)
                sp.dma_start(st_s[:, h, :, :].rearrange("b p v -> p b v"), s0[:, :, :]).then_inc(ga_so, 16)
            sp.wait_ge(ga_so, 32 * GH)
            sp.wait_ge(pa_out, 32 * GH)
            sp.wait_ge(ga_oo[0], 16 * 20)
            sp.wait_ge(ga_oo[1], 16 * 20)
            barrier(sp, 7)

            sp.dma_start(gnb[:, :], gnorm.broadcast_to((P, DV))).then_inc(po_set, 16)
            for n, (i, at0, r) in enumerate(OT):
                if n >= 4:
                    sp.wait_ge(po_tr, n - 3)
                sp.dma_start(oin[:r, n % 4, :], o_d[at0:at0 + r, :]).then_inc(po_in[n % 4], 16)
                sp.dma_start(ogin[:r, n % 4, :], gvog_d[at0:at0 + r, 1024:2048]).then_inc(po_in[n % 4], 16)
            barrier(sp, 8)
            load_gates(gst2, 1024, part_d, pst2, base=U_PG)
            barrier(sp, 9)

            sp.wait_ge(mg_lo, KC)
            sp.dma_start(res[:, 0:8, :], h_d[0:SEQ, :].rearrange("(t p) c -> p t c", p=P)).then_inc(res_in, 16)
            sp.dma_start(res[0:80, 8, :], h_d[SEQ:T, :]).then_inc(res_in, 16)
            sp.dma_start(lg2[:, :], ln_p[2:3, :].broadcast_to((P, D))).then_inc(ln2_in, 16)
            sp.dma_start(lb2[:, :], ln_p[3:4, :].broadcast_to((P, D))).then_inc(ln2_in, 16)
            load_units(41, 45)
            barrier(sp, 10)
            sp.dma_start(lg2[:, :], ln_p[4:5, :].broadcast_to((P, D))).then_inc(ln2_in, 16)
            sp.dma_start(lb2[:, :], ln_p[5:6, :].broadcast_to((P, D))).then_inc(ln2_in, 16)
            with sp.Fori(0, (N_UNITS - 45) // 2) as i:
                for s in range(2):
                    load_unit(2 * i + 45 + s, 1 - s, 2 * i + 44 + s)
            for t in range(NT):
                sp.wait_ge(n_h, 2 * NT + t + 1)
                if t < 8:
                    sp.dma_start(y_p[P * t:P * t + P, :], res[:, t, :]).then_inc(misc_out, 16)
                else:
                    sp.dma_start(y_s, res[META:80, t, :]).then_inc(misc_out, 16)
            sp.wait_ge(misc_out, 16 * (6 + 9))

        @block.tensor
        def _(pe):
            def unit_f(s, ready, free):
                pe.wait_ge(w_split, ready)
                for c in range(2):
                    if free[c] is not None:
                        pe.wait_ge(evac, free[c])
                    for n in range(3):
                        out = ps[:, 3 * c + n, 0:N3]
                        cols = slice(N3 * n, N3 * n + N3)
                        for k in range(KC):
                            at0 = (KC * c + k) * P
                            hi, lo = w_hi[:, s, at0:at0 + P], w_lo[:, s, at0:at0 + P]
                            pe.matmul(out, hi, xt_hi[:, k, cols], start=k == 0, stop=False)
                            pe.matmul(out, hi, xt_lo[:, k, cols], start=False, stop=False)
                            last = pe.matmul(out, lo, xt_hi[:, k, cols], start=False, stop=k == KC - 1)
                    last.then_inc(unit_done if c else half_done, 1)

            def unit_n(s, ready, free, wait=None):
                pe.wait_ge(w_split, ready)
                for t in range(NT):
                    pe.wait_ge(evac, free + t)
                    r = rows_of(t)
                    out = ps[:r, t % 3, 0:256]
                    cols = slice(P * t, P * t + r)
                    for k in range(KC):
                        w = slice(256 * k, 256 * k + 256)
                        pe.matmul(out, xt_hi[:, k, cols], w_hi[:, s, w], start=k == 0, stop=False)
                        pe.matmul(out, xt_lo[:, k, cols], w_hi[:, s, w], start=False, stop=False)
                        last = pe.matmul(out, xt_hi[:, k, cols], w_lo[:, s, w], start=False, stop=k == KC - 1)
                    last.then_inc(unit_done if t == NT - 1 else half_done, 1)

            def transpose_tile(src, r, bank, done):
                for k in range(KC):
                    last = pe.transpose(flat[:, 512 * bank + P * k:512 * bank + P * k + r],
                                        src[:r, P * k:P * k + P], ident[:r, :r])
                last.then_inc(done, 1)

            pe.wait_ge(consts, 7)
            for t in range(NT):
                pe.wait_ge(n_h, t + 1)
                if t >= 4:
                    pe.wait_ge(lo_ok, t - 3)
                transpose_tile(h_sb[:, t, :], rows_of(t), 2 * (t % 4), tr_ok)
            pe.wait_ge(lo_ok, NT)
            barrier(pe, 1)

            for u in range(4):
                unit_f(u % 2, u + 1, [2 * u + c - 1 if 2 * u + c >= 2 else None for c in range(2)])
            for t in range(NT):
                r = rows_of(t)
                if t >= 2:
                    pe.wait_ge(kn_ok, t - 1)
                for c in range(3):
                    last = pe.transpose(ps[:r, 6 + t % 2, P * c:P * c + P], kT3[:, c, P * t:P * t + r], ident[:, :])
                last.then_inc(kn_tr, 1)

            pe.wait_ge(ks_ok, 1)
            pe.wait_ge(kn_ok, NT)
            pe.wait_ge(evac, 8)
            for i in range(1, 8):
                _, w, np_ = keys_of(i)
                pe.wait_ge(q_lo_ok, i)
                for h in range(IH):
                    g = IH * (i - 1) + h
                    if g >= 2:
                        pe.wait_ge(ix_relu, g - 1)
                    for p in range(np_):
                        out, keys = ps[:, 4 * (g % 2) + p, 0:w], kiS[:, w * p:w * p + w]
                        pe.matmul(out, qhi[:, h, :], keys, start=True, stop=False)
                        last = pe.matmul(out, qlo[:, h, :], keys, start=False, stop=True)
                    last.then_inc(ix_mm, 1)
            barrier(pe, 2)

            pe.wait_ge(sx_in, 16 * 16)
            pe.wait_ge(wb_ok, 1)
            width = [512] * 4 + [DS]
            for b in range(DB):
                def tr(grp):
                    gg = 4 * b + grp
                    if gg >= 2:
                        pe.wait_ge(kx_ev, 5 * ((gg - 2) // 4) + 2 + (gg - 2) % 4)
                    for j in range(4):
                        last = pe.transpose(ps[0:HD, gg % 2, P * j:P * j + P], kxraw[b % 2][:, 4 * grp + j, :], ident[:, :])
                    last.then_inc(kx_tr, 1)

                def sc(p):
                    q = 5 * b + p
                    pe.wait_ge(kx_ev, 5 * b + min(2 + p, 5))
                    if q >= 2:
                        pe.wait_ge(s_relu, q - 1)
                    pe.matmul(ps[0:HD, 2 + q % 2, 0:width[p]], qiS[:, b, :, :].rearrange("p h t -> p (h t)"),
                              kxT[:, 512 * p:512 * p + width[p]], start=True, stop=True).then_inc(s_mm, 1)

                def ws(p):
                    q = 5 * b + p
                    pe.wait_ge(s_relu, q + 1)
                    if q >= 2:
                        pe.wait_ge(i_ev, q - 1)
                    pe.matmul(ps[0:DS, 4 + q % 2, 0:width[p]], wb[:, b, :], relu2[:, q % 2, 0:width[p]],
                              start=True, stop=True).then_inc(i_mm, 1)

                pe.wait_ge(kx_in[b % 2], 256 * (b // 2 + 1))
                tr(0); tr(1); sc(0); tr(2); sc(1); ws(0); tr(3)
                sc(2); ws(1); sc(3); ws(2); sc(4); ws(3); ws(4)
            barrier(pe, 3)

            with pe.Fori(0, 4) as i:
                for s in range(2):
                    e0 = evacs_before(U_Q) + 2 * s
                    unit_f(s, 2 * i + (U_Q + s + 1), [4 * i + (e0 + c - 1) for c in range(2)])
            pe.wait_ge(evac, evacs_before(U_N))
            unit_n(0, U_N + 1, evacs_before(U_N) - 2)
            pe.wait_ge(evac, evacs_before(U_N + 1))

            def fill(f):
                u, m, last_one = fill_unit(f)
                s = u % 2
                if m == 0:
                    pe.wait_ge(w_split, u + 1)
                ahead = f < F_EARLY
                bank = 6 + f % 2 if ahead else 7
                if f - ahead > 0:
                    pe.wait_ge(fill_ev, f - ahead)
                if f < 8 * NT:
                    r = rows_of(m)
                    out, cols = ps[:r, bank, 0:256], slice(P * m, P * m + r)
                    for k in range(KC):
                        w = slice(256 * k, 256 * k + 256)
                        pe.matmul(out, xt_hi[:, k, cols], w_hi[:, s, w], start=k == 0, stop=False)
                        pe.matmul(out, xt_lo[:, k, cols], w_hi[:, s, w], start=False, stop=False)
                        last = pe.matmul(out, xt_hi[:, k, cols], w_lo[:, s, w], start=False, stop=k == KC - 1)
                else:
                    out, cols = ps[:, bank, 0:N3], slice(N3 * (m % 3), N3 * (m % 3) + N3)
                    for k in range(KC):
                        at0 = (KC * (m // 3) + k) * P
                        hi, lo = w_hi[:, s, at0:at0 + P], w_lo[:, s, at0:at0 + P]
                        pe.matmul(out, hi, xt_hi[:, k, cols], start=k == 0, stop=False)
                        pe.matmul(out, hi, xt_lo[:, k, cols], start=False, stop=False)
                        last = pe.matmul(out, lo, xt_hi[:, k, cols], start=False, stop=k == KC - 1)
                last.then_inc(unit_done if last_one else fill_mm, 1)

            for f in range(F_EARLY):
                fill(f)
            barrier(pe, 4)

            def qk(hh):
                i, n, g = hh // NH, hh % NH // G, hh % G
                r = rows_of(i)
                L, w, np_ = keys_of(i)
                if g == 0:
                    pe.wait_ge(cq_lo, hh // G + 1)
                free = hh if i == 7 or (i == 8 and hh % NH < 2) else hh - 1
                if free > 0:
                    pe.wait_ge(mx_ok, free)
                bank = 0 if np_ == 3 else 2 * (hh % 2)
                for p in range(np_):
                    out, keys = ps[:r, bank + p, 0:w], kS[:, n, w * p:w * p + w]
                    pe.matmul(out, qh2[:, g, :r], keys, start=True, stop=False)
                    last = pe.matmul(out, ql2[:, g, :r], keys, start=False, stop=True)
                last.then_inc(qk_ok, 1)

            def chunks_of(i):
                return [(0, META)] + ([(META + P * j, P) for j in range(i + 1)] if i < 8 else [])

            def tr(hh, j):
                i = hh // NH
                r = rows_of(i)
                if j == 0:
                    pe.wait_ge(exp_ok, hh + 1)
                before = batches_before(hh, j % 2) + j // 2
                if before:
                    pe.wait_ge(pt_a if j == 1 else pt_v, before)
                for m, (at0, wid) in enumerate(chunks_of(i)[4 * j:4 * j + 4]):
                    last = pe.transpose(ps[:wid, 4 + j % 2, P * m:P * m + r], pP[:r, hh % 2, at0:at0 + wid], ident[:r, :r])
                last.then_inc(pt_tr, 1)

            def av(hh, j):
                i, n = hh // NH, hh % NH // G
                r = rows_of(i)
                chunks = chunks_of(i)
                pe.wait_ge(pt_a if j == 1 else pt_v, batches_before(hh, j % 2) + (2 if j == 2 else 1))
                if j == 0 and hh:
                    pe.wait_ge(o_ev, hh)
                for m, (at0, wid) in enumerate(chunks[4 * j:4 * j + 4]):
                    vt = 8 if at0 == 0 else (at0 - META) // P
                    last = pe.matmul(ps[:r, 6, 0:HD], probs_t(hh, j)[:wid, P * m:P * m + r],
                                     vnat[:wid, vt, HD * n:HD * n + HD],
                                     start=at0 == 0, stop=at0 == chunks[-1][0])
                last.then_inc(pv_ok, 1)

            for f in range(F_EARLY, F_START):
                fill(f)
            pe.wait_ge(c_ks_ok, NKV)
            f = F_START
            qk(0)
            qk(1)
            for hh in range(NH * NT):
                nb = batches_of(hh // NH)
                for j in range(min(nb, 2)):
                    tr(hh, j)
                if hh + 2 < NH * NT:
                    qk(hh + 2)
                if f < fills_by(hh):
                    fill(f)
                    f += 1
                if nb == 3:
                    tr(hh, 2)
                for j in range(batches_of((hh - 1) // NH) if hh else 0):
                    av(hh - 1, j)
            av(NH * NT - 1, 0)
            barrier(pe, 5)

            def att_tile(i):
                pe.wait_ge(al_in[i % 2], 16 * (i // 2 + 1))
                transpose_tile(kT3[:, 2 + i % 2, 0:D], P if i < 8 else META, 5, att_tr)

            def ktr(gg):
                pe.wait_ge(kg_in[gg % 3], 64 * (gg // 3 + 1))
                if gg:
                    pe.wait_ge(kt_a, gg)
                    pe.wait_ge(kt_v, gg)
                for j in range(2):
                    for m in range(4):
                        last = pe.transpose(ps[:, 5 + j, P * m:P * m + P], kpg[:, gg % 3, m, P * j:P * j + P], ident[:, :])
                last.then_inc(kt_tr, 1)

            def o_transposed(b):
                pe.wait_ge(d_oc, b + 1)
                pe.transpose(ps[:, 4, 256:256 + P], oS[:, :, :].rearrange("p a d -> p (a d)"), ident[:, :]).then_inc(d_ot, 1)

            ktr(0)
            ktr(1)
            pe.wait_ge(d_cst, 16 * 16)
            pe.wait_ge(d_set, 2)
            for b in range(DB):
                def scores(p, keys, wid):
                    out = ps[:, p, 0:wid]
                    for j in range(2):
                        pe.matmul(out, qblk[:, j, b, :], keys(j), start=j == 0, stop=False)
                    return pe.matmul(out, esel[:, b, :, :].rearrange("p h t -> p (h t)"),
                                     maskS[:, 512 * p:512 * p + wid], start=False, stop=True)

                if b:
                    pe.wait_ge(d_exp, b)
                for grp in range(4):
                    gg = 4 * b + grp
                    pe.wait_ge(kt_a, gg + 1)
                    pe.wait_ge(kt_v, gg + 1)
                    scores(grp, lambda j: kt[:, gg % 2, j, :], 512).then_inc(kt_qk, 1)
                    if grp == 0 and b:
                        o_transposed(b - 1)
                        pe.wait_ge(d_pa, 2 * b)
                        pe.wait_ge(d_pv, 3 * b)
                    if grp < 2:
                        ktr(gg + 2)
                if b:
                    pe.wait_ge(d_oev, b)
                scores(4, lambda j: kT3[:, j, TP + DS * b:TP + DS * b + DS], DS).then_inc(d_qk, 1)
                att_tile(b)
                pe.wait_ge(lo_ok, NT + b + 1)
                if b + 1 < DB:
                    ktr(4 * b + 4)
                    ktr(4 * b + 5)
                    pe.wait_ge(kt_a, 4 * b + 6)
                    pe.wait_ge(kt_v, 4 * b + 6)
                pe.wait_ge(d_p, b + 1)
                pe.wait_ge(vn_in[b % 2], 16 * (b // 2 + 1))

                def ptr(j):
                    if j >= 2:
                        pe.wait_ge(d_pa if j % 2 else d_pv, 2 * b + (j - 2) // 2 + 1 if j % 2 else 3 * b + (j - 2) // 2 + 1)
                    if j < 4:
                        for m in range(4):
                            last = pe.transpose(ps[:, 5 + j % 2, P * m:P * m + P],
                                                pS[:, 512 * j + P * m:512 * j + P * m + P], ident[:, :])
                    else:
                        last = pe.transpose(ps[:DS, 5 + j % 2, 0:P], pS[:, PAST:NK], ident[:, :])
                    last.then_inc(d_ptr, 1)

                def av(j):
                    pe.wait_ge(d_pa if j % 2 else d_pv, 2 * b + j // 2 + 1 if j % 2 else 3 * b + j // 2 + 1)
                    if j < 4:
                        pe.wait_ge(vg_in[j], 64 * (b + 1))
                    wid = P if j < 4 else DS
                    for m in range(4 if j < 4 else 1):
                        last = pe.matmul(ps[:, 7, 0:NKV * HD], ptS[:wid, j % 2, P * m:P * m + P],
                                         vpg[:, j, m, :] if j < 4 else vnew[:, b % 2, :],
                                         start=j == 0 and m == 0, stop=j == 4)
                    last.then_inc(d_o if j == 4 else s_done, 1)

                ptr(0)
                for j in range(5):
                    if j < 4:
                        ptr(j + 1)
                    av(j)
            o_transposed(DB - 1)
            pe.wait_ge(d_pv, 3 * DB)
            pe.wait_ge(d_pa, 2 * DB)
            att_tile(8)
            barrier(pe, 6)

            def project(h, q):
                s = (U_PA + h) % 2
                if q == 0:
                    pe.wait_ge(w_split, U_PA + h + 1)
                if 6 * h + q >= 2:
                    pe.wait_ge(pa_ev, 6 * h + q - 1)
                out, cols = ps[:, 3 if q % 2 else 7, 0:N3], slice(N3 * (q % 3), N3 * (q % 3) + N3)
                for k in range(KC):
                    at0 = (KC * (q // 3) + k) * P
                    hi, lo = w_hi[:, s, at0:at0 + P], w_lo[:, s, at0:at0 + P]
                    pe.matmul(out, hi, xt_hi[:, k, cols], start=k == 0, stop=False)
                    pe.matmul(out, hi, xt_lo[:, k, cols], start=False, stop=False)
                    last = pe.matmul(out, lo, xt_hi[:, k, cols], start=False, stop=k == KC - 1)
                last.then_inc(unit_done if q == 5 else pa_mm, 1)

            for h in range(GH):
                project(h, 0)
                project(h, 1)
                if h == 0:
                    pe.wait_ge(ga_set, 48)
                else:
                    pe.wait_ge(ga_head, h)
                for n in range(3):
                    last = pe.matmul(ps[:, n, 0:N3], wa2[:, DK * h:DK * h + DK], a1T[:, N3 * n:N3 * n + N3],
                                     start=True, stop=True)
                last.then_inc(ga_lg, 1)
                for q in range(2, 6):
                    project(h, q)
                pe.wait_ge(ga_ready, h + 1)
                order = [OT[8]] + OT[:8] + [OT[9]]

                def intra(n):
                    i, at0, r = order[n]
                    e = 10 * h + n
                    if e >= 2:
                        pe.wait_ge(ga_am, e - 1)
                        pe.wait_ge(ga_kn, e - 1)
                    if n in (0, 9):
                        pe.matmul(ps[:r, e % 2, 0:r], kd[:, at0:at0 + r], gq[:, at0:at0 + r], start=True, stop=True)
                    else:
                        for c in range(2):
                            cols = slice(at0 + CH * c, at0 + CH * c + CH)
                            pe.matmul(ps[CH * c:CH * c + CH, e % 2, 0:CH], kd[:, cols], gq[:, cols], start=True, stop=True)
                    pe.transpose(ps[:r, 2 + e % 2, 0:DK], gk[:, at0:at0 + r], ident[:, :]).then_inc(ga_at, 1)

                intra(0)
                for n in range(10):
                    i, at0, r = order[n]
                    e = 10 * h + n
                    if n == 0:
                        pe.wait_ge(pa_ev, 6 * (h + 1))
                    if n < 9:
                        intra(n + 1)
                    pe.wait_ge(ga_am, e + 1)
                    pe.wait_ge(ga_kn, e + 1)
                    if n == 9:
                        pe.wait_ge(ga_q, h + 1)
                        pe.wait_ge(ga_oe, e)
                        out = ps[:TS, 6, 0:DV]
                        pe.matmul(out, at[:TS, e % 2, :], gvs[:, :], start=True, stop=False)
                        for b in range(DB):
                            last = pe.matmul(out, qdm[:, TS * b:TS * b + TS], s0[:, b, :], start=False, stop=b == DB - 1)
                        last.then_inc(ga_o, 1)
                        for half in range(4):
                            pe.wait_ge(ga_s, 26 * h + 17 + 2 * max(half - 1, 0))
                            for m in range(2):
                                b = 2 * half + m
                                last = pe.matmul(ps[:, 4 + half % 2, DV * m:DV * m + DV], kem[:, b, :], gvs[:, :],
                                                 start=True, stop=True)
                            last.then_inc(ga_u, 1)
                        continue
                    if n:
                        pe.wait_ge(ga_s, 26 * h + 2 * (n - 1) + 1)
                    elif h:
                        pe.wait_ge(ga_s, 26 * h)
                    if n == 0:
                        pe.matmul(ps[:, 4, 0:DV], ken[:r, e % 2, :], gv[:r, 8, :], start=True, stop=True).then_inc(ga_u, 1)
                    else:
                        for c in range(2):
                            rows = slice(CH * c, CH * c + CH)
                            last = pe.matmul(ps[:, 4 + c, 0:DV], ken[rows, e % 2, :],
                                             gv[rows, i, :], start=True, stop=True)
                        last.then_inc(ga_u, 1)
                    if e:
                        pe.wait_ge(ga_oe, e)
                    if n == 0:
                        pe.matmul(ps[:r, 6, 0:DV], at[:r, e % 2, 0:r], gv[:r, 8, :], start=True, stop=True).then_inc(ga_o, 1)
                    else:
                        for c in range(2):
                            rows = slice(CH * c, CH * c + CH)
                            pe.matmul(ps[rows, 6, 0:DV], at[rows, e % 2, :], gv[rows, i, :], start=True, stop=False)
                            chunk = 2 * (n - 1) + c
                            pe.wait_ge(ga_s, 26 * h + chunk + 1)
                            last = pe.matmul(ps[rows, 6, 0:DV], gq[:, at0 + CH * c:at0 + CH * c + CH],
                                             sx[:, chunk % 4, :], start=False, stop=True)
                        last.then_inc(ga_o, 1)
            barrier(pe, 7)
            for n, (i, at0, r) in enumerate(OT):
                pe.wait_ge(po_ok, n + 1)
                if n >= 4:
                    pe.wait_ge(po_lo, n - 3)
                transpose_tile(oin[:, n % 4, :], r, 2 * (n % 4), po_tr)
            pe.wait_ge(po_lo, 10)
            barrier(pe, 8)

            for u in range(U_PG, U_O):
                e0 = evacs_before(u)
                unit_f(u % 2, u + 1, [e0 + c - 1 for c in range(2)])
            pe.wait_ge(evac, evacs_before(U_O))
            barrier(pe, 9)
            pe.wait_ge(mg_lo, KC)
            for u in range(U_O, U_FF):
                unit_n(u % 2, u + 1, evacs_before(u) - 2)
            for t in range(NT):
                if t == 0:
                    pe.wait_ge(evac, evacs_before(U_FF))
                if t >= 4:
                    pe.wait_ge(l_lo, t - 3)
                pe.wait_ge(n_h, NT + t + 1)
                transpose_tile(res[:, t, :], rows_of(t), 2 * (t % 4), l_tr)
            pe.wait_ge(l_lo, NT)
            barrier(pe, 10)

            def up(s, ready, free):
                pe.wait_ge(w_split, ready)
                for c in range(2):
                    if free is not None:
                        pe.wait_ge(f_relu, free + c)
                    for n in range(3):
                        out = ps[:, 3 * c + n, 0:N3]
                        cols = slice(N3 * n, N3 * n + N3)
                        for k in range(KC):
                            at0 = (KC * c + k) * P
                            hi, lo = w_hi[:, s, at0:at0 + P], w_lo[:, s, at0:at0 + P]
                            pe.matmul(out, hi, xt_hi[:, k, cols], start=k == 0, stop=False)
                            pe.matmul(out, hi, xt_lo[:, k, cols], start=False, stop=False)
                            last = pe.matmul(out, lo, xt_hi[:, k, cols], start=False, stop=k == KC - 1)
                    last.then_inc(unit_done if c else half_done, 1)

            def down(s, a, ready, hidden, adds):
                pe.wait_ge(w_split, ready)
                pe.wait_ge(f_lo, hidden)
                for m in range(2 * NT):
                    t, hf = m // 2, m % 2
                    r = rows_of(t)
                    if adds is not None:
                        pe.wait_ge(f_add, adds + m - 1)
                    elif m >= 2:
                        pe.wait_ge(f_add, m - 1)
                    out = ps[:r, 6 + m % 2, :]
                    for k in range(2):
                        cols = slice(P * t, P * t + r)
                        w = slice(1024 * k + 512 * hf, 1024 * k + 512 * hf + 512)
                        pe.matmul(out, a_hi[:, a, k, cols], w_hi[:, s, w], start=k == 0, stop=False)
                        pe.matmul(out, a_lo[:, a, k, cols], w_hi[:, s, w], start=False, stop=False)
                        last = pe.matmul(out, a_hi[:, a, k, cols], w_lo[:, s, w], start=False, stop=k == 1)
                    last.then_inc(unit_done if m == 2 * NT - 1 else f_half, 1)

            up(1, U_FF + 1, None)
            up(0, U_FF + 2, 1)
            down(1, 0, U_FF + 3, 2, None)
            with pe.Fori(0, (FB - 2) // 2) as i:
                for o in range(2):
                    up(0, 4 * i + (U_FF + 4 + 2 * o), 4 * i + (2 * o + 3))
                    down(1, 1 - o, 4 * i + (U_FF + 5 + 2 * o), 4 * i + (4 + 2 * o), 36 * i + 18 * (o + 1))
            down(0, 1, N_UNITS, 2 * FB, 18 * (FB - 1))

        @block.scalar
        def _(act):
            def chunk_ready(c, halves, units):
                act.wait_ge(unit_done if c else half_done, units if c else halves)

            def to_dram(e, dst, src, done):
                act.wait_ge(evac, e)
                act.dma_start(dst, src).then_inc(done, 16)

            def norm(which, x, transposed=None, ok=None, lag=4):
                n0 = NT * which
                for t in range(NT + (lag if ok else 1)):
                    if t < NT:
                        r = rows_of(t)
                        act.wait_ge(n_var, n0 + t + 1)
                        act.activation(small[:r, 2 + t % 2:3 + t % 2], small[:r, t % 2:t % 2 + 1], ACT.Sqrt).then_inc(n_std, 1)
                    if 1 <= t <= NT:
                        u = t - 1
                        r = rows_of(u)
                        act.wait_ge(n_shift, n0 + u + 1)
                        act.activation(x[:r, u, :], x[:r, u, :], ACT.Identity, bias=small[:r, 6 + u % 2:7 + u % 2],
                                       scale=small[:r, 4 + u % 2:5 + u % 2]).then_inc(n_z, 1)
                    if ok and t >= lag:
                        u = t - lag
                        r = rows_of(u)
                        act.wait_ge(transposed, u + 1)
                        src = flat[:, 1024 * (u % 4):1024 * (u % 4) + 1024].rearrange("p (k n) -> p k n", n=P)
                        act.activation(xt_hi[:, :, P * u:P * u + r], src[:, :, :r], ACT.Copy).then_inc(ok, 1)

            norm(0, h_sb, tr_ok, hi_ok)
            barrier(act, 1)

            for e in range(8):
                u, c = e // 2, e % 2
                chunk_ready(c, u + 1, u + 1)
                dst = kT3[:, e, :] if e < 4 else stg[:, c, :]
                if e >= 6:
                    act.wait_ge(st_out[c], 16)
                act.activation(dst.rearrange("p (n m) -> p n m", m=N3), ps[:, 3 * c:3 * c + 3, 0:N3], ACT.Copy).then_inc(evac, 1)
                if e >= 4:
                    to_dram(e + 1, qiT_d[P * (e - 4):P * (e - 4) + P, :], dst, st_out[c])
            act.wait_ge(ks_in, 64)
            act.activation(kiS[:, 0:TP], kraw, ACT.Copy).then_inc(ks_hi, 1)
            def qi_hi(i):
                act.wait_ge(q_in[i % 2], 32 * ((i + 1) // 2 if i % 2 else i // 2))
                if i > 1:
                    act.wait_ge(ix_mm, IH * (i - 1))
                act.activation(qhi[:, :, :], qraw[:, i % 2, :, :], ACT.Copy).then_inc(q_hi_ok, 1)

            qi_hi(1)
            for i in range(1, 8):
                _, w, np_ = keys_of(i)
                for h in range(IH):
                    if h == IH - 1 and i < 7:
                        qi_hi(i + 1)
                    g = IH * (i - 1) + h
                    act.wait_ge(ix_mm, g + 1)
                    if g >= 2:
                        act.wait_ge(ix_acc, g - 1)
                    act.activation(relu[:, g % 2, 0:w * np_].rearrange("p (n m) -> p n m", m=w),
                                   ps[:, 4 * (g % 2):4 * (g % 2) + np_, 0:w], ACT.Relu,
                                   scale=HD ** -0.5).then_inc(ix_relu, 1)
            barrier(act, 2)
            width = [512] * 4 + [DS]
            for q in range(5 * DB):
                w = width[q % 5]
                act.wait_ge(s_mm, q + 1)
                if q >= 2:
                    act.wait_ge(i_mm, q - 1)
                act.activation(relu2[:, q % 2, 0:w], ps[0:HD, 2 + q % 2, 0:w], ACT.Relu, scale=HD ** -0.5).then_inc(s_relu, 1)
            barrier(act, 3)

            def f_out(i, u0, per, n_before, dst, func):
                for s in range(2):
                    for c in range(2):
                        u = u0 + s
                        e = 4 * i + (evacs_before(u) + c)
                        chunk_ready(c, 2 * i + (halves_before(u) + 1), 2 * i + (u + 1))
                        act.wait_ge(st_out[c], 32 * i + 16 * (n_before + s))
                        act.activation(stg[:, c, :].rearrange("p (n m) -> p n m", m=N3),
                                       ps[:, 3 * c:3 * c + 3, 0:N3], func).then_inc(evac, 1)
                        rows = dst[bass.ds(512 * i + P * (2 * s + c), P), :]
                        to_dram(e + 1, rows, stg[:, c, :], st_out[c])

            with act.Fori(0, 4) as i:
                f_out(i, U_Q, 0, 2, qT_d, ACT.Copy)
            for t in range(NT):
                r = rows_of(t)
                if t == NT - 1:
                    act.wait_ge(unit_done, U_N + 1)
                else:
                    act.wait_ge(half_done, halves_before(U_N) + t + 1)
                act.activation(vnat[:r, t, :], ps[:r, t % 3, 0:256], ACT.Copy).then_inc(evac, 1)

            for c in range(2):
                act.wait_ge(st_out[c], 16 * 10)

            def fill_out(f):
                u, m, last_one = fill_unit(f)
                if last_one:
                    act.wait_ge(unit_done, u + 1)
                else:
                    act.wait_ge(fill_mm, fill_count(f))
                s = f % 3
                if f >= 3:
                    act.wait_ge(fst_out[s], 16 * (f // 3))
                if f < 8 * NT:
                    r, wid = rows_of(m), 256
                    col = 256 * (u - U_N - 1)
                    dst = gvog_d[P * m:P * m + r, col:col + 256]
                else:
                    r, wid = P, N3
                    row = P * (2 * (u - U_GATE) + m // 3)
                    dst = gate_d[row:row + P, N3 * (m % 3):N3 * (m % 3) + N3]
                bank = 6 + f % 2 if f < F_EARLY else 7
                act.activation(fill_at[:r, s, 0:wid], ps[:r, bank, 0:wid], ACT.Copy).then_inc(fill_ev, 1)
                act.wait_ge(fill_ev, f + 1)
                act.dma_start(dst, fill_at[:r, s, 0:wid]).then_inc(fst_out[s], 16)

            for f in range(F_EARLY):
                fill_out(f)
            barrier(act, 4)

            for f in range(F_EARLY, F_START - NKV):
                fill_out(f)
            for n in range(NKV):
                act.wait_ge(c_ks_in[n % 2], 64 * (n // 2 + 1))
                act.activation(kS[:, n, 0:TP], pP[:, n % 2, 0:TP], ACT.Copy).then_inc(c_ks_hi, 1)
                fill_out(F_START - NKV + n)
            act.wait_ge(c_ks_ok, NKV)

            def q_split(j):
                r = rows_of(j // NKV)
                act.wait_ge(cq_in[j % 2], 32 * (j // 2 + 1))
                if j:
                    act.wait_ge(qk_ok, G * j)
                act.activation(qh2[:, :, :r], qraw2[:, j % 2, :, :r], ACT.Copy).then_inc(cq_hi, 1)

            def exp(hh):
                i = hh // NH
                r = rows_of(i)
                _, w, np_ = keys_of(i)
                act.wait_ge(mx_ok, hh + 1)
                part = pP[:r, hh % 2, 0:w * np_]
                act.activation(part, part, ACT.Exp, bias=mx[:r, hh % 2:hh % 2 + 1], scale=-1.0,
                               accum_out=rsum[:r, hh % NH:hh % NH + 1])
                act.drain().then_inc(exp_ok, 1)

            q_split(0)
            exp(0)
            f = F_START
            for hh in range(NH * NT):
                i = hh // NH
                r = rows_of(i)
                if hh + 1 < NH * NT:
                    if hh % G == G - 2 and hh + 2 < NH * NT:
                        q_split((hh + 2) // G)
                    exp(hh + 1)
                if batches_of(i) > 1:
                    size = min(4, i + 2 - 4)
                    act.wait_ge(pt_tr, tr_before(hh) + 2)
                    act.activation(probs_t(hh, 1)[:, 0:P * size], ps[:, 5, 0:P * size], ACT.Copy).then_inc(pt_a, 1)
                if f < fills_by(hh):
                    fill_out(f)
                    f += 1
            for s in range(3):
                act.wait_ge(fst_out[s], 16 * (N_FILL // 3))
            barrier(act, 5)

            def att_hi(i):
                r = P if i < 8 else META
                act.wait_ge(att_tr, i + 1)
                src = flat[:, 2560:3584].rearrange("p (k n) -> p k n", n=P)
                act.activation(xt_hi[:, :, P * i:P * i + r], src[:, :, :r], ACT.Copy).then_inc(hi_ok, 1)

            def kt_upper(gg):
                act.wait_ge(kt_tr, gg + 1)
                if gg >= 2:
                    act.wait_ge(kt_qk, gg - 1)
                act.activation(kt[:, gg % 2, 1, :], ps[:, 6, :], ACT.Copy).then_inc(kt_a, 1)

            def load_v(b, grp):
                if b >= 1:
                    act.wait_ge(s_done, 4 * (b - 1) + grp + 1)
                load_pages(act, vpg[:, grp, :, :], cache_v, b, grp, vg_in[grp])

            kt_upper(0)
            kt_upper(1)
            for b in range(DB):
                load_v(b, 0)
                kt_upper(4 * b + 2)
                kt_upper(4 * b + 3)
                load_v(b, 1)
                att_hi(b)
                act.wait_ge(d_mx, b + 1)
                if b:
                    act.wait_ge(d_ptr, 5 * b)
                act.activation(pS[:, :], flat[:, 0:NK], ACT.Exp, bias=mx[:, 1:2], scale=HD ** -0.5,
                               accum_out=rsum[:, 0:1])
                act.drain().then_inc(d_exp, 1)
                if b + 1 < DB:
                    kt_upper(4 * b + 4)
                    kt_upper(4 * b + 5)
                for j in (1, 3):
                    act.wait_ge(d_ptr, 5 * b + j + 1)
                    if j == 3:
                        act.wait_ge(s_done, 4 * b + 2)
                    elif b:
                        act.wait_ge(d_o, b)
                    act.activation(ptS[:, 1, :], ps[:, 6, :], ACT.Copy).then_inc(d_pa, 1)
            att_hi(8)
            act.wait_ge(d_oev, DB)
            act.activation(xt_hi[:, :, TP:T], attT[:, :, :], ACT.Copy).then_inc(hi_ok, 1)
            barrier(act, 6)

            def sigmoid(dst, m, per, n0):
                act.wait_ge(g_in[m % 2], n0 + per * (m // 2 + 1))
                act.activation(dst[:, m % 2, :], dst[:, m % 2, :], ACT.Sigmoid).then_inc(g_sig, 1)

            for c in range(2):
                sigmoid(gst, c, 16, 0)
            act.wait_ge(ga_set, 48)
            for h in range(GH):
                act.wait_ge(ga_lg, h + 1)
                act.activation(zz[:, :].rearrange("p (n m) -> p n m", m=N3), ps[:, 0:3, 0:N3], ACT.Identity,
                               bias=ba[:, h:h + 1]).then_inc(ga_z, 1)
                act.wait_ge(ga_step, 4 * h + 1)
                act.activation(kd[:, :], kd[:, :], ACT.Exp)
                act.drain()
                act.activation(kd[:, :], kd[:, :], ACT.Ln, bias=1.0).then_inc(ga_e, 1)
                act.wait_ge(ga_step, 4 * h + 2)
                act.activation(zz[:, :], bb[:, :], ACT.Exp, scale=1.0 / TAU).then_inc(ga_e, 1)
                act.wait_ge(ga_step, 4 * h + 3)
                act.activation(zz[:, :], bb[:, :], ACT.Exp, scale=-1.0 / TAU).then_inc(ga_e, 1)
                act.wait_ge(ga_step, 4 * h + 4)
                act.activation(zz[:, :], zz[:, :], ACT.Exp, scale=1.0 / TAU).then_inc(ga_e, 1)
                order = [OT[8]] + OT[:8] + [OT[9]]
                for n in range(11):
                    if n < 10:
                        i, at0, r = order[n]
                        e = 10 * h + n
                        act.wait_ge(ga_at, e + 1)
                        if e >= 2:
                            act.wait_ge(ga_o, e - 1)
                            act.wait_ge(ga_u, 13 * h + n - 1 if n >= 2 else 13 * h)
                        act.activation(ken[:r, e % 2, :], ps[:r, 2 + e % 2, 0:DK], ACT.Copy).then_inc(ga_kn, 1)
                    if n:
                        i, at0, r = order[n - 1]
                        e = 10 * h + n - 1
                        act.wait_ge(ga_o, e + 1)
                        if e >= 2:
                            act.wait_ge(ga_oo[e % 2], 16 * (e // 2))
                        act.activation(zz[:r, 0:DV], ps[:r, 6, 0:DV], ACT.Square, accum_out=ssq[:r, i, h:h + 1])
                        act.activation(ostg[:r, e % 2, :], ps[:r, 6, 0:DV], ACT.Copy).then_inc(ga_oe, 1)
                if h + 1 < GH:
                    for c in range(2):
                        sigmoid(gst, 2 * h + 2 + c, 16, 0)
            barrier(act, 7)

            act.wait_ge(po_v, 1)
            act.activation(ssq[:, :, :], ssq[:, :, :], ACT.Sqrt).then_inc(po_sd, 1)
            for n in range(12):
                if n < 10:
                    i, at0, r = OT[n]
                    act.wait_ge(po_in[n % 4], 32 * (n // 4 + 1))
                    act.activation(ogin[:r, n % 4, :], ogin[:r, n % 4, :], ACT.Silu).then_inc(po_sl, 1)
                if n >= 2:
                    i, at0, r = OT[n - 2]
                    act.wait_ge(po_tr, n - 1)
                    src = flat[:, 1024 * ((n - 2) % 4):1024 * ((n - 2) % 4) + 1024].rearrange("p (k n) -> p k n", n=P)
                    act.activation(xt_hi[:, :, at0:at0 + r], src[:, :, :r], ACT.Copy).then_inc(po_hi, 1)
            barrier(act, 8)
            for m in range(KC):
                sigmoid(gst2, m, 32, 64)
            barrier(act, 9)
            for c in range(KC):
                act.activation(xt_hi[:, c, :], merged[:, c, :], ACT.Copy).then_inc(mg_hi, 1)

            norm(1, res, l_tr, l_hi, NT)
            barrier(act, 10)

            def hidden(a, halves, units, lows, squares, used):
                for c in range(2):
                    chunk_ready(c, halves, units)
                    if lows is not None:
                        act.wait_ge(f_lo, lows + c)
                    act.activation(rl[:, c, :].rearrange("p (n m) -> p n m", m=N3), ps[:, 3 * c:3 * c + 3, 0:N3],
                                   ACT.Relu).then_inc(f_relu, 1)
                    act.wait_ge(f_sq, squares + c)
                    if used is not None:
                        act.wait_ge(unit_done, used)
                    act.activation(a_hi[:, a, c, :], rl[:, c, :], ACT.Copy).then_inc(f_hi, 1)

            hb = halves_before(U_FF)
            hidden(0, hb + 1, U_FF + 1, None, 1, None)
            hidden(1, hb + 2, U_FF + 2, 1, 3, None)
            with act.Fori(0, (FB - 2) // 2) as i:
                for o in range(2):
                    hidden(o, 2 * i + (hb + 3 + o), 4 * i + (U_FF + 4 + 2 * o), 4 * i + (3 + 2 * o),
                           4 * i + (5 + 2 * o), 4 * i + (U_FF + 3 + 2 * o))
            norm(2, res)

        @block.vector
        def _(dve):
            def norm(which, x, g, before=None, hi=None, lo=None, lag=4):
                n0 = NT * which
                for t in range(NT + (lag if lo else 2)):
                    if t < NT:
                        r = rows_of(t)
                        if before:
                            before(t)
                        for half in range(2):
                            dve.bn_stats(stats[:r, t % 2, half, :], x[:r, t, 512 * half:512 * half + 512])
                        dve.drain()
                        dve.bn_aggr(mv[:r, t % 2, :], stats[:r, t % 2, :, :])
                        dve.drain()
                        dve.tensor_scalar(small[:r, t % 2:t % 2 + 1], mv[:r, t % 2, 1:2], EPS, None, ALU.add).then_inc(n_var, 1)
                    if 1 <= t <= NT:
                        u = t - 1
                        r = rows_of(u)
                        inv = small[:r, 4 + u % 2:5 + u % 2]
                        dve.wait_ge(n_std, n0 + u + 1)
                        dve.reciprocal(inv, small[:r, 2 + u % 2:3 + u % 2])
                        dve.drain()
                        dve.tensor_scalar(small[:r, 6 + u % 2:7 + u % 2], mv[:r, u % 2, 0:1], inv, -1.0,
                                          ALU.mult, ALU.mult).then_inc(n_shift, 1)
                    if 2 <= t <= NT + 1:
                        u = t - 2
                        r = rows_of(u)
                        dve.wait_ge(n_z, n0 + u + 1)
                        dve.tensor_tensor(x[:r, u, :], x[:r, u, :], g[:r, :], ALU.mult).then_inc(n_g, 1)
                    if lo and t >= lag:
                        u = t - lag
                        dve.wait_ge(hi, u + 1)
                        lo_part(slice(P * u, P * u + rows_of(u)), u % 4, lo)

            def lo_part(cols, slot, ok):
                n = cols.stop - cols.start
                src = flat[:, 1024 * slot:1024 * slot + 1024].rearrange("p (k n) -> p k n", n=P)
                dve.tensor_tensor(xt_lo[:, :, cols], src[:, :, :n], xt_hi[:, :, cols].bitcast(F32),
                                  ALU.subtract).then_inc(ok, 1)

            def x_landed(t):
                dve.wait_ge(x_in[(0, 1, 2, 2, 2, 3, 3, 3, 4)[t]], 16)
                if t == 2:
                    dve.wait_ge(ln_in, 48)

            norm(0, h_sb, lg, x_landed, hi_ok, lo_ok)
            dve.memset(ssq[:, :, :], 0.0)
            dve.wait_ge(consts, 7)
            dve.tensor_reduce(delta[:, :], d8[:, :, :].rearrange("p i j -> p j i"), AX.X, ALU.add)
            dve.tensor_reduce(bsel[:, :], d8[:, :, :], AX.X, ALU.add)
            for t in range(DS):
                dve.memset(m8[:TS, t:t + 1], float(t))
            dve.drain()
            dve.tensor_tensor(triS[:, :], delta[:, :], m8[:TS, :], ALU.mult)
            dve.drain()
            dve.tensor_reduce(small[:TS, 8:9], triS[:, :], AX.X, ALU.add)
            dve.drain()
            dve.tensor_scalar(triS[:, :], m8[:TS, :], small[:TS, 8:9], NEG, ALU.is_gt, ALU.mult)
            barrier(dve, 1)

            dve.memset(kiS[:, TP:1056].bitcast(F32), 0.0)
            dve.wait_ge(ks_hi, 1)
            lower = slice(HD, P)
            dve.tensor_tensor(kiS[lower, 0:TP], kraw[lower, :], kiS[lower, 0:TP].bitcast(F32),
                              ALU.subtract).then_inc(ks_ok, 1)
            for t in range(NT):
                r = rows_of(t)
                dve.wait_ge(kn_tr, t + 1)
                if t >= 2:
                    dve.wait_ge(kn_out[t % 2], 32 * (t // 2))
                dve.tensor_scalar(winat[:r, t, :], ps[:r, 6 + t % 2, 256 + HD:256 + HD + IH], IH ** -0.5, None, ALU.mult)
                dve.tensor_copy(knat[t % 2][:r, :], ps[:r, 6 + t % 2, 0:384]).then_inc(kn_ok, 1)
            def qi_lo(i):
                dve.wait_ge(q_hi_ok, i)
                dve.tensor_tensor(qlo[:, :, :], qraw[:, i % 2, :, :], qhi[:, :, :].bitcast(F32),
                                  ALU.subtract).then_inc(q_lo_ok, 1)

            qi_lo(1)
            for i in range(1, 8):
                L, w, np_ = keys_of(i)
                acc = isc[:, mask_at(i):mask_at(i) + L]
                if i == 6:
                    dve.wait_ge(kn_out[0], 32 * 4 + 64)
                    dve.wait_ge(kn_out[1], 32 * 4)
                for h in range(IH):
                    g = IH * (i - 1) + h
                    if h == IH - 1 and i < 7:
                        qi_lo(i + 1)
                    dve.wait_ge(ix_relu, g + 1)
                    if h == 0:
                        dve.tensor_scalar(acc, relu[:, g % 2, 0:L], winat[:, i, 0:1], None, ALU.mult).then_inc(ix_acc, 1)
                    else:
                        dve.wait_ge(ix_acc, g)
                        dve.scalar_tensor_tensor(acc, relu[:, g % 2, 0:L], winat[:, i, h:h + 1], acc,
                                                 ALU.mult, ALU.add).then_inc(ix_acc, 1)
                dve.drain()
                dve.tensor_tensor(acc[:, L - P:L], acc[:, L - P:L], tri[:, :], ALU.add)
            barrier(dve, 2)

            dve.wait_ge(sx_in, 16 * 16)
            for b in range(DB):
                dve.tensor_scalar(wb[:, b, :], delta[:, :], wsel[:, b:b + 1], IH ** -0.5, ALU.mult, ALU.mult)
            dve.drain().then_inc(wb_ok, 1)
            width = [512] * 4 + [DS]
            for b in range(DB):
                def ev(grp):
                    gg = 4 * b + grp
                    dve.wait_ge(kx_tr, gg + 1)
                    dve.tensor_copy(kxT[:, 512 * grp:512 * grp + 512], ps[0:HD, gg % 2, :]).then_inc(kx_ev, 1)

                def ib_ev(p):
                    q = 5 * b + p
                    dve.wait_ge(i_mm, q + 1)
                    dve.tensor_copy(ib[:, 512 * p:512 * p + width[p]], ps[0:DS, 4 + q % 2, 0:width[p]]).then_inc(i_ev, 1)

                if b:
                    dve.wait_ge(s_mm, 5 * b)
                dve.tensor_copy(kxT[:, PAST:NK], kT3[0:HD, 2, TP + DS * b:TP + DS * b + DS]).then_inc(kx_ev, 1)
                ev(0); ev(1); ev(2)
                if b:
                    dve.wait_ge(ib_out, 16 * b)
                ib_ev(0); ev(3); ib_ev(1); ib_ev(2); ib_ev(3); ib_ev(4)
            dve.wait_ge(ib_out, 16 * DB)
            dve.tensor_tensor(iscS[:, PAST:NK], iscS[:, PAST:NK], triS[:, :], ALU.add)
            barrier(dve, 3)

            sets = [(isc[:, mask_at(i):mask_at(i) + keys_of(i)[0]], masks[:, mask_at(i):mask_at(i) + keys_of(i)[0]],
                     P, keys_of(i)[0]) for i in range(1, 8)] + [(iscS[:, :], maskS[:, :], TS, NK)]

            def as_float(dst, src):
                dve.tensor_scalar(low_m[:, :], src[:, :], 31, 0x7FFFFFFF, ALU.arith_shift_right, ALU.bitwise_and)
                dve.drain()
                dve.scalar_tensor_tensor(dst[:, :], low_m[:, :], -1, src[:, :], ALU.bitwise_xor, ALU.bitwise_xor)
                dve.drain()

            dve.memset(cut[:, :], 0)
            dve.memset(cnt[:, :], 0.0)
            dve.memset(bit[:, :], 1)
            dve.drain()
            dve.tensor_scalar(bit[:, :], bit[:, :], 31, None, ALU.logical_shift_left)
            with dve.Fori(0, 32):
                dve.drain()
                dve.tensor_tensor(cand[:, :], cut[:, :], bit[:, :], ALU.bitwise_or)
                dve.drain()
                as_float(take, cand)
                for j, (x, m, r, n) in enumerate(sets):
                    dve.tensor_scalar(m, x, take[:r, j:j + 1].bitcast(F32), None, ALU.is_ge, ALU.add,
                                      accum_out=cnt[:r, j:j + 1])
                dve.drain()
                dve.tensor_scalar(low_m[:, :], cnt[:, :], float(TOPK), -1.0, ALU.is_ge, ALU.mult)
                dve.drain()
                dve.tensor_tensor(low_m[:, :], low_m[:, :], bit[:, :], ALU.bitwise_and)
                dve.drain()
                dve.tensor_tensor(cut[:, :], cut[:, :], low_m[:, :], ALU.bitwise_or)
                dve.tensor_scalar(bit[:, :], bit[:, :], 1, None, ALU.logical_shift_right)
            dve.drain()
            as_float(take, cut)
            for j, (x, m, r, n) in enumerate(sets):
                dve.tensor_scalar(m, x, take[:r, j:j + 1].bitcast(F32), None, ALU.is_gt, ALU.add,
                                  accum_out=cnt[:r, j:j + 1])
            dve.drain()
            dve.tensor_scalar(need[:, :], cnt[:, :], -1.0, float(TOPK), ALU.mult, ALU.add)
            dve.drain()
            for j, (x, m, r, n) in enumerate(sets):
                eq = eqb[:r, 0:n]
                dve.tensor_scalar(eq, x, take[:r, j:j + 1].bitcast(F32), None, ALU.is_equal)
                dve.drain()
                dve.tensor_tensor_scan(x, eq, eq, 0.0, ALU.add, ALU.max)
                dve.drain()
                dve.scalar_tensor_tensor(eq, x, need[:r, j:j + 1], eq, ALU.is_le, ALU.mult)
                dve.drain()
                dve.tensor_tensor(m, m, eq, ALU.add)
                dve.drain()
                dve.tensor_scalar(m, m, 1.0, -NEG, ALU.subtract, ALU.mult)
                dve.drain()
                last, add = (m[:, n - P:n], tri[:, :]) if r == P else (m[:, PAST:NK], triS[:, :])
                dve.tensor_tensor(last, last, add, ALU.add)
            dve.memset(masks[:, 0:META], 0.0)
            dve.tensor_copy(masks[:, META:META + P], tri[:, :])
            dve.memset(masks[:, mask_at(7) + TP:IW], NEG)
            barrier(dve, 4)

            for n in range(NKV):
                dve.memset(kS[:, n, TP:1056].bitcast(F32), 0.0)
                dve.wait_ge(c_ks_hi, n + 1)
                dve.tensor_tensor(kS[lower, n, 0:TP], pP[lower, n % 2, 0:TP], kS[lower, n, 0:TP].bitcast(F32),
                                  ALU.subtract).then_inc(c_ks_ok, 1)

            def q_split(j):
                r = rows_of(j // NKV)
                dve.wait_ge(cq_hi, j + 1)
                dve.tensor_tensor(ql2[:, :, :r], qraw2[:, j % 2, :, :r], qh2[:, :, :r].bitcast(F32),
                                  ALU.subtract).then_inc(cq_lo, 1)

            def masked_max(hh):
                i = hh // NH
                r = rows_of(i)
                _, w, np_ = keys_of(i)
                bank = 0 if np_ == 3 else 2 * (hh % 2)
                mask = masks[:r, mask_at(i):mask_at(i) + w * np_] if i < 8 else tri16[:r, :]
                dve.wait_ge(qk_ok, hh + 1)
                if hh >= 2:
                    dve.wait_ge(pt_tr, tr_before(hh - 1))
                v = lambda a: a.rearrange("p (n m) -> p n m", m=w)
                dve.tensor_tensor_reduce(out=v(pP[:r, hh % 2, 0:w * np_]), in0=ps[:r, bank:bank + np_, 0:w],
                                         in1=v(mask), scale=-HD ** -0.5, scalar=3e38, op0=ALU.add, op1=ALU.min,
                                         accum_out=mx[:r, hh % 2:hh % 2 + 1]).then_inc(mx_ok, 1)

            def evac_p(hh, j):
                i = hh // NH
                r, size = rows_of(i), min(4, (i + 2 if i < 8 else 1) - 4 * j)
                dve.wait_ge(pt_tr, tr_before(hh) + j + 1)
                first = 0
                if j == 0:
                    last = dve.tensor_copy(probs_t(hh, 0)[:META, 0:r], ps[:META, 4, 0:r])
                    first = 1
                if size > first:
                    last = dve.tensor_copy(probs_t(hh, j)[:, P * first:P * size], ps[:, 4, P * first:P * size])
                last.then_inc(pt_v, 1)

            def scale(hh):
                i, m = hh // NH, hh % NH
                r = rows_of(i)
                inv = small[:r, 12 + m % 2:13 + m % 2]
                dve.wait_ge(exp_ok, hh + 1)
                dve.reciprocal(inv, rsum[:r, m:m + 1])
                dve.drain()
                if m % 8 == 0 and i:
                    dve.wait_ge(att_out[m // 8], 16 * i)
                dve.wait_ge(pv_ok, tr_before(hh + 1))
                dve.tensor_scalar(attn[:r, HD * m:HD * m + HD], ps[:r, 6, 0:HD], inv, None,
                                  ALU.mult).then_inc(o_ev, 1)

            q_split(0)
            masked_max(0)
            masked_max(1)
            for hh in range(NH * NT):
                if hh % G == G - 2 and hh + 2 < NH * NT:
                    q_split((hh + 2) // G)
                evac_p(hh, 0)
                if batches_of(hh // NH) == 3:
                    evac_p(hh, 2)
                if hh + 2 < NH * NT:
                    masked_max(hh + 2)
                if hh:
                    scale(hh - 1)
            scale(NH * NT - 1)
            barrier(dve, 5)

            dve.memset(qblk[:, :, :, :], 0.0)
            dve.drain().then_inc(d_set, 1)
            for b in range(DB):
                dve.tensor_scalar(esel[:, b, :, :], delta[:, None, :].broadcast_to((TS, NH, DS)), bsel[:, b:b + 1],
                                  None, ALU.mult)
            dve.drain().then_inc(d_set, 1)
            def att_lo(i):
                r = P if i < 8 else META
                cols = slice(P * i, P * i + r)
                dve.wait_ge(hi_ok, NT + i + 1)
                src = flat[:, 2560:3584].rearrange("p (k n) -> p k n", n=P)
                dve.tensor_tensor(xt_lo[:, :, cols], src[:, :, :r], xt_hi[:, :, cols].bitcast(F32),
                                  ALU.subtract).then_inc(lo_ok, 1)

            def kt_lower(gg):
                dve.wait_ge(kt_tr, gg + 1)
                if gg >= 2:
                    dve.wait_ge(kt_qk, gg - 1)
                dve.tensor_copy(kt[:, gg % 2, 0, :], ps[:, 5, :]).then_inc(kt_v, 1)

            def o_out(b):
                dve.wait_ge(d_ot, b + 1)
                for half in range(2):
                    rows = slice(HD * half, HD * half + HD)
                    src = ps[rows, 4, 256:256 + P].rearrange("p (c a t) -> p c a t", a=2, t=DS)
                    last = dve.tensor_copy(attT[rows, :, DS * b:DS * b + DS], src[:, :, half, :])
                last.then_inc(d_oev, 1)

            kt_lower(0)
            kt_lower(1)
            for b in range(DB):
                if b:
                    o_out(b - 1)
                kt_lower(4 * b + 2)
                kt_lower(4 * b + 3)
                dve.wait_ge(d_qk, b + 1)
                dve.tensor_reduce(mx[:, 0:1], flat[:, 0:NK], AX.X, ALU.max)
                dve.drain()
                dve.tensor_scalar(mx[:, 1:2], mx[:, 0:1], -HD ** -0.5, None, ALU.mult).then_inc(d_mx, 1)
                att_lo(b)
                if b + 1 < DB:
                    kt_lower(4 * b + 4)
                dve.wait_ge(d_exp, b + 1)
                dve.reciprocal(small[:, 9:10], rsum[:, 0:1])
                dve.drain()
                dve.tensor_scalar(pS[:, :], pS[:, :], small[:, 9:10], None, ALU.mult).then_inc(d_p, 1)
                if b + 1 < DB:
                    kt_lower(4 * b + 5)
                for j in (0, 2, 4):
                    dve.wait_ge(d_ptr, 5 * b + j + 1)
                    if j:
                        dve.wait_ge(s_done, 4 * b + j - 1)
                    wid, n = (P, 512) if j < 4 else (DS, P)
                    dve.tensor_copy(ptS[:wid, 0, 0:n], ps[:wid, 5, 0:n]).then_inc(d_pv, 1)
                dve.wait_ge(d_o, b + 1)
                for n in range(NKV):
                    rows = slice(32 * n, 32 * n + 32)
                    last = dve.tensor_copy(oS[rows, :, :], ps[rows, 7, HD * n:HD * n + HD][:, None, :].broadcast_to((32, 2, HD)))
                last.then_inc(d_oc, 1)
            o_out(DB - 1)
            att_lo(8)
            dve.wait_ge(hi_ok, 2 * NT + 1)
            dve.tensor_tensor(xt_lo[:, :, TP:T], attT[:, :, :], xt_hi[:, :, TP:T].bitcast(F32), ALU.subtract)
            barrier(dve, 6)

            def gated(m, base, g, dst, add=None, sig=0):
                e = evacs_before(base) + m
                u = base + m // 2
                if m % 2:
                    dve.wait_ge(unit_done, u + 1)
                else:
                    dve.wait_ge(half_done, halves_before(u) + 1)
                dve.wait_ge(g_sig, sig + m + 1)
                v = lambda a: a.rearrange("p (n m) -> p n m", m=N3)
                ins = dve.tensor_tensor(v(dst), ps[:, 3 * (m % 2):3 * (m % 2) + 3, 0:N3], v(g[:, m % 2, :]), ALU.mult)
                if add is not None:
                    dve.drain()
                    ins = dve.tensor_tensor(dst, dst, add[:, m % 2, :], ALU.add)
                ins.then_inc(evac, 1)

            def pa_gated(h, q):
                dve.wait_ge(unit_done if q == 5 else pa_mm, U_PA + h + 1 if q == 5 else 5 * h + q + 1)
                dve.wait_ge(g_sig, 2 * h + q // 3 + 1)
                part = gst[:, q // 3, N3 * (q % 3):N3 * (q % 3) + N3]
                dve.tensor_tensor(part, ps[:, 3 if q % 2 else 7, 0:N3], part, ALU.mult).then_inc(pa_ev, 1)

            dve.memset(reset[:, :], 1.0)
            dve.memset(qdm[:, :], 0.0)
            dve.drain()
            dve.memset(reset[:, 0:SEQ].rearrange("p (c n) -> p c n", n=CH)[:, :, 0:1], 0.0)
            dve.memset(reset[:, SEQ:SEQ + 1], 0.0)
            dve.memset(reset[:, TP:T].rearrange("p (c n) -> p c n", n=DS)[:, :, 0:1], 0.0)
            dve.tensor_tensor(bd64[:, :].rearrange("p (b t) -> p b t", t=DS),
                              causal[:TS, :].rearrange("p (b t) -> p b t", t=DS),
                              bsel[:, :].unsqueeze(2).broadcast_to((TS, DB, DS)), ALU.mult)
            segs = [(0, SEQ, CH), (SEQ, TP, META), (TP, T, DS)]
            for h in range(GH):
                pa_gated(h, 0)
                dve.wait_ge(ga_z, h + 1)
                dve.scalar_tensor_tensor(kd[:, :], zz[:, :], -1.0, zz[:, :], ALU.mult, ALU.min).then_inc(ga_step, 1)
                pa_gated(h, 1)
                dve.wait_ge(ga_e, 4 * h + 1)
                dve.scalar_tensor_tensor(zz[:, :], zz[:, :], 0.0, kd[:, :], ALU.min, ALU.subtract)
                dve.drain()
                dve.tensor_tensor_scan(bb[:, :], reset[:, :], zz[:, :], 0.0, ALU.mult, ALU.add).then_inc(ga_step, 1)
                pa_gated(h, 2)
                dve.wait_ge(ga_in, 96 * (h + 1))
                dve.wait_ge(ga_e, 4 * h + 2)
                dve.scalar_tensor_tensor(gq[:, :], gq[:, :], DK ** -0.5, zz[:, :], ALU.mult, ALU.mult)
                for (a, z, n), at0 in zip(segs, (0, 16, 17)):
                    k = (z - a) // n
                    dve.tensor_copy(dec[:, at0:at0 + k].unsqueeze(2),
                                    zz[:, a:z].rearrange("p (c n) -> p c n", n=n)[:, :, n - 1:n])
                dve.drain().then_inc(ga_step, 1)
                pa_gated(h, 3)
                dve.wait_ge(ga_e, 4 * h + 3)
                dve.tensor_tensor(kd[:, :], gk[:, :], zz[:, :], ALU.mult)
                dve.drain()
                for a, z, n in segs:
                    v = bb[:, a:z].rearrange("p (c n) -> p c n", n=n)
                    dve.tensor_tensor(zz[:, a:z].rearrange("p (c n) -> p c n", n=n),
                                      v[:, :, n - 1:n].broadcast_to((P, (z - a) // n, n)), v, ALU.subtract)
                dve.drain().then_inc(ga_step, 1)
                pa_gated(h, 4)
                dve.wait_ge(ga_e, 4 * h + 4)
                dve.tensor_tensor(gk[:, :], gk[:, :], zz[:, :], ALU.mult)
                dve.tensor_copy(qdm[:, :].rearrange("p (b c) -> p b c", c=72)[:, :, 0:DS],
                                gq[:, TP:T].rearrange("p (b t) -> p b t", t=DS))
                dve.drain().then_inc(ga_ready, 1)
                pa_gated(h, 5)
                order = [OT[8]] + OT[:8] + [OT[9]]
                if h:
                    dve.wait_ge(ga_so, 32 * h)
                for n in range(11):
                    if n < 10:
                        i, at0, r = order[n]
                        e = 10 * h + n
                        dve.wait_ge(ga_at, e + 1)
                        if e >= 2:
                            dve.wait_ge(ga_o, e - 1)
                        wid = META if n == 0 else CH
                        m = bd64 if n == 9 else causal
                        dve.tensor_tensor(at[:r, e % 2, 0:wid], ps[:r, e % 2, 0:wid], m[:r, 0:wid], ALU.mult).then_inc(ga_am, 1)
                    if n == 0:
                        continue
                    nn = n - 1
                    e = 10 * h + nn
                    if nn == 0:
                        dve.wait_ge(ga_u, 13 * h + 1)
                        dve.tensor_copy(sx[:, 0, :], ps[:, 4, 0:DV]).then_inc(ga_s, 1)
                    elif nn < 9:
                        dve.wait_ge(ga_u, 13 * h + nn + 1)
                        for c in range(2):
                            chunk = 2 * (nn - 1) + c
                            dve.wait_ge(ga_s, 26 * h + chunk + 1)
                            if chunk >= 3:
                                dve.wait_ge(ga_o, 10 * h + (chunk - 3) // 2 + 2)
                            dve.scalar_tensor_tensor(sx[:, (chunk + 1) % 4, :], sx[:, chunk % 4, :],
                                                     dec[:, chunk:chunk + 1],
                                                     ps[:, 4 + c, 0:DV], ALU.mult, ALU.add).then_inc(ga_s, 1)
                i, at0, r = order[9]
                dve.wait_ge(ga_kn, 10 * h + 10)
                dve.tensor_tensor(kem[:, :, :], ken[:TS, (10 * h + 9) % 2, :][:, None, :].broadcast_to((TS, DB, DK)),
                                  bsel[:, :].unsqueeze(2).broadcast_to((TS, DB, DK)), ALU.mult).then_inc(ga_q, 1)
                dve.wait_ge(ga_o, 10 * h + 10)
                for b in range(DB):
                    if b % 2 == 0:
                        dve.wait_ge(ga_u, 13 * h + 9 + b // 2 + 1)
                    dve.scalar_tensor_tensor(s0[:, b, :], s0[:, b, :], dec[:, 17 + b:18 + b],
                                             ps[:, 4 + (b // 2) % 2, DV * (b % 2):DV * (b % 2) + DV],
                                             ALU.mult, ALU.add).then_inc(ga_s, 1)
                dve.drain().then_inc(ga_s, 1)
                dve.wait_ge(ga_oe, 10 * h + 10)
                dve.drain().then_inc(ga_head, 1)
            barrier(dve, 7)

            dve.memset(small[:, 10:11], 0.0)
            dve.tensor_scalar(ssq[:, :, :], ssq[:, :, :], 1.0 / DV, EPS, ALU.mult, ALU.add).then_inc(po_v, 1)
            dve.wait_ge(po_sd, 1)
            dve.reciprocal(ssq[:, :, :], ssq[:, :, :])
            dve.wait_ge(po_set, 16)
            dve.drain()
            for n in range(12):
                if n < 10:
                    i, at0, r = OT[n]
                    dve.wait_ge(po_in[n % 4], 32 * (n // 4 + 1))
                    o = oin[:r, n % 4, :].rearrange("p (h v) -> p h v", v=DV)
                    for h in range(GH):
                        dve.scalar_tensor_tensor(o[:, h, :], o[:, h, :], ssq[:r, i, h:h + 1], gnb[:r, :], ALU.mult, ALU.mult)
                    dve.wait_ge(po_sl, n + 1)
                    dve.drain()
                    dve.tensor_tensor(oin[:r, n % 4, :], oin[:r, n % 4, :], ogin[:r, n % 4, :], ALU.mult).then_inc(po_ok, 1)
                if n >= 2:
                    i, at0, r = OT[n - 2]
                    dve.wait_ge(po_hi, n - 1)
                    lo_part(slice(at0, at0 + r), (n - 2) % 4, po_lo)
            barrier(dve, 8)
            for m in range(KC):
                gated(m, U_PG, gst2, merged[:, m, :], pst2, KC)
            barrier(dve, 9)
            for c in range(KC):
                dve.wait_ge(mg_hi, c + 1)
                dve.tensor_tensor(xt_lo[:, c, :], merged[:, c, :], xt_hi[:, c, :].bitcast(F32), ALU.subtract).then_inc(mg_lo, 1)

            dve.wait_ge(res_in, 32)
            def onto_res(u, t):
                r = rows_of(t)
                if t == NT - 1:
                    dve.wait_ge(unit_done, u + 1)
                else:
                    dve.wait_ge(half_done, halves_before(u) + t + 1)
                dst = res[:r, t, 256 * (u - U_O):256 * (u - U_O) + 256]
                dve.scalar_tensor_tensor(dst, dst, ALPHA, ps[:r, t % 3, 0:256], ALU.mult, ALU.add).then_inc(evac, 1)

            for u in range(U_O, U_FF - 1):
                for t in range(NT):
                    onto_res(u, t)

            def last_unit(t):
                onto_res(U_FF - 1, t)
                dve.drain()

            dve.wait_ge(ln2_in, 32)
            norm(1, res, lg2, last_unit, l_hi, l_lo, NT)
            barrier(dve, 10)

            def square(c, relus):
                dve.wait_ge(f_relu, relus + c)
                dve.tensor_tensor(rl[:, c, :], rl[:, c, :], rl[:, c, :], ALU.mult).then_inc(f_sq, 1)

            def low(c, a, his):
                dve.wait_ge(f_hi, his + c)
                dve.tensor_tensor(a_lo[:, a, c, :], rl[:, c, :], a_hi[:, a, c, :].bitcast(F32), ALU.subtract).then_inc(f_lo, 1)

            def sums(m0, m1, halves, units, first=False):
                for m in range(m0, m1):
                    t, hf = m // 2, m % 2
                    r = rows_of(t)
                    if m == 2 * NT - 1:
                        dve.wait_ge(unit_done, units)
                    else:
                        dve.wait_ge(f_half, halves + m)
                    dst = res[:r, t, 512 * hf:512 * hf + 512]
                    if first:
                        dve.scalar_tensor_tensor(dst, dst, ALPHA, ps[:r, 6 + m % 2, :], ALU.mult, ALU.add).then_inc(f_add, 1)
                    else:
                        dve.tensor_tensor(dst, dst, ps[:r, 6 + m % 2, :], ALU.add).then_inc(f_add, 1)

            for j in range(2):
                for c in range(2):
                    square(c, 2 * j + 1)
                    low(c, j, 2 * j + 1)
            sums(0, 18, 1, U_FF + 3, True)
            with dve.Fori(0, (FB - 2) // 2) as i:
                for o in range(2):
                    n = 4 * i + (5 + 2 * o)
                    square(0, n)
                    low(0, o, n)
                    hv, uv = 34 * i + 17 * (o + 1) + 1, 4 * i + (U_FF + 5 + 2 * o)
                    square(1, n)
                    sums(0, 2, hv, uv)
                    low(1, o, n)
                    sums(2, 18, hv, uv)
            dve.wait_ge(ln2_in, 64)

            def last_sums(t):
                sums(2 * t, 2 * t + 2, 17 * (FB - 1) + 1, N_UNITS)
                dve.drain()

            norm(2, res, lg2, last_sums)


def tr_before(hh):
    return sum(batches_of(h // NH) for h in range(hh))


def _units(inp):
    def f_unit(w, c0, c1):
        parts = [w[:, c:c + P].reshape(KC, P, P).transpose(1, 0, 2) for c in (c0, c1)]
        return np.concatenate(parts, axis=1).reshape(P, UNIT)

    def n_unit(w, c0):
        return w[:, c0:c0 + 256].reshape(KC, P, 256).transpose(1, 0, 2).reshape(P, UNIT)

    w, wa, wg, wo = inp["w_in"][0], inp["w_proj_attn"][0], inp["w_proj_gla"][0], inp["w_out"][0]
    up, down = inp["w_ff_up"][0], inp["w_ff_down"][0]
    us = [f_unit(w, C_K, C_K + P), f_unit(w, C_KI, C_A1)]
    us += [f_unit(w, C_QI + 256 * j, C_QI + 256 * j + P) for j in range(2)]
    us += [f_unit(w, C_Q + 256 * j, C_Q + 256 * j + P) for j in range(4)]
    us += [f_unit(w, c + 256 * j, c + 256 * j + P) for c in (C_GQ, C_GK) for j in range(2)]
    us += [n_unit(w, C_V)]
    us += [n_unit(w, c + 256 * j) for c in (C_GV, C_OG) for j in range(4)]
    us += [f_unit(w, C_GT + 256 * j, C_GT + 256 * j + P) for j in range(8)]
    us += [f_unit(m, 256 * j, 256 * j + P) for m in (wa, wg) for j in range(4)]
    us += [n_unit(wo, 256 * j) for j in range(4)]
    ups = [f_unit(up, 256 * j, 256 * j + P) for j in range(FB)]
    downs = [down[256 * j:256 * j + 256].reshape(2, P, D).transpose(1, 0, 2).reshape(P, UNIT) for j in range(FB)]
    us += [ups[0]]
    for j in range(1, FB):
        us += [ups[j], downs[j - 1]]
    return np.stack(us + [downs[FB - 1]])


def kernel(**inputs):
    import concourse.bacc as bacc
    from concourse.bass_utils import run_bass_kernel_spmd

    inp = {k: np.asarray(v) for k, v in inputs.items()}
    f = np.ascontiguousarray
    pool = inp["cache_k"].shape[1]
    arrays = {
        "x_all": f(np.concatenate([inp["x_prompt"][0], inp["meta_tokens"], inp["x_sample"].reshape(TS, D)])),
        "cache_k": f(inp["cache_k"][0].reshape(pool, PAGE, NKV * HD)),
        "cache_v": f(inp["cache_v"][0].reshape(pool, PAGE, NKV * HD)),
        "cache_kidx": f(inp["cache_kidx"][0]),
        "state": f(inp["state_gla"][0]),
        "page_table": f(inp["page_table"].reshape(1, DB * NPG)),
        "ln_p": f(np.stack([inp["ln_in_g"], inp["ln_in_b"], inp["ln1_g"][0], inp["ln1_b"][0],
                            inp["ln2_g"][0], inp["ln2_b"][0]])),
        "w_stream": f(_units(inp)),
        "w_a2": f(inp["w_gla_a2"][0]),
        "b_a": f(inp["b_gla_a"][0]),
        "gnorm": f(inp["gla_norm_g"]),
    }
    outs = [("y_p", (SEQ, D)), ("y_s", (TS, D)), ("k_p", (TP, 256)), ("v_p", (TP, 256)), ("ki_p", (TP, HD)),
            ("st_p", (GH, DK, DV)), ("k_s", (TS, 256)), ("v_s", (TS, 256)), ("ki_s", (TS, HD)),
            ("st_s", (DB, GH, DK, DV))]
    nc = bacc.Bacc("TRN2", target_bir_lowering=False, num_devices=1)
    ins = [nc.dram_tensor(n, a.shape, mybir.dt.from_np(a.dtype), kind="ExternalInput").ap() for n, a in arrays.items()]
    out_aps = [nc.dram_tensor(n, s, F32, kind="ExternalOutput").ap() for n, s in outs]
    build(nc, *ins, out_aps)
    r = run_bass_kernel_spmd(nc, [arrays], core_ids=[0]).results[0]
    return (r["y_p"].reshape(1, SEQ, D), r["y_s"].reshape(DB, DS, D),
            r["k_p"].reshape(1, 1, TP, NKV, HD), r["v_p"].reshape(1, 1, TP, NKV, HD), r["ki_p"].reshape(1, 1, TP, HD),
            r["st_p"].reshape(1, 1, GH, DK, DV), r["k_s"].reshape(1, DB, DS, NKV, HD),
            r["v_s"].reshape(1, DB, DS, NKV, HD), r["ki_s"].reshape(1, DB, DS, HD),
            r["st_s"].reshape(1, DB, GH, DK, DV))
```
